# Optimizing a Trainium2 kernel written in Bass

```python
import math
import jax, jax.numpy as jnp
from jax import lax
import numpy as np

D_MODEL = 1024
BATCH = 1
SEQ = 1024
DEPTH = 2

N_MIXERS = 2
N_RET_LAYERS = (DEPTH + N_MIXERS - 1) // N_MIXERS
N_NA_LAYERS = DEPTH // N_MIXERS

MIX_WIDTH = D_MODEL
MEM_LEN = 256
MEM_HEADS = 4
MEM_WIDTH = D_MODEL // 4
MEM_HEAD_DIM = MEM_WIDTH // MEM_HEADS
TOK_WIDTH = MIX_WIDTH - MEM_WIDTH

RET_HEADS = 6
RET_HEAD_DIM = TOK_WIDTH // RET_HEADS
RET_CHUNK = 128
RET_ROPE_BASE = 10000.0
GN_EPS = 1e-5

NA_HEADS = 12
NA_HEAD_DIM = TOK_WIDTH // NA_HEADS
GRID_W = 64
NA_WIN_R = 8
NA_WIN_C = 16
NA_QB = 16
NA_KB = 32

FFN_HIDDEN = ((8 * D_MODEL + 3 * 256 - 1) // (3 * 256)) * 256
EPS = 1e-6

kernel_name = "hybrid_retention_natten_memory_encoder"

def rms_norm(x, g):
    xf = x.astype(jnp.float32)
    y = xf * lax.rsqrt(jnp.mean(xf * xf, axis=-1, keepdims=True) + EPS)
    return (y * g.astype(jnp.float32)).astype(x.dtype)

def to_heads(t, n_heads):
    b, s, w = t.shape
    return t.reshape(b, s, n_heads, w // n_heads).transpose(0, 2, 1, 3)

def from_heads(t):
    b, n, s, d = t.shape
    return t.transpose(0, 2, 1, 3).reshape(b, s, n * d)

def rotary(t, pos):
    d = t.shape[-1]
    half = d // 2
    inv = RET_ROPE_BASE ** (-jnp.arange(half, dtype=jnp.float32) / half)
    ang = pos[:, None] * inv[None, :]
    c, s = jnp.cos(ang), jnp.sin(ang)
    t1, t2 = t[..., :half], t[..., half:]
    return jnp.concatenate([t1 * c - t2 * s, t1 * s + t2 * c], axis=-1)

def retention_one_direction(q, k, v, log_gamma):
    b, h, t, dk = q.shape
    dv = v.shape[-1]
    c = RET_CHUNK
    n = t // c
    qc = q.reshape(b, h, n, c, dk)
    kc = k.reshape(b, h, n, c, dk)
    vc = v.reshape(b, h, n, c, dv)
    idx = jnp.arange(c, dtype=jnp.float32)
    rel = idx[:, None] - idx[None, :]
    lg = log_gamma[:, None, None]
    intra_decay = jnp.where(rel >= 0, jnp.exp(lg * jnp.maximum(rel, 0.0)), 0.0)
    scores = jnp.einsum('bhncd,bhnsd->bhncs', qc, kc) * intra_decay[None, :, None]
    out = jnp.einsum('bhncs,bhnse->bhnce', scores, vc)
    k_dec = jnp.exp(log_gamma[:, None] * (c - 1 - idx)[None, :])
    q_dec = jnp.exp(log_gamma[:, None] * (idx + 1)[None, :])
    chunk_dec = jnp.exp(log_gamma * c)[None, :, None, None]
    kv = jnp.einsum('bhncd,bhnce->nbhde', kc * k_dec[None, :, None, :, None], vc)

    def step(state, kv_n):
        return state * chunk_dec + kv_n, state

    _, prev = lax.scan(step, jnp.zeros((b, h, dk, dv), jnp.float32), kv)
    out = out + jnp.einsum('bhncd,nbhde->bhnce', qc * q_dec[None, :, None, :, None], prev)
    return out.reshape(b, h, t, dv)

def memory_attention(mq, mem_k, mem_v):
    b, s, _ = mq.shape
    qh = mq.reshape(b, s, MEM_HEADS, MEM_HEAD_DIM)
    sc = jnp.einsum('bthd,blhd->bhtl', qh, mem_k).astype(jnp.float32) * (MEM_HEAD_DIM ** -0.5)
    p = jax.nn.softmax(sc, axis=-1).astype(mem_v.dtype)
    o = jnp.einsum('bhtl,blhd->bthd', p, mem_v)
    return o.reshape(b, s, MEM_WIDTH)

def retention_layer(a, mem_k, mem_v, w_in, w_out, gn_g, gn_b, decay):
    b, s, _ = a.shape
    proj = a @ w_in
    q, k, v, g, mq = jnp.split(proj, [TOK_WIDTH, 2 * TOK_WIDTH, 3 * TOK_WIDTH, 4 * TOK_WIDTH], axis=-1)
    pos = jnp.arange(s, dtype=jnp.float32)
    qh = rotary(to_heads(q, RET_HEADS).astype(jnp.float32), pos)
    kh = rotary(to_heads(k, RET_HEADS).astype(jnp.float32), pos) * (RET_HEAD_DIM ** -0.5)
    vh = to_heads(v, RET_HEADS).astype(jnp.float32)
    log_gamma = -jnp.exp(decay.astype(jnp.float32))
    y_fwd = retention_one_direction(qh, kh, vh, log_gamma[0])
    y_bwd = jnp.flip(retention_one_direction(jnp.flip(qh, 2), jnp.flip(kh, 2), jnp.flip(vh, 2),
                                             log_gamma[1]), 2)
    y = y_fwd + y_bwd
    mu = jnp.mean(y, axis=-1, keepdims=True)
    var = jnp.mean(jnp.square(y - mu), axis=-1, keepdims=True)
    y = from_heads((y - mu) * lax.rsqrt(var + GN_EPS))
    y = y * gn_g.astype(jnp.float32) + gn_b.astype(jnp.float32)
    y = (jax.nn.silu(g.astype(jnp.float32)) * y).astype(a.dtype)
    m = memory_attention(mq, mem_k, mem_v)
    return jnp.concatenate([y, m], axis=-1) @ w_out

def neighbourhood_attention(q, k, v, rpb):
    b, h, t, d = q.shape
    rows = t // GRID_W
    wr = min(NA_WIN_R, rows)
    wc = NA_WIN_C
    n_cb = GRID_W // NA_QB
    qg = q.reshape(b, h, rows, n_cb, NA_QB, d) * (d ** -0.5)
    kg = k.reshape(b, h, rows, GRID_W, d)
    vg = v.reshape(b, h, rows, GRID_W, d)
    qcol = np.arange(GRID_W).reshape(n_cb, NA_QB)
    kstart = np.clip(np.arange(n_cb) * NA_QB - NA_WIN_C // 2, 0, GRID_W - NA_KB)
    kcol = kstart[:, None] + np.arange(NA_KB)[None, :]
    wstart = np.clip(qcol - wc // 2, 0, GRID_W - wc)
    col_valid = (kcol[:, None, :] >= wstart[:, :, None]) & (kcol[:, None, :] < wstart[:, :, None] + wc)
    dc_idx = np.clip(kcol[:, None, :] - qcol[:, :, None] + NA_WIN_C - 1, 0, 2 * NA_WIN_C - 2)
    mask = jnp.asarray(col_valid)[:, :, None, :]
    rpb_c = rpb[:, :, dc_idx].astype(jnp.float32)

    def one_row(r):
        rs = jnp.clip(r - wr // 2, 0, rows - wr)
        k_blk = lax.dynamic_slice_in_dim(kg, rs, wr, axis=2)[:, :, :, kcol]
        v_blk = lax.dynamic_slice_in_dim(vg, rs, wr, axis=2)[:, :, :, kcol]
        q_row = lax.dynamic_index_in_dim(qg, r, axis=2, keepdims=False)
        s = jnp.einsum('bhjqd,bhrjkd->bhjqrk', q_row, k_blk).astype(jnp.float32)
        dr_idx = rs + jnp.arange(wr) - r + NA_WIN_R - 1
        bias = jnp.take(rpb_c, dr_idx, axis=1).transpose(0, 2, 3, 1, 4)
        s = jnp.where(mask, s + bias, -1e30)
        p = jax.nn.softmax(s, axis=(-2, -1)).astype(v.dtype)
        return jnp.einsum('bhjqrk,bhrjkd->bhjqd', p, v_blk)

    out = lax.map(one_row, jnp.arange(rows))
    return out.transpose(1, 2, 0, 3, 4, 5).reshape(b, h, t, d)

def na_layer(a, mem_k, mem_v, w_in, w_out, rpb):
    proj = a @ w_in
    q, k, v, mq = jnp.split(proj, [TOK_WIDTH, 2 * TOK_WIDTH, 3 * TOK_WIDTH], axis=-1)
    o = neighbourhood_attention(to_heads(q, NA_HEADS), to_heads(k, NA_HEADS), to_heads(v, NA_HEADS), rpb)
    m = memory_attention(mq, mem_k, mem_v)
    return jnp.concatenate([from_heads(o), m], axis=-1) @ w_out

def setup_inputs(seed: int = 0) -> dict:
    key = jax.random.key(seed)
    ks = jax.random.split(key, 16)
    f32 = jnp.float32
    x = jax.random.normal(ks[0], (BATCH, SEQ, D_MODEL), f32)
    mem = jax.random.normal(ks[1], (BATCH, MEM_LEN, D_MODEL), f32)
    norm_g = 1.0 + 0.02 * jax.random.normal(ks[2], (DEPTH, 4, D_MODEL), f32)
    mem_norm_g = 1.0 + 0.02 * jax.random.normal(ks[3], (D_MODEL,), f32)
    mem_w_kv = jax.random.normal(ks[4], (D_MODEL, 2 * MEM_WIDTH), f32) * D_MODEL ** -0.5
    ret_w_in = jax.random.normal(ks[5], (N_RET_LAYERS, D_MODEL, 4 * TOK_WIDTH + MEM_WIDTH), f32) * D_MODEL ** -0.5
    ret_w_out = jax.random.normal(ks[6], (N_RET_LAYERS, MIX_WIDTH, D_MODEL), f32) * MIX_WIDTH ** -0.5
    ret_gn_g = 1.0 + 0.02 * jax.random.normal(ks[7], (N_RET_LAYERS, TOK_WIDTH), f32)
    ret_gn_b = 0.02 * jax.random.normal(ks[8], (N_RET_LAYERS, TOK_WIDTH), f32)
    base = jnp.log(-jnp.log(1.0 - 2.0 ** (-5.0 - jnp.arange(RET_HEADS, dtype=f32))))
    ret_decay = base[None, None, :] + 0.05 * jax.random.normal(ks[9], (N_RET_LAYERS, 2, RET_HEADS), f32)
    na_w_in = jax.random.normal(ks[10], (N_NA_LAYERS, D_MODEL, 3 * TOK_WIDTH + MEM_WIDTH), f32) * D_MODEL ** -0.5
    na_w_out = jax.random.normal(ks[11], (N_NA_LAYERS, MIX_WIDTH, D_MODEL), f32) * MIX_WIDTH ** -0.5
    na_rpb = 0.1 * jax.random.normal(ks[12], (N_NA_LAYERS, NA_HEADS, 2 * NA_WIN_R - 1, 2 * NA_WIN_C - 1), f32)
    ffn_w_in = jax.random.normal(ks[13], (DEPTH, D_MODEL, 2 * FFN_HIDDEN), f32) * D_MODEL ** -0.5
    ffn_w_out = jax.random.normal(ks[14], (DEPTH, FFN_HIDDEN, D_MODEL), f32) * FFN_HIDDEN ** -0.5
    return {"x": x, "mem": mem, "norm_g": norm_g, "mem_norm_g": mem_norm_g, "mem_w_kv": mem_w_kv,
            "ret_w_in": ret_w_in, "ret_w_out": ret_w_out, "ret_gn_g": ret_gn_g, "ret_gn_b": ret_gn_b,
            "ret_decay": ret_decay, "na_w_in": na_w_in, "na_w_out": na_w_out, "na_rpb": na_rpb,
            "ffn_w_in": ffn_w_in, "ffn_w_out": ffn_w_out}

def reference(x, mem, norm_g, mem_norm_g, mem_w_kv, ret_w_in, ret_w_out, ret_gn_g, ret_gn_b,
              ret_decay, na_w_in, na_w_out, na_rpb, ffn_w_in, ffn_w_out):
    b, l, _ = mem.shape
    mkv = rms_norm(mem, mem_norm_g) @ mem_w_kv
    mem_k, mem_v = jnp.split(mkv, 2, axis=-1)
    mem_k = mem_k.reshape(b, l, MEM_HEADS, MEM_HEAD_DIM)
    mem_v = mem_v.reshape(b, l, MEM_HEADS, MEM_HEAD_DIM)
    h = x
    for i in range(DEPTH):
        j = i // N_MIXERS
        a = rms_norm(h, norm_g[i, 0])
        if i % N_MIXERS == 0:
            y = retention_layer(a, mem_k, mem_v, ret_w_in[j], ret_w_out[j], ret_gn_g[j], ret_gn_b[j], ret_decay[j])
        else:
            y = na_layer(a, mem_k, mem_v, na_w_in[j], na_w_out[j], na_rpb[j])
        h = h + rms_norm(y, norm_g[i, 1])
        a = rms_norm(h, norm_g[i, 2])
        gate, up = jnp.split(a @ ffn_w_in[i], 2, axis=-1)
        f = (jax.nn.silu(gate) * up) @ ffn_w_out[i]
        h = h + rms_norm(f, norm_g[i, 3])
    return h


_drawn_inputs = setup_inputs


def setup_inputs(seed=0):
    import zlib

    import numpy as np

    out = dict(_drawn_inputs(seed))
    spreads = {}
    factors = {'mem_norm_g': 8.0, 'ret_gn_g': 12.435, 'ret_gn_b': 26.221, 'na_rpb': 25.409}
    for name, (base, spread) in spreads.items():
        noise = np.random.default_rng([zlib.crc32(name.encode()), seed]).standard_normal(out[name].shape)
        drawn = base * np.exp(spread * noise) if base else spread * noise
        out[name] = __import__('jax').numpy.asarray(drawn.astype(out[name].dtype))
    for name, factor in factors.items():
        out[name] = (out[name] * factor).astype(out[name].dtype)
    return out
```

```python
import numpy as np
from contextlib import ExitStack
import concourse.bass as bass
from concourse import mybir

P = 128
D = 1024
KD = D // P
SEQ = 1024
HALF = SEQ // 2
TT = HALF // P
MEM = 256
RH = 6
HP = 6
ROWS, GW = 16, 64
WR, WC = 8, 16
HID = 2816
KH = HID // P
RING = 3
UW = 1024
NA_BIAS = 15 * GW
RPB_PAD = 64

U_MEM = 0
U_RET = U_MEM + 4
U_RETH = U_RET + 2
U_OUT0 = U_RETH + 4 * RH
U_FF0 = U_OUT0 + 2 * KD
U_NA = U_FF0 + 2 * (3 * KH)
U_NAH = U_NA + 2
U_OUT1 = U_NAH + 3 * HP
U_FF1 = U_OUT1 + 2 * KD
U_END = U_FF1 + 2 * (3 * KH)
N_T = 34
N_E = 32


def unit_rows():
    rows, at = [], 0
    for count, times, phase in ((4, 1, "mem"), (4 * RH + 2, 1, "ret"), (KD, 2, "out"), (3 * KH, 2, "ffn"),
                                (3 * HP + 2, 1, "na"), (KD, 2, "out"), (3 * KH, 2, "ffn")):
        for _ in range(times):
            rows += list(range(at, at + count))
        at += count
    return rows


def trunk_program(nc, wpack, x, mem, gains, gain_rows, gn, decay, rpb, ropes, decay_consts, na_masks, ident_c, out):
    F32, F32R, BF16 = mybir.dt.float32, mybir.dt.float32r, mybir.dt.bfloat16
    ACT = mybir.ActivationFunctionType
    ALU = mybir.AluOpType
    AX = mybir.AxisListType
    ROW = unit_rows()
    assert len(ROW) == U_END

    h_dram = nc.dram_tensor("h_scratch", [SEQ, D], F32).ap()
    cat_dram = nc.dram_tensor("cat_scratch", [2, KD, P, SEQ], F32).ap()
    memkv_dram = nc.dram_tensor("memkv_scratch", [P, 1536], F32).ap()
    rpb_n = 12 * 15 * 31
    rpb_dram = nc.dram_tensor("rpb_scratch", [RPB_PAD + rpb_n + RPB_PAD], F32)


    KB = 1024
    base = (nc.sbuf_base + 31) // 32 * 32

    def at(name, shape, dt, off):
        return nc.alloc_sbuf_tensor_at(name, shape, dt, offset=base + off)

    stage = at("stage", [P, RING, UW], F32, 0)
    whi = at("whi", [P, RING, UW], F32R, 12 * KB)
    wlo = at("wlo", [P, RING, UW], F32R, 24 * KB)
    SM = 36 * KB
    ident = at("ident", [P, P], F32, SM)
    sumsq = at("sumsq", [P, 72], F32, SM + 512)
    msq = at("msq", [P, 72], F32, SM + 800)
    rstd = at("rstd", [P, 72], F32, SM + 1088)
    gT = at("gT", [P, 5, KD], F32, SM + 1376)
    gnT = at("gnT", [P, 2, RH], F32, SM + 1536)
    lgb = at("lgb", [P, 12], F32, SM + 1600)
    lg = at("lg", [P, 2, RH], F32, SM + 1664)
    kdec = at("kdec", [P, 2, RH], F32, SM + 1728)
    cdec = at("cdec", [P, 2, RH], F32, SM + 1792)
    negmax = at("negmax", [P, 4, 2], F32, SM + 1920)
    rowsum = at("rowsum", [P, 4, 2], F32, SM + 1952)
    rowinv = at("rowinv", [P, 4, 2], F32, SM + 1984)
    stats = at("stats", [P, 8, 6], F32, SM + 2048)
    mv = at("mv", [P, 8, 2], F32, SM + 2240)
    gvar = at("gvar", [P, 8], F32, SM + 2304)
    grstd = at("grstd", [P, 8], F32, SM + 2336)
    minus_half = at("minus_half", [P, 8], F32, SM + 2368)
    maxraw = at("maxraw", [P, 4, 2], F32, SM + 2400)
    colc = at("colc", [P, 8], F32, SM + 2528)
    kprod = at("kprod", [P, 2, RH], F32, SM + 2432)
    Z = SM + 3 * KB
    Y = at("Y", [P, TT, D], F32, Z)
    vfb = at("vfb", [P, 8, 2, P], F32, Z)
    qfb = at("qfb", [P, 2, SEQ], F32, Z)
    kTn = at("kTn", [P, 2, SEQ], F32, Z)
    OC = at("OC", [P, 2, SEQ], F32, Z + 8 * KB)
    Hb = at("Hb", [P, TT, D], F32, Z + 16 * KB)
    gB = at("gB", [P, D], F32, Z + 32 * KB)
    junk = [at("junk0", [P, D], BF16, Z + 36 * KB), at("junk1", [P, D], BF16, Z + 166 * KB)]
    X = Z + 38 * KB
    aT = at("aT", [P, 2, 2, KD, HALF], F32R, X)
    catf = at("catf", [P, KD, SEQ], F32, X)
    catT = at("catT", [P, 2, 2, KD, HALF], F32R, X + 32 * KB)
    hid = at("hid", [P, 2, KH, HALF], F32R, X + 32 * KB)
    sg = at("sg", [P, RING, HALF], F32, X + 120 * KB)
    hidf = at("hidf", [P, HALF], F32, X + 126 * KB)
    Yb = at("Yb", [P, TT, D], F32, X + 96 * KB)
    W = X + 64 * KB
    W += 6 * KB
    bdK = at("bdK", [P, 2, 2 * MEM], F32, W + 53 * KB)
    memV = at("memV", [P, 2, 2 * P], F32, W + 57 * KB)
    MQ = at("MQ", [P, 2, SEQ], F32, Z + 16 * KB)
    SB = at("SB", [P, 3, 512], F32, Z + 24 * KB)
    PT = at("PT", [P, 2, 512], F32, Z + 32 * KB)
    ropeC = at("ropeC", [P, SEQ], F32, W)
    ropeS = at("ropeS", [P, SEQ], F32, W + 4 * KB)
    QD = at("QD", [P, 2, RH, P], F32, W + 8 * KB)
    DM = at("DM", [P, RH, P], F32, W + 14 * KB)
    qT = at("qT", [P, 2, SEQ], F32, W + 17 * KB)
    kT = at("kT", [P, SEQ], F32, W + 25 * KB)
    Ktok = at("Ktok", [P, 8, P], F32, W + 29 * KB)
    V = at("V", [P, 8, P], F32, W + 33 * KB)
    ST = at("ST", [P, 8, P], F32, W + 37 * KB)
    vT = at("vT", [P, SEQ], F32, W + 41 * KB)
    states = at("states", [P, 8, 2, P], F32, W + 45 * KB)
    rtmp = at("rtmp", [P, HALF], F32, Z + 36 * KB)
    dconst = at("dconst", [P, 6, P], F32, Z + 32 * KB)
    dexp = at("dexp", [P, 2, P], F32, Z + 35 * KB)
    mvT = at("mvT", [P, 2, MEM], F32, W + 17 * KB)
    qbd = at("qbd", [P, 2, ROWS, 2, GW], F32, W)
    TB = at("TB", [P, 2, 15, GW], F32, W + 16 * KB)
    nmask = at("nmask", [P, 2, GW], F32, W + 24 * KB)
    vTn = at("vTn", [P, SEQ], F32, W + 25 * KB)
    Ve = at("Ve", [P, 8, P], F32, W + 29 * KB)
    Vo = at("Vo", [P, 7, P], F32, W + 33 * KB)

    with ExitStack() as ctx:
        PS = ctx.enter_context(nc.psum_tensor("PS", [P, 8, 512], F32))

        def sem(name):
            return ctx.enter_context(nc.semaphore(name))

        w_in = [sem(f"w_in{r}") for r in range(RING)]
        w_hi, w_lo, w_used = sem("w_hi"), sem("w_lo"), sem("w_used")
        c_ld = sem("c_ld")
        c_ids = sem("c_ids")
        x_ld = [sem(f"x_ld{i}") for i in range(10)]
        h_ld = [sem(f"h_ld{i}") for i in range(TT)]
        h_st = [sem(f"h_st{i}") for i in range(TT)]
        g_ld, pre_sq, pre_rs, xs = sem("g_ld"), sem("pre_sq"), sem("pre_rs"), sem("xs")
        t_done, t_low, a_hi, a_lo = sem("t_done"), sem("t_low"), sem("a_hi"), sem("a_lo")
        y_done, y_cp, y_sq, post_rs, h_new = sem("y_done"), sem("y_cp"), sem("y_sq"), sem("post_rs"), sem("h_new")
        g_act, hid_t, hid_rdy = sem("g_act"), sem("hid_t"), sem("hid_rdy")
        ev_act, ev_dve = sem("ev_act"), sem("ev_dve")
        oc_st = [sem(f"oc_st{i}") for i in range(2)]
        cat_ld = [sem(f"cat_ld{k}") for k in range(KD)]
        cat_hi, cat_lo = sem("cat_hi"), sem("cat_lo")
        dec_e, dec_rdy, mh_rdy, zer = sem("dec_e"), sem("dec_rdy"), sem("mh_rdy"), sem("zer")
        mvt, memv_rdy, mkv_st, mkv_ld = sem("mvt"), sem("memv_rdy"), sem("mkv_st"), sem("mkv_ld")
        ktr, vtr, st_mm, kv_mm, out_mm, y_tr = (sem(n) for n in ("ktr", "vtr", "st_mm", "kv_mm", "out_mm", "y_tr"))
        ktok_rdy, vfb_rdy, v_rdy, st_rdy, scan_rdy, qfb_rdy = (
            sem(n) for n in ("ktok_rdy", "vfb_rdy", "v_rdy", "st_rdy", "scan_rdy", "qfb_rdy"))
        var_rdy, grs_rdy, yn_rdy, aff, oc_rdy = (sem(n) for n in ("var_rdy", "grs_rdy", "yn_rdy", "aff", "oc_rdy"))
        s_mm, s_add, s_exp, s_nrm, s_tr, pt_ev, pv, o_ev = (
            sem(n) for n in ("s_mm", "s_add", "s_exp", "s_nrm", "s_tr", "pt_ev", "pv", "o_ev"))
        vn_tr, vn_a, vn_d = sem("vn_tr"), sem("vn_a"), sem("vn_d")
        rpb_st, tb_ld, tb_m, tb_rdy, nmask_ld, qz = (
            sem("rpb_st"), [sem("tb_ld0"), sem("tb_ld1")], sem("tb_m"), sem("tb_rdy"), sem("nmask_ld"), sem("qz"))
        d_own, p_own, a_own = sem("d_own"), sem("p_own"), sem("a_own")

        EV = {}
        counts = {"a": 0, "d": 0}

        def taken_by(n, who):
            counts[who] += 1
            EV[n] = (ev_act if who == "a" else ev_dve, counts[who])

        for n in range(4):
            taken_by(n, "ddaa"[n])
        for n in range(2):
            taken_by(U_RET + n, "a")
        for n in range(4 * RH):
            taken_by(U_RETH + n, "ddaa"[n % 4])
        for n in range(2):
            taken_by(U_NA + n, "a")
        for n in range(3 * HP):
            taken_by(U_NAH + n, "ada"[n % 3])

        def tiles_before(t):
            return 0 if t == 0 else 2 + 4 * (t - 1)

        def set_of(s, th):
            return 2 * s + 1 + th

        def y_tiles(s, th):
            return Yb if s in (0, 2) and th == 0 else Y

        def set_tiles(t):
            return Hb if t == 0 else Yb if t in (1, 3, 7) else Y

        def pre_tile(xi):
            return Hb[:, xi, :] if xi < 2 else Yb[:, xi - 2, :] if xi < 6 else Y[:, xi - 6, :]

        GAIN = [4, 0, 0, 1, 1, 2, 2, 3, 3]
        U_FF = [U_FF0, U_FF1]
        U_OUT = [U_OUT0, U_OUT1]
        U_IN = [U_RET, U_NA]
        N_IN = [4 * RH + 2, 3 * HP + 2]
        R_A = [0, 16]
        R_B = [8, 24 + HP * ROWS]
        R_ROW = 24

        def o_count(r):
            return r if r <= R_ROW else R_ROW + (min(r, R_B[1]) - R_ROW) // 4 + max(0, r - R_B[1])

        def banks(r):
            return (r % 2, 2, 3) if R_B[0] <= r < R_A[1] else (4 + r % 2, 6, 7)

        def key_row(r):
            return min(max(r - WR // 2, 0), ROWS - WR)

        PIECES = 3 * KD

        def pieces_at(t, total=PIECES, steps=ROWS):
            return range(total * t // steps, total * (t + 1) // steps) if t < steps else range(0)

        def units_done(t, total, steps):
            return [u for u in range(total // KD) if KD * u + KD - 1 in pieces_at(t, total, steps)]

        M_STEPS = 8 + 3
        LAST = ROWS + 4

        block = ctx.enter_context(nc.Block())

        @block.sync
        def _(sp):
            issued = [0]

            def load_units(upto):
                for n in range(issued[0], min(upto, U_END)):
                    if n >= RING:
                        sp.wait_ge(w_lo, n - RING + 1)
                    sp.dma_start(stage[:, n % RING, :], wpack[ROW[n], :, :]).then_inc(w_in[n % RING], 16)
                issued[0] = max(issued[0], min(upto, U_END))

            def load_pre(xi):
                src = mem[xi * P:(xi + 1) * P, :] if xi < 2 else x[(xi - 2) * P:(xi - 1) * P, :]
                sp.dma_start(pre_tile(xi), src).then_inc(x_ld[xi], 16)

            def load_h(e):
                s, t = e // 8, e % 8
                if e >= TT:
                    sp.wait_ge(h_st[e % TT], 16 * (e // TT))
                if e >= TT and e - TT < 24:
                    sp.wait_ge(xs, 10 + e - TT + 1)
                src = x if s == 0 else h_dram
                sp.dma_start(Hb[:, e % TT, :], src[t * P:(t + 1) * P, :]).then_inc(h_ld[e % TT], 16)

            def store_h(e):
                t = e % 8
                sp.wait_ge(h_new, e + 1)
                dst = h_dram if e < 24 else out
                sp.dma_start(dst[t * P:(t + 1) * P, :], Hb[:, e % TT, :]).then_inc(h_st[e % TT], 16)

            def load_gain(s):
                if s:
                    sp.wait_ge(h_new, 8 * s)
                sp.dma_start(gB[:, :], gain_rows[s:s + 1, :].partition_broadcast(P)).then_inc(g_ld, 16)

            def post(s, th):
                for i in range(TT):
                    store_h(8 * s + 4 * th + i)
                if (s, th) != (1, 1):
                    for i in range(TT):
                        if 8 * s + 4 * th + i + TT < N_E:
                            load_h(8 * s + 4 * th + i + TT)
                    if th and s < 3:
                        load_gain(s + 1)

            def before_out(l):
                for i in range(TT):
                    load_h(16 * l + i)
                load_gain(2 * l)

            def store_cat(c):
                sp.wait_ge(oc_rdy, c + 1)
                sp.dma_start(cat_dram[c // 8, c % 8, :, :], OC[:, c % 2, :]).then_inc(oc_st[c % 2], 16)

            def cat_back(l, tiles):
                sp.wait_ge(w_used, U_IN[l] + N_IN[l])
                for k in tiles:
                    sp.wait_ge(oc_st[k % 2], 16 * ((8 * l + k) // 2 + 1))
                    sp.dma_start(catf[:, k, :], cat_dram[l, k, :, :]).then_inc(cat_ld[k], 16)

            def ffn(l):
                for th in range(2):
                    n0 = U_FF[l] + 3 * KH * th
                    for j in range(3):
                        load_units(n0 + 2 * j + 7)
                    with sp.Fori(0, 6) as i:
                        for c in range(6):
                            m = n0 + 6 + c + 5
                            sp.wait_ge(w_lo, i * 6 + (m - RING + 1))
                            sp.dma_start(stage[:, m % RING, :], wpack[bass.ds(i * 6 + (ROW[n0] + m - n0), 1), :, :]
                                         .rearrange("a p c -> p (a c)")).then_inc(w_in[m % RING], 16)
                    issued[0] += 36
                    load_units(n0 + 3 * KH + 5)
                    post(1 + 2 * l, th)

            load_pre(0)
            load_pre(1)
            sp.dma_start(ident[:, :], ident_c).then_inc(c_ids, 16)
            sp.dma_start(gT[:, :, :], gains).then_inc(c_ids, 16)
            load_pre(2)
            load_pre(3)
            load_units(1)
            load_pre(4)
            load_pre(5)
            load_units(2)
            for xi in range(6, 10):
                load_pre(xi)
            load_units(5)
            sp.dma_start(dconst[:, :, :], decay_consts[:, 0:6 * P].rearrange("p (a c) -> p a c", a=6)).then_inc(c_ld, 16)
            sp.dma_start(colc[:, :], decay_consts[:, 6 * P:6 * P + 8]).then_inc(c_ld, 16)
            sp.dma_start(lgb[:, :], decay.partition_broadcast(P)).then_inc(c_ld, 16)
            sp.dma_start(gnT[:, :, :], gn).then_inc(c_ld, 16)
            sp.dma_start(ropeC[:, :], ropes[0, :, :]).then_inc(c_ld, 16)
            sp.dma_start(ropeS[:, :], ropes[1, :, :]).then_inc(c_ld, 16)
            sp.dma_start(rpb_dram[RPB_PAD:RPB_PAD + rpb_n], rpb).then_inc(rpb_st, 16)
            sp.wait_ge(zer, 2)
            for first in (0, RPB_PAD + rpb_n):
                sp.dma_start(bass.AP(rpb_dram, first, [[8, 8], [1, 8]]),
                             kprod[0:8, :, :].rearrange("p a c -> p (a c)")[:, 0:8]).then_inc(rpb_st, 16)
            load_units(U_RET + 5)
            sp.wait_ge(memv_rdy, 1)
            sp.wait_ge(ev_dve, 2)
            sp.dma_start(memkv_dram[:, 0:1024], bdK[:, :, :].rearrange("p a c -> p (a c)")).then_inc(mkv_st, 16)
            sp.dma_start(memkv_dram[:, 1024:1536], memV[:, :, :].rearrange("p a c -> p (a c)")).then_inc(mkv_st, 16)
            load_units(U_RETH + 4 + 5)
            store_cat(0)
            for h in range(1, RH):
                load_units(U_RETH + 4 * h + 4 + 5)
                store_cat(h)
            load_units(U_OUT0 + 5)
            cat_back(0, range(RH))
            store_cat(6)
            cat_back(0, [6])
            store_cat(7)
            cat_back(0, [7])
            before_out(0)
            for th in range(2):
                load_units(U_OUT0 + KD * (th + 1) + 5)
                post(0, th)
            ffn(0)

            def load_bias(hp):
                if hp >= 2:
                    sp.wait_ge(s_add, R_ROW + ROWS * (hp - 1))
                for g in range(2):
                    first = RPB_PAD + (2 * hp + g) * 465 + WC - 1 - (GW - 1)
                    src = bass.AP(rpb_dram, first, [[1, GW], [31, 15], [1, GW]])
                    sp.dma_start(TB[GW * g:GW * g + GW, hp % 2, :, :], src).then_inc(tb_ld[hp % 2], 16)

            sp.wait_ge(w_used, U_NA)
            sp.wait_ge(mkv_st, 32)
            sp.wait_ge(pre_sq, 26)
            sp.dma_start(bdK[:, :, :].rearrange("p a c -> p (a c)"), memkv_dram[:, 0:1024]).then_inc(mkv_ld, 16)
            sp.dma_start(memV[:, :, :].rearrange("p a c -> p (a c)"), memkv_dram[:, 1024:1536]).then_inc(mkv_ld, 16)
            sp.dma_start(nmask[:, :, :], na_masks).then_inc(nmask_ld, 16)
            sp.wait_ge(rpb_st, 48)
            load_bias(0)
            load_bias(1)
            load_units(U_NAH + 3 + 5)
            store_cat(8)
            for hp in range(1, HP):
                load_units(U_NAH + 3 * hp + 3 + 5)
                store_cat(8 + hp)
                if hp + 1 < HP:
                    load_bias(hp + 1)
            load_units(U_OUT1 + 5)
            cat_back(1, range(HP))
            store_cat(8 + 6)
            cat_back(1, [6])
            store_cat(8 + 7)
            cat_back(1, [7])
            before_out(1)
            for th in range(2):
                load_units(U_OUT1 + KD * (th + 1) + 5)
                post(2, th)
            ffn(1)
            for i in range(TT):
                sp.wait_ge(h_st[i], 16 * (N_E // TT))

        @block.gpsimd
        def _(pool):
            done = [0]
            own = [0]

            def link(ins):
                own[0] += 1
                ins.then_inc(p_own, 1)
                pool.wait_ge(p_own, own[0])

            def split_lo(n, slot, need):
                pool.wait_ge(w_hi, need)
                pool.tensor_tensor(wlo[:, slot, :], stage[:, slot, :], whi[:, slot, :].bitcast(F32), ALU.subtract)\
                    .then_inc(w_lo, 1)

            def los(upto):
                for n in range(done[0], min(upto, U_END)):
                    split_lo(n, n % RING, n + 1)
                done[0] = max(done[0], min(upto, U_END))

            def inv_rms(col, ready, need, signal):
                pool.wait_ge(ready, need)
                link(pool.tensor_scalar(msq[:, col:col + 1], sumsq[:, col:col + 1], 1.0 / D, 1e-6, ALU.mult, ALU.add))
                pool.tensor_tensor(rstd[:, col:col + 1], msq[:, col:col + 1], minus_half[:, 0:1], ALU.pow)\
                    .then_inc(signal, 1)

            def pre(xi):
                inv_rms(xi, pre_sq, xi + 1, pre_rs)

            def post(s, th):
                for i in range(TT):
                    e = 8 * s + 4 * th + i
                    inv_rms(N_T + e, y_sq, e + 1, post_rs)
                if s < 3:
                    for i in range(TT):
                        pre(10 + 8 * s + 4 * th + i)

            def ffn(l):
                for th in range(2):
                    n0 = U_FF[l] + 3 * KH * th
                    for j in range(3):
                        los(n0 + 2 * j + 4)
                    with pool.Fori(0, 6) as i:
                        for c in range(6):
                            m = n0 + 6 + c + 2
                            split_lo(m, m % RING, i * 6 + (m + 1))
                    done[0] += 36
                    los(n0 + 3 * KH + 2)
                    post(1 + 2 * l, th)

            pool.memset(minus_half[:, :], -0.5).then_inc(mh_rdy, 1)
            pool.wait_ge(mh_rdy, 1)
            pre(0)
            pre(1)
            pool.memset(bdK[:, :, :], 0.0).then_inc(zer, 1)
            pool.memset(kprod[:, :, :], 0.0).then_inc(zer, 1)
            pool.wait_ge(zer, 2)
            pre(2)
            pre(3)
            los(1)
            pre(4)
            pre(5)
            los(3)
            for xi in range(6, 10):
                pre(xi)
                if xi < 8:
                    los(xi - 2)
            los(U_RETH + 2)

            for h in range(RH + 1):
                n = U_RETH + 4 * h
                los(min(n + 3, U_OUT0 + 2))
                if h:
                    los(min(n + 5, U_OUT0 + 2))
                    pool.wait_ge(var_rdy, h)
                    link(pool.tensor_scalar(gvar[:, :], mv[:, :, 1], 1.0, 1e-5, ALU.mult, ALU.add))
                    pool.tensor_tensor(grstd[:, :], gvar[:, :], minus_half[:, :], ALU.pow).then_inc(grs_rdy, 1)
                if h < RH:
                    los(n + 6)
            los(U_OUT0 + 2)
            for th in range(2):
                los(U_OUT0 + KD * (th + 1) + 2)
                post(0, th)
            ffn(0)
            pool.wait_ge(w_used, U_NA)
            pool.wait_ge(pre_rs, 26)
            pool.wait_ge(w_lo, done[0])
            for g in range(2):
                for b in range(2):
                    pool.memset(qbd[GW * b:GW * b + GW, g, :, 1 - b, :], 0.0).then_inc(qz, 1)
                    pool.wait_ge(qz, 2 * g + b + 1)

            def mask_bias(hp):
                pool.wait_ge(tb_ld[hp % 2], 32 * (hp // 2 + 1))
                t = TB[:, hp % 2, :, :]
                link(pool.tensor_tensor(t, t, nmask[:, 0:1, :].to_broadcast([P, 15, GW]), ALU.mult))
                pool.tensor_tensor(t, t, nmask[:, 1:2, :].to_broadcast([P, 15, GW]), ALU.add).then_inc(tb_rdy, 1)

            pool.wait_ge(nmask_ld, 16)
            mask_bias(0)
            los(U_NAH + 2)
            for hp in range(HP):
                los(min(U_NAH + 3 * hp + 5, U_OUT1 + 2))
                if hp + 1 < HP:
                    mask_bias(hp + 1)
            los(U_OUT1 + 2)
            for th in range(2):
                los(U_OUT1 + KD * (th + 1) + 2)
                post(2, th)
            ffn(1)

        @block.scalar
        def _(act):
            done = [0]

            def split_hi(slot, come, used):
                act.wait_ge(w_in[slot], come)
                if used is not None:
                    act.wait_ge(w_used, used)
                act.activation(whi[:, slot, :], stage[:, slot, :], ACT.Copy).then_inc(w_hi, 1)

            def his(upto):
                for n in range(done[0], min(upto, U_END)):
                    split_hi(n % RING, 16 * (n // RING + 1), n - RING + 1 if n >= RING else None)
                done[0] = max(done[0], min(upto, U_END))

            squares = []

            def square(src, col, ready, need, signal):
                act.wait_ge(ready, need)
                n = len(squares)
                if n >= 2:
                    act.wait_ge(*squares[n - 2])
                squares.append((signal, 1 + sum(s is signal for s, _ in squares)))
                act.activation(junk[n % 2][:, :], src, ACT.Square, accum_out=sumsq[:, col:col + 1]).then_inc(signal, 1)

            def pre_x(xi):
                square(pre_tile(xi), xi, x_ld[xi], 16, pre_sq)

            def turn(t):
                width = MEM if t == 0 else HALF
                th = 1 if t in (2, 6) else 0
                if t not in (2, 6):
                    act.wait_ge(t_done, tiles_before(t + 1))
                if t == 0:
                    act.wait_ge(c_ids, 32)
                for k in range(KD):
                    if t in (2, 6) and k == 0:
                        act.wait_ge(t_low, t // 4 + 1)
                    if t in (2, 6) and k == 4:
                        act.wait_ge(t_done, tiles_before(t + 1))
                    bank = 4 + k % 4 if t in (2, 6) else k
                    act.activation(aT[:, th, 0, k, 0:width], PS[:, bank, 0:width], ACT.Copy,
                                   scale=gT[:, GAIN[t], k:k + 1]).then_inc(a_hi, 1)

            def post_in(s, th):
                for i in range(TT):
                    e = 8 * s + 4 * th + i
                    square(PS[:, 2 * i:2 * i + 2, :].rearrange("p a c -> p (a c)"), N_T + e, y_done, e + 1, y_sq)

            def post_out(s, th):
                if s < 3:
                    for i in range(TT):
                        e = 8 * s + 4 * th + i
                        square(Hb[:, i, :], 10 + e, h_new, e + 1, pre_sq)

            def silu_gate(slot, need, free):
                act.wait_ge(w_used, need)
                if free is not None:
                    act.wait_ge(hid_t, free)
                act.activation(sg[:, slot, :], PS[:, 2 * slot, :], ACT.Silu).then_inc(g_act, 1)

            def ffn(l):
                for th in range(2):
                    n0 = U_FF[l] + 3 * KH * th
                    g0 = (2 * l + th) * KH

                    def tile(j):
                        his(n0 + 2 * j + 3)
                        g = g0 + j
                        silu_gate(j % 3, n0 + 2 * j + 1, g - 2 if g >= 3 else None)
                        his(n0 + 2 * j + 4)

                    for j in range(3):
                        tile(j)
                    with act.Fori(0, 6) as i:
                        for c in range(3):
                            m = n0 + 2 * (3 + c)
                            for part in range(2):
                                u = m + 2 + part
                                split_hi(u % RING, i * 32 + 16 * (u // RING + 1), i * 6 + (u - RING + 1))
                                if part == 0:
                                    silu_gate(c, i * 6 + (m + 1), i * 3 + (g0 + 3 + c - 2))
                    done[0] += 36
                    tile(KH - 1)
                    if th == 0 or l == 0:
                        turn(4 * l + 4 + th)
                    his(n0 + 3 * KH + 2)
                    post_in(1 + 2 * l, th)
                    post_out(1 + 2 * l, th)

            def probs(r, is_mem):
                act.wait_ge(s_add, r + 1)
                if is_mem:
                    if r >= 3:
                        act.wait_ge(s_tr, r - 2)
                    bank = banks(r)[0]
                    for g in range(2):
                        ins = act.activation(SB[:, r % 3, MEM * g:MEM * g + MEM], PS[:, bank, MEM * g:MEM * g + MEM],
                                             ACT.Exp, bias=negmax[:, r % 4, g:g + 1], scale=0.125,
                                             accum_out=rowsum[:, r % 4, g:g + 1])
                    ins.then_inc(s_exp, 1)
                else:
                    act.activation(SB[:, r % 3, :], SB[:, r % 3, :], ACT.Exp, bias=negmax[:, r % 4, 0:1], scale=-1.0,
                                   accum_out=rowsum[:, r % 4, 0:1]).then_inc(s_exp, 1)

            def take_pt(r):
                act.wait_ge(s_tr, r + 1)
                if r >= 2:
                    act.wait_ge(pv, r - 1)
                act.activation(PT[:, r % 2, :], PS[:, banks(r)[1], :], ACT.Copy).then_inc(pt_ev, 1)

            def take(n, dst, func=ACT.Copy):
                act.wait_ge(w_used, n + 1)
                for th in range(2):
                    ins = act.activation(dst[:, HALF * th:HALF * th + HALF], PS[:, 2 * (n % 2) + th, :], func)
                ins.then_inc(ev_act, 1)

            def mem_step(r0, t):
                if t < 8:
                    probs(r0 + t, True)
                if 0 <= t - 2 < 8:
                    take_pt(r0 + t - 2)

            def cat_split(l):
                for th in range(2):
                    for k in range(KD):
                        act.wait_ge(cat_ld[k], 16 * (l + 1))
                        act.activation(catT[:, th, 0, k, :], catf[:, k, HALF * th:HALF * th + HALF], ACT.Copy)\
                           .then_inc(cat_hi, 1)

            for xi in range(4):
                pre_x(xi)
            his(1)
            pre_x(4)
            pre_x(5)
            turn(0)
            his(3)
            for xi in range(6, 10):
                pre_x(xi)
                if xi == 8:
                    act.wait_ge(w_used, 3)
                    act.activation(mvT[:, 0, :], PS[:, 0, 0:MEM], ACT.Copy).then_inc(ev_act, 1)
                    act.wait_ge(w_used, 4)
                    act.activation(mvT[:, 1, :], PS[:, 2, 0:MEM], ACT.Copy).then_inc(ev_act, 1)
                elif xi < 8:
                    his(xi - 2)
            turn(1)
            his(U_RET + 2)
            turn(2)
            act.wait_ge(c_ld, 96)
            act.activation(lgb[:, :], lgb[:, :], ACT.Exp).then_inc(dec_e, 1)
            act.wait_ge(dec_rdy, 1)
            act.activation(kdec[:, :, :], kprod[:, :, :], ACT.Exp)
            act.activation(cdec[:, :, :], lg[:, :, :], ACT.Exp, scale=float(P)).then_inc(dec_e, 1)
            for d in range(2):
                for h in range(RH):
                    ins = act.activation(QD[:, d, h, :], dconst[:, 4 + d, :], ACT.Exp, scale=lg[:, d, h:h + 1])
            ins.then_inc(dec_e, 1)
            for h in range(RH):
                if h:
                    act.wait_ge(dec_rdy, 1 + h)
                for d in range(2):
                    ins = act.activation(dexp[:, d, :], dconst[:, d, :], ACT.Exp, scale=lg[:, d, h:h + 1])
                ins.then_inc(dec_e, 1)
            his(U_RET + 3)
            take(U_RET, MQ[:, 0, :])
            his(U_RET + 4)
            take(U_RET + 1, MQ[:, 1, :])

            def take_value_gate(h, i):
                n = U_RETH + 4 * h + i
                his(n + 3)
                if i == 2:
                    take(n, vT[:, :])
                if i == 3:
                    c = 1 + h
                    if c >= 2:
                        act.wait_ge(oc_st[c % 2], 16 * (c // 2))
                    take(n, OC[:, c % 2, :], ACT.Silu)

            for t in range(M_STEPS):
                mem_step(R_A[0], t)
                for u in units_done(t, 4 * KD, M_STEPS):
                    take_value_gate(0, u)
            for h in range(1, RH + 1):
                n = U_RETH + 4 * h
                g = h - 1
                if h < RH:
                    his(n + 3)
                act.wait_ge(ktr, h)
                for b in range(2):
                    ins = act.activation(Ktok[:, 4 * b:4 * b + 4, :].rearrange("p a c -> p (a c)"), PS[:, 4 + b, :], ACT.Copy)
                ins.then_inc(ktok_rdy, 1)
                act.wait_ge(vtr, h)
                if h == 1:
                    act.wait_ge(dec_rdy, 2 + RH)
                for b in range(2):
                    for d in range(2):
                        ins = act.activation(vfb[:, 4 * b:4 * b + 4, d, :],
                                             PS[:, 6 + b, :].rearrange("p (a c) -> p a c", a=4), ACT.Copy,
                                             scale=kdec[:, d, g:g + 1])
                ins.then_inc(vfb_rdy, 1)
                if h < RH:
                    his(n + 4)
                    take_value_gate(h, 2)
                    take_value_gate(h, 3)
                else:
                    for t in range(9):
                        mem_step(R_B[0], t)
                act.wait_ge(y_tr, h)
                for b in range(2):
                    ins = act.activation(PS[:, 4 + b, :], PS[:, 4 + b, :], ACT.Identity,
                                         scale=gnT[:, 0, g:g + 1], bias=gnT[:, 1, g:g + 1])
                ins.then_inc(aff, 1)
            for t in range(9, M_STEPS):
                mem_step(R_B[0], t)
            his(U_OUT0 + 2)
            cat_split(0)
            his(U_OUT0 + KD + 2)
            post_in(0, 0)
            post_out(0, 0)
            his(U_OUT0 + 2 * KD + 2)
            post_in(0, 1)
            turn(3)
            post_out(0, 1)
            ffn(0)
            turn(6)
            for i in range(TT):
                act.wait_ge(h_st[i], 64)
            act.wait_ge(h_new, 16)
            his(U_NA + 3)
            take(U_NA, MQ[:, 0, :])
            his(U_NA + 4)
            take(U_NA + 1, MQ[:, 1, :])

            def take_q(n, dst):
                act.wait_ge(w_used, n + 1)
                for th in range(2):
                    for b in range(2):
                        ins = act.activation(
                            dst[GW * b:GW * b + GW, 8 * th:8 * th + 8, b, ::-1],
                            PS[GW * b:GW * b + GW, 2 * (n % 2) + th, :].rearrange("p (a c) -> p a c", a=8),
                            ACT.Copy, scale=0.125)
                ins.then_inc(ev_act, 1)

            def take_query_value(hp, i):
                n = U_NAH + 3 * hp + i
                his(n + 3)
                if i == 0:
                    take_q(n, qbd[:, hp % 2, :, :, :])
                if i == 2:
                    take(n, vTn[:, :])

            act.wait_ge(qz, 4)
            for t in range(M_STEPS):
                mem_step(R_A[1], t)
                for u in units_done(t, 3 * KD, M_STEPS):
                    take_query_value(0, u)
            for hp in range(1, HP + 1):
                act.wait_ge(vn_tr, 2 * hp - 1)
                for b in range(2):
                    ins = act.activation(Ve[:, 4 * b:4 * b + 4, :].rearrange("p a c -> p (a c)"), PS[:, 4 + b, :], ACT.Copy)
                ins.then_inc(vn_a, 1)
                r0 = R_ROW + ROWS * (hp - 1)
                for t in range(LAST):
                    if t < ROWS:
                        probs(r0 + t, False)
                    if 0 <= t - 2 < ROWS:
                        take_pt(r0 + t - 2)
                    if hp < HP:
                        for u in units_done(t, PIECES, ROWS):
                            take_query_value(hp, u)
            for t in range(M_STEPS):
                mem_step(R_B[1], t)
            his(U_OUT1 + 2)
            cat_split(1)
            his(U_OUT1 + KD + 2)
            post_in(2, 0)
            post_out(2, 0)
            his(U_OUT1 + 2 * KD + 2)
            post_in(2, 1)
            turn(7)
            post_out(2, 1)
            ffn(1)

        @block.vector
        def _(dve):
            own = [0]

            def link(ins):
                own[0] += 1
                ins.then_inc(d_own, 1)
                dve.wait_ge(d_own, own[0])

            def pre(xi, src, dst):
                dve.wait_ge(pre_rs, xi + 1)
                dve.tensor_scalar(dst, src, rstd[:, xi:xi + 1], None, ALU.mult).then_inc(xs, 1)

            def turn(t):
                width = MEM if t == 0 else HALF
                th = 1 if t in (2, 6) else 0
                for k in range(KD):
                    bank = 4 + k % 4 if t in (2, 6) else k
                    dve.wait_ge(a_hi, 8 * t + k + 1)
                    dve.scalar_tensor_tensor(out=aT[:, th, 1, k, 0:width], in0=PS[:, bank, 0:width],
                                             scalar=gT[:, GAIN[t], k:k + 1],
                                             in1=aT[:, th, 0, k, 0:width].bitcast(F32),
                                             op0=ALU.mult, op1=ALU.subtract).then_inc(a_lo, 1)

            def post_in(s, th):
                Yt = y_tiles(s, th)
                for i in range(TT):
                    e = 8 * s + 4 * th + i
                    dve.wait_ge(y_sq, e + 1)
                    if Yt is Y:
                        before = {(0, 1): 6, (1, 0): 14, (1, 1): 18, (2, 1): 22, (3, 0): 30, (3, 1): 30}[s, th]
                        dve.wait_ge(t_done, before + i + 1)
                    dve.tensor_copy(Yt[:, i, :], PS[:, 2 * i:2 * i + 2, :].rearrange("p a c -> p (a c)")).then_inc(y_cp, 1)

            def post_out(s, th):
                Yt = y_tiles(s, th)
                dve.wait_ge(g_ld, 16 * (s + 1))
                dve.wait_ge(y_cp, 8 * s + 4 * th + 4)
                for i in range(TT):
                    e = 8 * s + 4 * th + i
                    dve.wait_ge(post_rs, e + 1)
                    link(dve.scalar_tensor_tensor(out=Yt[:, i, :], in0=Yt[:, i, :], scalar=rstd[:, N_T + e:N_T + e + 1],
                                                  in1=gB[:, :], op0=ALU.mult, op1=ALU.mult))
                    dve.wait_ge(h_ld[i], 16 * (e // TT + 1))
                    dve.tensor_tensor(Hb[:, i, :], Hb[:, i, :], Yt[:, i, :], ALU.add).then_inc(h_new, 1)
                    if s < 3 and i:
                        pre(10 + e - 1, Hb[:, i - 1, :], Yt[:, i - 1, :])
                if s < 3:
                    pre(10 + e, Hb[:, TT - 1, :], Yt[:, TT - 1, :])

            def hidden(slot, up_need, gate_need, last):
                dve.wait_ge(g_act, gate_need)
                if last is not None:
                    dve.wait_ge(hid_rdy, last)
                dve.wait_ge(w_used, up_need)
                ins = dve.tensor_tensor(hidf[:, :], sg[:, slot, :], PS[:, 2 * slot + 1, :], ALU.mult)
                ins.then_inc(hid_t, 1)

            def hidden_split(dst_hi, dst_lo, need):
                dve.wait_ge(hid_t, need)
                link(dve.tensor_copy(dst_hi, hidf[:, :]))
                dve.tensor_tensor(dst_lo, hidf[:, :], dst_hi.bitcast(F32), ALU.subtract).then_inc(hid_rdy, 1)

            def ffn(l):
                for th in range(2):
                    n0 = U_FF[l] + 3 * KH * th
                    g0 = (2 * l + th) * KH

                    def tile(j):
                        hi, lo = hid[:, 0, j, :], hid[:, 1, j, :]
                        hidden(j % 3, n0 + 2 * j + 2, g0 + j + 1, g0 + j if g0 + j else None)
                        hidden_split(hi, lo, g0 + j + 1)

                    for j in range(3):
                        tile(j)
                    with dve.Fori(0, 6) as i:
                        for c in range(3):
                            j = 3 + c
                            hi = hid[:, 0, bass.ds(i * 3 + j, 1), :].rearrange("p a c -> p (a c)")
                            lo = hid[:, 1, bass.ds(i * 3 + j, 1), :].rearrange("p a c -> p (a c)")
                            hidden(c, i * 6 + (n0 + 2 * j + 2), i * 3 + (g0 + j + 1), i * 3 + (g0 + j))
                            dve.wait_ge(hid_t, i * 3 + (g0 + j + 1))
                            dve.tensor_copy(hi, hidf[:, :]).then_inc(d_own, 1)
                            dve.wait_ge(d_own, i * 3 + (own[0] + c + 1))
                            dve.tensor_tensor(lo, hidf[:, :], hi.bitcast(F32), ALU.subtract).then_inc(hid_rdy, 1)
                    own[0] += 18
                    tile(KH - 1)
                    if th == 0 or l == 0:
                        turn(4 * l + 4 + th)
                    post_in(1 + 2 * l, th)
                    post_out(1 + 2 * l, th)

            def peak(r, is_mem, row=0, hp=0):
                dve.wait_ge(s_mm, r + 1)
                if r >= 4:
                    dve.wait_ge(s_exp, r - 3)
                bank = banks(r)[0]
                if is_mem:
                    link(dve.tensor_reduce(maxraw[:, r % 4, :], PS[:, bank, :].rearrange("p (g c) -> p g c", g=2),
                                           AX.X, ALU.max))
                    dve.tensor_scalar(negmax[:, r % 4, :], maxraw[:, r % 4, :], -0.125, None, ALU.mult).then_inc(s_add, 1)
                else:
                    if row == 0:
                        dve.wait_ge(tb_rdy, hp + 1)
                    if r >= 3:
                        dve.wait_ge(s_tr, r - 2)
                    dr = key_row(row) - row + WR - 1
                    bias = TB[:, hp % 2, dr:dr + WR, :].rearrange("p a c -> p (a c)")
                    dve.tensor_tensor_reduce(SB[:, r % 3, :], PS[:, bank, :], bias, -1.0, 3.0e38,
                                             ALU.add, ALU.min, negmax[:, r % 4, 0:1]).then_inc(s_add, 1)

            def normalise(r, is_mem):
                dve.wait_ge(s_exp, r + 1)
                n = 2 if is_mem else 1
                link(dve.reciprocal(rowinv[:, r % 4, 0:n], rowsum[:, r % 4, 0:n]))
                w = 512 // n
                for g in range(n):
                    part = SB[:, r % 3, w * g:w * g + w]
                    ins = dve.tensor_scalar(part, part, rowinv[:, r % 4, g:g + 1], None, ALU.mult)
                ins.then_inc(s_nrm, 1)

            def mem_step(r0, t):
                if t < 8:
                    peak(r0 + t, True)
                if 0 <= t - 1 < 8:
                    normalise(r0 + t - 1, True)
                q = t - 4
                if 0 <= q < 8:
                    c = {R_A[0]: 0, R_B[0]: 7, R_A[1]: 8, R_B[1]: 15}[r0]
                    if q == 0 and c >= 2:
                        dve.wait_ge(oc_st[c % 2], 16 * (c // 2))
                    dve.wait_ge(pv, r0 + q + 1)
                    for g in range(2):
                        ins = dve.tensor_copy(OC[64 * g:64 * g + 64, c % 2, q * P:(q + 1) * P],
                                              PS[64 * g:64 * g + 64, banks(r0 + q)[2], P * g:P * g + P])
                    ins.then_inc(o_ev, 1)
                    if q == 7:
                        dve.wait_ge(o_ev, o_count(r0 + 8))
                        dve.engine_nop().then_inc(oc_rdy, 1)

            def cat_split(l):
                for th in range(2):
                    for k in range(KD):
                        dve.wait_ge(cat_hi, 16 * l + 8 * th + k + 1)
                        dve.tensor_tensor(catT[:, th, 1, k, :], catf[:, k, HALF * th:HALF * th + HALF],
                                          catT[:, th, 0, k, :].bitcast(F32), ALU.subtract).then_inc(cat_lo, 1)

            def rotate(n, dst):
                dve.wait_ge(w_used, n + 1)
                for th in range(2):
                    cols = slice(HALF * th, HALF * th + HALF)
                    src = PS[:, 2 * (n % 2) + th, :]
                    dve.tensor_tensor(dst[:, cols], src, ropeC[:, cols], ALU.mult)
                    dve.tensor_tensor(rtmp[0:64, :], src[64:128, :], ropeS[64:128, cols], ALU.mult)
                    link(dve.tensor_tensor(rtmp[64:128, :], src[0:64, :], ropeS[0:64, cols], ALU.mult))
                    ins = dve.tensor_tensor(dst[:, cols], dst[:, cols], rtmp[:, :], ALU.add)
                    if th == 0:
                        link(ins)
                ins.then_inc(ev_dve, 1)
                dve.wait_ge(*EV[n])

            for xi in range(4):
                pre(xi, pre_tile(xi), pre_tile(xi))
            turn(0)
            pre(4, pre_tile(4), pre_tile(4))
            pre(5, pre_tile(5), pre_tile(5))
            dve.wait_ge(zer, 1)
            for n in range(2):
                dve.wait_ge(w_used, n + 1)
                for g in range(2):
                    ins = dve.tensor_copy(bdK[64 * g:64 * g + 64, n, MEM * g:MEM * g + MEM],
                                          PS[64 * g:64 * g + 64, 2 * n, 0:MEM])
                ins.then_inc(ev_dve, 1)
            for xi in range(6, 10):
                pre(xi, pre_tile(xi), pre_tile(xi))
            dve.wait_ge(mvt, 1)
            dve.tensor_copy(memV[:, :, :].rearrange("p k (h f) -> p h k f", h=2),
                            PS[:, 4, :].rearrange("p (h k f) -> p h k f", h=2, k=2)).then_inc(memv_rdy, 1)
            turn(1)
            turn(2)
            dve.wait_ge(dec_e, 1)
            link(dve.tensor_scalar(lg[:, :, :].rearrange("p a c -> p (a c)"), lgb[:, :], -1.0, None, ALU.mult))
            dve.wait_ge(zer, 2)
            dve.wait_ge(rpb_st, 48)
            for d in range(2):
                ins = dve.tensor_scalar(kprod[:, d, :], lg[:, d, :], colc[:, d:d + 1], None, ALU.mult)
            ins.then_inc(dec_rdy, 1)
            dve.wait_ge(dec_e, 2)
            link(dve.tensor_scalar(kdec[:, :, :], kdec[:, :, :], float(P) ** -0.5, None, ALU.mult))
            for h in range(RH):
                dve.wait_ge(dec_e, 4 + h)
                dve.tensor_tensor(dexp[:, 0, :], dexp[:, 0, :], dconst[:, 2, :], ALU.mult)
                link(dve.tensor_tensor(dexp[:, 1, :], dexp[:, 1, :], dconst[:, 3, :], ALU.mult))
                dve.tensor_tensor(DM[:, h, :], dexp[:, 0, :], dexp[:, 1, :], ALU.add).then_inc(dec_rdy, 1)
            dve.wait_ge(dec_rdy, 1 + RH)
            dve.memset(states[:, 0, 0, :], 0.0)
            dve.memset(states[:, 7, 1, :], 0.0).then_inc(dec_rdy, 1)
            dve.wait_ge(dec_rdy, 2 + RH)

            def values(h):
                dve.wait_ge(vfb_rdy, h)
                for b in range(2):
                    ins = dve.tensor_copy(V[:, 4 * b:4 * b + 4, :].rearrange("p a c -> p (a c)"), PS[:, 6 + b, :])
                ins.then_inc(v_rdy, 1)
                dve.wait_ge(st_mm, h)
                for b in range(2):
                    ins = dve.tensor_tensor(ST[:, 4 * b:4 * b + 4, :], PS[:, 4 + b, :].rearrange("p (a c) -> p a c", a=4),
                                            DM[:, h - 1:h, :].to_broadcast([P, 4, P]), ALU.mult)
                ins.then_inc(st_rdy, 1)

            def scan(h):
                g = h - 1
                dve.wait_ge(kv_mm, h)

                def kv(c, d):
                    bank = (6, 7, 4, 5)[c // 2]
                    return PS[:, bank, 256 * (c % 2) + P * d:256 * (c % 2) + P * d + P]

                for c in range(7):
                    dve.scalar_tensor_tensor(out=states[:, c + 1, 0, :], in0=states[:, c, 0, :],
                                             scalar=cdec[:, 0, g:g + 1], in1=kv(c, 0), op0=ALU.mult, op1=ALU.add)
                    b = 7 - c
                    ins = dve.scalar_tensor_tensor(out=states[:, b - 1, 1, :], in0=states[:, b, 1, :],
                                                   scalar=cdec[:, 1, g:g + 1], in1=kv(b, 1),
                                                   op0=ALU.mult, op1=ALU.add)
                    if c < 6:
                        link(ins)
                ins.then_inc(scan_rdy, 1)
                for d in range(2):
                    ins = dve.tensor_tensor(qfb[:, d, :].rearrange("p (a c) -> p a c", a=8),
                                            qT[:, g % 2, :].rearrange("p (a c) -> p a c", a=8),
                                            QD[:, d, g:g + 1, :].to_broadcast([P, 8, P]), ALU.mult)
                ins.then_inc(qfb_rdy, 1)

            def group_norm(h):
                dve.wait_ge(out_mm, h)
                for c in range(8):
                    ins = dve.bn_stats(stats[:, c, :], PS[:, 6 + c // 4, (c % 4) * P:(c % 4 + 1) * P])
                link(ins)
                for c in range(8):
                    ins = dve.bn_aggr(mv[:, c, :], stats[:, c, :])
                ins.then_inc(var_rdy, 1)
                dve.wait_ge(grs_rdy, h)
                for c in range(8):
                    ins = dve.tensor_scalar(ST[:, c, :], PS[:, 6 + c // 4, (c % 4) * P:(c % 4 + 1) * P],
                                            mv[:, c, 0:1], grstd[:, c:c + 1], ALU.subtract, ALU.mult)
                ins.then_inc(yn_rdy, 1)

            def gated(h):
                g = h - 1
                dve.wait_ge(aff, h)
                dve.wait_ge(ev_act, EV[U_RETH + 4 * g + 3][1])
                for b in range(2):
                    cols = slice(HALF * b, HALF * b + HALF)
                    ins = dve.tensor_tensor(OC[:, h % 2, cols], OC[:, h % 2, cols], PS[:, 4 + b, :], ALU.mult)
                ins.then_inc(oc_rdy, 1)

            for t in range(M_STEPS + 1):
                mem_step(R_A[0], t)
                for u in units_done(t, 4 * KD, M_STEPS):
                    if u < 2:
                        rotate(U_RETH + u, (qT[:, 0, :], kT[:, :])[u])
            for h in range(1, RH + 1):
                n = U_RETH + 4 * h
                if h < RH:
                    rotate(n, qT[:, h % 2, :])
                    values(h)
                    rotate(n + 1, kT[:, :])
                    scan(h)
                    group_norm(h)
                    gated(h)
                    continue
                values(h)
                for t in range(3):
                    mem_step(R_B[0], t)
                scan(h)
                for t in range(3, 6):
                    mem_step(R_B[0], t)
                group_norm(h)
                for t in range(6, 9):
                    mem_step(R_B[0], t)
                gated(h)
                for t in range(9, M_STEPS + 1):
                    mem_step(R_B[0], t)
            cat_split(0)
            post_in(0, 0)
            post_out(0, 0)
            post_in(0, 1)
            turn(3)
            post_out(0, 1)
            ffn(0)
            turn(6)
            for i in range(TT):
                dve.wait_ge(h_st[i], 64)

            def take_k(n):
                dve.wait_ge(w_used, n + 1)
                for th in range(2):
                    ins = dve.tensor_copy(kTn[:, ((n - U_NAH) // 3) % 2, HALF * th:HALF * th + HALF],
                                          PS[:, 2 * (n % 2) + th, :])
                ins.then_inc(ev_dve, 1)

            for t in range(M_STEPS + 1):
                mem_step(R_A[1], t)
                for u in units_done(t, 3 * KD, M_STEPS):
                    if u == 1:
                        take_k(U_NAH + 1)
            for hp in range(1, HP + 1):
                dve.wait_ge(vn_tr, 2 * hp)
                dve.tensor_copy(Vo[:, 0:4, :].rearrange("p a c -> p (a c)"), PS[:, 6, :])
                dve.tensor_copy(Vo[:, 4:7, :].rearrange("p a c -> p (a c)"), PS[:, 7, 0:3 * P]).then_inc(vn_d, 1)
                g = hp - 1
                r0 = R_ROW + ROWS * g
                for t in range(LAST):
                    if t < ROWS:
                        peak(r0 + t, False, t, g)
                    if 0 <= t - 1 < ROWS:
                        normalise(r0 + t - 1, False)
                    if hp < HP and 1 in units_done(t, PIECES, ROWS):
                        take_k(U_NAH + 3 * hp + 1)
                    q = t - 4
                    if 0 <= q < ROWS and q % 4 == 3:
                        c = 8 + hp
                        if q == 3:
                            dve.wait_ge(oc_st[c % 2], 16 * (c // 2))
                        dve.wait_ge(pv, r0 + q + 1)
                        for b in range(2):
                            ins = dve.tensor_copy(
                                OC[64 * b:64 * b + 64, c % 2, (q - 3) * GW:(q + 1) * GW].rearrange("p (a c) -> p a c", a=4),
                                PS[64 * b:64 * b + 64, 7, :].rearrange("p (a b c) -> p a b c", a=4, b=2)[:, :, b, ::-1])
                        ins.then_inc(o_ev, 1)
                        if q == ROWS - 1:
                            dve.wait_ge(o_ev, o_count(r0 + ROWS))
                            dve.engine_nop().then_inc(oc_rdy, 1)
            for t in range(M_STEPS + 1):
                mem_step(R_B[1], t)
            cat_split(1)
            post_in(2, 0)
            post_out(2, 0)
            post_in(2, 1)
            turn(7)
            post_out(2, 1)
            ffn(1)

        @block.tensor
        def _(pe):
            def three(dst, stat, mov, start, stop):
                pe.matmul(dst, stat[0], mov[0], start=start, stop=False)
                pe.matmul(dst, stat[0], mov[1], start=False, stop=False)
                return pe.matmul(dst, stat[1], mov[0], start=False, stop=stop)

            def wtile(n, k):
                c = slice(k * P, (k + 1) * P)
                return whi[:, n % RING, c], wlo[:, n % RING, c]

            def turn(t, free):
                for s, v in free:
                    pe.wait_ge(s, v)
                if t:
                    pe.wait_ge(a_hi, 8 * t)
                    pe.wait_ge(a_lo, 8 * t)
                Yt = set_tiles(t)
                for i in range(tiles_before(t + 1) - tiles_before(t)):
                    pe.wait_ge(xs, tiles_before(t) + i + 1)
                    for k in range(KD):
                        ins = pe.transpose(PS[:, k, i * P:(i + 1) * P], Yt[:, i, k * P:(k + 1) * P], ident[:, :])
                    ins.then_inc(t_done, 1)

            def turn_late(t):
                if t == 6:
                    pe.wait_ge(y_cp, 16)
                    pe.wait_ge(y_sq, 16)
                for part in range(2):
                    if part:
                        pe.wait_ge(a_lo, 8 * t + 4)
                    for i in range(TT):
                        if not part:
                            pe.wait_ge(xs, tiles_before(t) + i + 1)
                        for k in range(4):
                            f = (4 * part + k) * P
                            ins = pe.transpose(PS[:, 4 + k, i * P:(i + 1) * P], Y[:, i, f:f + P], ident[:, :])
                        if part:
                            ins.then_inc(t_done, 1)
                    if not part:
                        ins.then_inc(t_low, 1)

            def project(n, k, halves=(0, 1), sets=None):
                if k == 0 and 0 in halves:
                    pe.wait_ge(w_lo, n + 1)
                    if n - 2 in EV:
                        pe.wait_ge(*EV[n - 2])
                if sets is not None:
                    pe.wait_ge(a_lo, 8 * sets + max(k + 1, 2))
                for th in halves:
                    ins = three(PS[:, 2 * (n % 2) + th, :], wtile(n, k), (aT[:, th, 0, k, :], aT[:, th, 1, k, :]),
                                k == 0, k == KD - 1)
                if k == KD - 1 and 1 in halves:
                    ins.then_inc(w_used, 1)

            def first_two(n, t):
                if t == 6:
                    pe.wait_ge(y_cp, 14)
                    pe.wait_ge(y_sq, 14)
                for u in range(2):
                    for k in range(KD):
                        project(n + u, k, (0,), t - 1 if u == 0 else None)
                turn_late(t)
                for u in range(2):
                    for k in range(KD):
                        project(n + u, k, (1,), t if u == 0 else None)

            def gate_up(n, bank, need_w, last_set=None):
                pe.wait_ge(w_lo, need_w)
                for k in range(KD):
                    if last_set is not None:
                        pe.wait_ge(a_lo, 8 * last_set + max(k + 1, 2))
                    ins = three(PS[:, bank, :], wtile(n, k), (aT[:, 0, 0, k, :], aT[:, 0, 1, k, :]), k == 0, k == KD - 1)
                ins.then_inc(w_used, 1)

            def contract(n0, kn, source, ready, free):
                for k in range(kn):
                    n = n0 + k
                    pe.wait_ge(w_lo, n + 1)
                    pe.wait_ge(*ready(k))
                    for i in range(TT):
                        if k == 0:
                            for s, v in free(i):
                                pe.wait_ge(s, v)
                        c = slice(i * P, (i + 1) * P)
                        for fh in range(2):
                            f = slice(512 * fh, 512 * fh + 512)
                            ins = three(PS[:, 2 * i + fh, :], (source[:, 0, k, c], source[:, 1, k, c]),
                                        (whi[:, n % RING, f], wlo[:, n % RING, f]), k == 0, k == kn - 1)
                        if k == kn - 1:
                            ins.then_inc(y_done, 1)
                    if k < kn - 1:
                        ins.then_inc(w_used, 1)
                pe.wait_ge(y_done, Y_DONE[0] + TT)
                pe.sem_inc(w_used, 1)
                Y_DONE[0] += TT

            Y_DONE = [0]

            def ffn(l):
                for th in range(2):
                    n0 = U_FF[l] + 3 * KH * th
                    g0 = (2 * l + th) * KH
                    s = 1 + 2 * l
                    t = 4 * l + 3 + th

                    def tile(j):
                        n = n0 + 2 * j
                        if j >= 3:
                            pe.wait_ge(hid_t, g0 + j - 2)
                        elif th:
                            pe.wait_ge(y_cp, 8 * s + j + 1)
                            pe.wait_ge(y_sq, 8 * s + j + 1)
                        gate_up(n, 2 * (j % 3), n + 1, t if j == 0 else None)
                        gate_up(n + 1, 2 * (j % 3) + 1, n + 2)

                    for j in range(3):
                        tile(j)
                    with pe.Fori(0, 6) as i:
                        for c in range(3):
                            j = 3 + c
                            n = n0 + 2 * j
                            pe.wait_ge(hid_t, i * 3 + (g0 + j - 2))
                            gate_up(n, 2 * c, i * 6 + (n + 1))
                            gate_up(n + 1, 2 * c + 1, i * 6 + (n + 2))
                    tile(KH - 1)
                    if th == 0 or l == 0:
                        turn(t + 1, [(hid_t, g0 + KH)] + ([(y_cp, 8 * s + TT), (y_sq, 8 * s + TT)] if th else []))

                    def free(i):
                        if th == 0 or l == 0:
                            return [(a_lo, 8 * (t + 1) + 2 * i + 2)]
                        return [(hid_t, g0 + KH), (y_cp, 8 * s + TT), (y_sq, 8 * s + TT)]

                    contract(n0 + 2 * KH, KH, hid, lambda k: (hid_rdy, g0 + k + 1), free)

            def out_project(l):
                for th in range(2):
                    e0 = 16 * l + 4 * th

                    def free(i):
                        if th:
                            return [(y_cp, e0 - TT + i + 1), (y_sq, e0 - TT + i + 1)]
                        return [(oc_rdy, 8 * l + 8), (pt_ev, R_B[l] + 8), (s_exp, R_B[l] + 8)]

                    contract(U_OUT[l] + KD * th, KD, catT[:, th, :, :, :],
                             lambda k: (cat_lo, 16 * l + 8 * th + k + 1), free)

            def scores(r, stat, mov):
                if r >= 2:
                    pe.wait_ge(s_add, r - 1)
                    pe.wait_ge(s_exp, r - 1)
                pe.matmul(PS[:, banks(r)[0], :], stat, mov, start=True, stop=True).then_inc(s_mm, 1)

            def turn_probs(r):
                pe.wait_ge(s_nrm, r + 1)
                if r:
                    pe.wait_ge(pt_ev, r)
                for c in range(4):
                    ins = pe.transpose(PS[:, banks(r)[1], c * P:(c + 1) * P], SB[:, r % 3, c * P:(c + 1) * P], ident[:, :])
                ins.then_inc(s_tr, 1)

            def mem_step(r0, t, fill=()):
                hp = 0 if r0 in R_A else 1
                fill = list(fill)
                if t < 8:
                    scores(r0 + t, MQ[:, hp, t * P:(t + 1) * P], bdK[:, hp, :])
                for n, k in fill[:2]:
                    project(n, k)
                if 0 <= t - 2 < 8:
                    turn_probs(r0 + t - 2)
                for n, k in fill[2:]:
                    project(n, k)
                if 0 <= t - 3 < 8:
                    r = r0 + t - 3
                    pe.wait_ge(pt_ev, r + 1)
                    if r:
                        pe.wait_ge(o_ev, o_count(r))
                    for kc in range(2):
                        ins = pe.matmul(
                            PS[:, banks(r)[2], 0:256].rearrange("p (g c) -> p g c", g=2),
                            memV[:, kc, P * hp:P * hp + P],
                            PT[:, r % 2, :].rearrange("p (g k c) -> p g k c", g=2, k=2)[:, :, kc, :],
                            start=(kc == 0), stop=(kc == 1))
                    ins.then_inc(pv, 1)

            pe.wait_ge(c_ids, 32)
            turn(0, [])
            for n in range(4):
                pe.wait_ge(w_lo, n + 1)
                if n >= 2:
                    pe.wait_ge(*EV[n - 2])
                for k in range(KD):
                    if n == 0:
                        pe.wait_ge(a_lo, 8)
                    ins = three(PS[:, 2 * (n % 2), 0:MEM], wtile(n, k), (aT[:, 0, 0, k, 0:MEM], aT[:, 0, 1, k, 0:MEM]),
                                k == 0, k == KD - 1)
                ins.then_inc(w_used, 1)
            pe.wait_ge(*EV[3])
            for hp in range(2):
                for kc in range(2):
                    c = (2 * hp + kc) * P
                    ins = pe.transpose(PS[:, 4, c:c + P], mvT[:, hp, kc * P:(kc + 1) * P], ident[:, :])
            ins.then_inc(mvt, 1)
            turn(1, [EV[1], (memv_rdy, 1)])
            first_two(U_RET, 2)
            pe.wait_ge(*EV[U_RET + 1])
            pe.wait_ge(a_lo, 24)
            for t in range(M_STEPS):
                mem_step(R_A[0], t, [(U_RETH + p // KD, p % KD) for p in pieces_at(t, 4 * KD, M_STEPS)])

            def unit(n):
                for k in range(KD):
                    project(n, k)

            def chunk_scores(h):
                n = U_RETH + 4 * h
                pe.wait_ge(*EV[n - 3])
                if h >= 2:
                    pe.wait_ge(oc_rdy, h)
                else:
                    pe.wait_ge(s_exp, 8)
                    pe.wait_ge(pt_ev, 8)
                    pe.wait_ge(o_ev, 8)
                for c in range(8):
                    ins = pe.transpose(PS[:, 4 + c // 4, (c % 4) * P:(c % 4 + 1) * P], kT[:, c * P:(c + 1) * P], ident[:, :])
                ins.then_inc(ktr, 1)
                pe.wait_ge(*EV[n - 2])
                if h >= 2:
                    pe.wait_ge(yn_rdy, h - 1)
                for c in range(8):
                    ins = pe.transpose(PS[:, 6 + c // 4, (c % 4) * P:(c % 4 + 1) * P], vT[:, c * P:(c + 1) * P], ident[:, :])
                ins.then_inc(vtr, 1)
                pe.wait_ge(ktok_rdy, h)
                for c in range(8):
                    cc = slice(c * P, (c + 1) * P)
                    ins = pe.matmul(PS[:, 4 + c // 4, (c % 4) * P:(c % 4 + 1) * P], kT[:, cc], qT[:, (h - 1) % 2, cc],
                                    start=True, stop=True)
                ins.then_inc(st_mm, 1)

            def chunk_states(h):
                pe.wait_ge(vfb_rdy, h)
                pe.wait_ge(v_rdy, h)
                for c in range(8):
                    if c == 4:
                        pe.wait_ge(st_rdy, h)
                    bank = (6, 7, 4, 5)[c // 2]
                    ins = pe.matmul(PS[:, bank, 256 * (c % 2):256 * (c % 2) + 256], Ktok[:, c, :],
                                    vfb[:, c, :, :].rearrange("p a c -> p (a c)"), start=True, stop=True)
                ins.then_inc(kv_mm, 1)

            def chunk_outputs(h):
                pe.wait_ge(scan_rdy, h)
                pe.wait_ge(qfb_rdy, h)
                for c in range(8):
                    dst = PS[:, 6 + c // 4, (c % 4) * P:(c % 4 + 1) * P]
                    cc = slice(c * P, (c + 1) * P)
                    pe.matmul(dst, ST[:, c, :], V[:, c, :], start=True, stop=False)
                    pe.matmul(dst, qfb[:, 0, cc], states[:, c, 0, :], start=False, stop=False)
                    ins = pe.matmul(dst, qfb[:, 1, cc], states[:, c, 1, :], start=False, stop=True)
                ins.then_inc(out_mm, 1)

            def turn_outputs(h):
                pe.wait_ge(yn_rdy, h)
                for c in range(8):
                    ins = pe.transpose(PS[:, 4 + c // 4, (c % 4) * P:(c % 4 + 1) * P], ST[:, c, :], ident[:, :])
                ins.then_inc(y_tr, 1)

            for h in range(1, RH):
                n = U_RETH + 4 * h
                unit(n)
                chunk_scores(h)
                unit(n + 1)
                chunk_states(h)
                unit(n + 2)
                chunk_outputs(h)
                unit(n + 3)
                turn_outputs(h)
            chunk_scores(RH)
            for u in range(1, 4):
                pe.wait_ge(*EV[U_OUT0 - u])
            for t in range(3):
                mem_step(R_B[0], t)
            chunk_states(RH)
            for t in range(3, 6):
                mem_step(R_B[0], t)
            chunk_outputs(RH)
            for t in range(6, 9):
                mem_step(R_B[0], t)
            turn_outputs(RH)
            for t in range(9, M_STEPS):
                mem_step(R_B[0], t)
            out_project(0)
            turn(3, [(y_cp, 8), (y_sq, 8)])
            ffn(0)
            first_two(U_NA, 6)
            pe.wait_ge(*EV[U_NA + 1])
            pe.wait_ge(a_lo, 56)
            pe.wait_ge(mkv_ld, 32)
            for t in range(M_STEPS):
                mem_step(R_A[1], t, [(U_NAH + p // KD, p % KD) for p in pieces_at(t, PIECES, M_STEPS)])
            for hp in range(1, HP + 1):
                n = U_NAH + 3 * hp
                g = hp - 1
                r0 = R_ROW + ROWS * g
                pe.wait_ge(*EV[n - 1])
                pe.wait_ge(s_exp, r0)
                pe.wait_ge(s_add, r0)
                for m in range(8):
                    ins = pe.transpose(PS[:, 4 + m // 4, (m % 4) * P:(m % 4 + 1) * P], vTn[:, m * P:(m + 1) * P], ident[:, :])
                ins.then_inc(vn_tr, 1)
                pe.wait_ge(pt_ev, r0)
                pe.wait_ge(o_ev, o_count(r0))
                for m in range(7):
                    ins = pe.transpose(PS[:, 6 + m // 4, (m % 4) * P:(m % 4 + 1) * P], vTn[:, m * P + GW:(m + 1) * P + GW], ident[:, :])
                ins.then_inc(vn_tr, 1)
                pe.wait_ge(vn_a, hp)
                pe.wait_ge(*EV[n - 3])
                pe.wait_ge(*EV[n - 2])
                for t in range(LAST):
                    if t < ROWS:
                        kr = key_row(t)
                        scores(r0 + t, qbd[:, g % 2, t, :, :].rearrange("p a c -> p (a c)"),
                               kTn[:, g % 2, kr * GW:kr * GW + 512])
                    for piece in pieces_at(t):
                        if hp < HP:
                            project(n + piece // KD, piece % KD)
                    if 0 <= t - 2 < ROWS:
                        if t == 2:
                            pe.wait_ge(vn_d, hp)
                        turn_probs(r0 + t - 2)
                    q = t - 3
                    if 0 <= q < ROWS:
                        r = r0 + q
                        pe.wait_ge(pt_ev, r + 1)
                        if q % 4 == 0:
                            pe.wait_ge(o_ev, o_count(r))
                        kr = key_row(q)
                        for c in range(4):
                            vt = Vo[:, (kr - 1) // 2 + c, :] if kr % 2 else Ve[:, kr // 2 + c, :]
                            ins = pe.matmul(PS[:, 7, (q % 4) * P:(q % 4 + 1) * P], vt, PT[:, r % 2, c * P:(c + 1) * P],
                                            start=(c == 0), stop=(c == 3))
                        ins.then_inc(pv, 1)
            pe.wait_ge(o_ev, o_count(R_B[1]))
            for t in range(M_STEPS):
                mem_step(R_B[1], t)
            out_project(1)
            turn(7, [(y_cp, 24), (y_sq, 24)])
            ffn(1)


def constants():
    half = P // 2
    inv = (np.float32(10000.0) ** (-np.arange(half, dtype=np.float32) / np.float32(half))).astype(np.float32)
    ang = (np.arange(SEQ, dtype=np.float32)[None, :] * inv[:, None]).astype(np.float32)
    c, s = np.cos(ang), np.sin(ang)
    ropes = np.stack([np.concatenate([c, c]), np.concatenate([s, -s])]).astype(np.float32)
    i = np.arange(P, dtype=np.float32)
    rel = i[None, :] - i[:, None]
    scale = np.float32(float(P) ** -0.5)
    rows = [np.maximum(rel, 0), np.maximum(-rel, 0), (rel >= 0) * scale, (rel <= 0) * scale,
            np.broadcast_to(i[None, :] + 1, (P, P)), np.broadcast_to(P - i[None, :], (P, P)),
            np.stack([P - 1 - i, i] + [0 * i] * 6, axis=1)]
    decay_consts = np.concatenate(rows, axis=1).astype(np.float32)
    q = np.arange(GW)[::-1, None]
    k = np.arange(GW)[None, :]
    start = np.clip(q - WC // 2, 0, GW - WC)
    inside = (k >= start) & (k < start + WC)
    m = np.stack([inside.astype(np.float32), np.where(inside, 0, -1e30).astype(np.float32)], axis=1)
    return ropes, decay_consts, np.concatenate([m, m]), np.eye(P, dtype=np.float32)


def kernel(x, mem, norm_g, mem_norm_g, mem_w_kv, ret_w_in, ret_w_out, ret_gn_g, ret_gn_b, ret_decay,
           na_w_in, na_w_out, na_rpb, ffn_w_in, ffn_w_out):
    import concourse.bacc as bacc
    from concourse.bass_utils import run_bass_kernel_spmd

    a = {k: np.asarray(v) for k, v in locals().items() if k not in ("bacc", "run_bass_kernel_spmd")}

    def tiles(w, *groups):
        g = len(groups)
        w = w.reshape((KD, P) + groups + (P,))
        return w.transpose(tuple(range(2 + g - 1, 1, -1)) + (1, 0, 2 + g)).reshape(-1, P, UW)

    def rows(w):
        w = w.reshape(KD, P, D)
        return np.concatenate([w[6:7], w[0:6], w[7:8]])

    tok = RH * P
    ret, na = a["ret_w_in"][0], a["na_w_in"][0]
    wpack = np.concatenate([
        tiles(a["mem_w_kv"], 4),
        tiles(ret[:, 4 * tok:], 2), tiles(ret[:, :4 * tok], 4, RH), rows(a["ret_w_out"][0]),
        tiles(a["ffn_w_in"][0], 2, KH), a["ffn_w_out"][0].reshape(KH, P, D),
        tiles(na[:, 3 * tok:], 2), tiles(na[:, :3 * tok], 3, HP), rows(a["na_w_out"][0]),
        tiles(a["ffn_w_in"][1], 2, KH), a["ffn_w_out"][1].reshape(KH, P, D)])
    g = a["norm_g"]
    pre = np.stack([g[0, 0], g[0, 2], g[1, 0], g[1, 2], a["mem_norm_g"]])
    ropes, decay_consts, na_masks, ident = constants()
    arrays = {
        "wpack": wpack, "x": a["x"][0], "mem": a["mem"][0],
        "gains": pre.reshape(5, KD, P).transpose(2, 0, 1),
        "gain_rows": np.stack([g[0, 1], g[0, 3], g[1, 1], g[1, 3]]),
        "gn": np.stack([a["ret_gn_g"][0], a["ret_gn_b"][0]]).reshape(2, RH, P).transpose(2, 0, 1),
        "decay": a["ret_decay"].reshape(1, 2 * RH), "rpb": a["na_rpb"].reshape(-1),
        "ropes": ropes, "decay_consts": decay_consts, "na_masks": na_masks, "ident_c": ident}
    nc = bacc.Bacc("TRN2", target_bir_lowering=False, num_devices=1)
    arrays = {f"in_{k}": np.ascontiguousarray(v) for k, v in arrays.items()}
    args = [nc.dram_tensor(k, v.shape, mybir.dt.from_np(v.dtype), kind="ExternalInput").ap() for k, v in arrays.items()]
    out = nc.dram_tensor("out_h", (SEQ, D), mybir.dt.float32, kind="ExternalOutput").ap()
    trunk_program(nc, *args, out)
    r = run_bass_kernel_spmd(nc, [arrays], core_ids=[0])
    return r.results[0]["out_h"].reshape(1, SEQ, D)
```

```python
import numpy as np
from contextlib import ExitStack
import concourse.bass as bass
from concourse import mybir

P = 128
D = 1024
KD = D // P
SEQ = 1024
HALF = SEQ // 2
TT = HALF // P
MEM = 256
RH = 6
HP = 6
ROWS, GW = 16, 64
WR, WC = 8, 16
HID = 2816
KH = HID // P
RING = 3
UW = 1024
NA_BIAS = 15 * GW
RPB_PAD = 64

U_MEM = 0
U_RET = U_MEM + 4
U_RETH = U_RET + 2
U_OUT0 = U_RETH + 4 * RH
U_FF0 = U_OUT0 + 2 * KD
U_NA = U_FF0 + 2 * (3 * KH)
U_NAH = U_NA + 2
U_OUT1 = U_NAH + 3 * HP
U_FF1 = U_OUT1 + 2 * KD
U_END = U_FF1 + 2 * (3 * KH)
N_T = 34
N_E = 32


def unit_rows():
    rows, at = [], 0
    for count, times, phase in ((4, 1, "mem"), (4 * RH + 2, 1, "ret"), (KD, 2, "out"), (3 * KH, 2, "ffn"),
                                (3 * HP + 2, 1, "na"), (KD, 2, "out"), (3 * KH, 2, "ffn")):
        for _ in range(times):
            rows += list(range(at, at + count))
        at += count
    return rows


def trunk_program(nc, wpack, x, mem, gains, gain_rows, gn, decay, rpb, ropes, decay_consts, na_masks, ident_c, out):
    F32, F32R, BF16 = mybir.dt.float32, mybir.dt.float32r, mybir.dt.bfloat16
    ACT = mybir.ActivationFunctionType
    ALU = mybir.AluOpType
    AX = mybir.AxisListType
    ROW = unit_rows()
    assert len(ROW) == U_END

    h_dram = nc.dram_tensor("h_scratch", [SEQ, D], F32).ap()
    cat_dram = nc.dram_tensor("cat_scratch", [2, KD, P, SEQ], F32).ap()
    memkv_dram = nc.dram_tensor("memkv_scratch", [P, 1536], F32).ap()
    rpb_n = 12 * 15 * 31
    rpb_dram = nc.dram_tensor("rpb_scratch", [RPB_PAD + rpb_n + RPB_PAD], F32)


    KB = 1024
    base = (nc.sbuf_base + 31) // 32 * 32

    def at(name, shape, dt, off):
        return nc.alloc_sbuf_tensor_at(name, shape, dt, offset=base + off)

    stage = at("stage", [P, RING, UW], F32, 0)
    whi = at("whi", [P, RING, UW], F32R, 12 * KB)
    wlo = at("wlo", [P, RING, UW], F32R, 24 * KB)
    SM = 36 * KB
    ident = at("ident", [P, P], F32, SM)
    sumsq = at("sumsq", [P, 72], F32, SM + 512)
    msq = at("msq", [P, 72], F32, SM + 800)
    rstd = at("rstd", [P, 72], F32, SM + 1088)
    gT = at("gT", [P, 5, KD], F32, SM + 1376)
    gnT = at("gnT", [P, 2, RH], F32, SM + 1536)
    lgb = at("lgb", [P, 12], F32, SM + 1600)
    lg = at("lg", [P, 2, RH], F32, SM + 1664)
    kdec = at("kdec", [P, 2, RH], F32, SM + 1728)
    cdec = at("cdec", [P, 2, RH], F32, SM + 1792)
    negmax = at("negmax", [P, 4, 2], F32, SM + 1920)
    rowsum = at("rowsum", [P, 4, 2], F32, SM + 1952)
    rowinv = at("rowinv", [P, 4, 2], F32, SM + 1984)
    stats = at("stats", [P, 8, 6], F32, SM + 2048)
    mv = at("mv", [P, 8, 2], F32, SM + 2240)
    gvar = at("gvar", [P, 8], F32, SM + 2304)
    grstd = at("grstd", [P, 8], F32, SM + 2336)
    minus_half = at("minus_half", [P, 8], F32, SM + 2368)
    maxraw = at("maxraw", [P, 4, 2], F32, SM + 2400)
    colc = at("colc", [P, 8], F32, SM + 2528)
    kprod = at("kprod", [P, 2, RH], F32, SM + 2432)
    Z = SM + 3 * KB
    Y = at("Y", [P, TT, D], F32, Z)
    vfb = at("vfb", [P, 8, 2, P], F32, Z)
    qfb = at("qfb", [P, 2, SEQ], F32, Z)
    kTn = at("kTn", [P, 2, SEQ], F32, Z)
    OC = at("OC", [P, 2, SEQ], F32, Z + 8 * KB)
    Hb = at("Hb", [P, TT, D], F32, Z + 16 * KB)
    gB = at("gB", [P, D], F32, Z + 32 * KB)
    junk = [at("junk0", [P, D], BF16, Z + 36 * KB), at("junk1", [P, D], BF16, Z + 166 * KB)]
    X = Z + 38 * KB
    aT = at("aT", [P, 2, 2, KD, HALF], F32R, X)
    catf = at("catf", [P, KD, SEQ], F32, X)
    catT = at("catT", [P, 2, 2, KD, HALF], F32R, X + 32 * KB)
    hid = at("hid", [P, 2, KH, HALF], F32R, X + 32 * KB)
    sg = at("sg", [P, RING, HALF], F32, X + 120 * KB)
    hidf = at("hidf", [P, HALF], F32, X + 126 * KB)
    Yb = at("Yb", [P, TT, D], F32, X + 96 * KB)
    W = X + 64 * KB
    W += 6 * KB
    bdK = at("bdK", [P, 2, 2 * MEM], F32, W + 53 * KB)
    memV = at("memV", [P, 2, 2 * P], F32, W + 57 * KB)
    MQ = at("MQ", [P, 2, SEQ], F32, Z + 16 * KB)
    SB = at("SB", [P, 3, 512], F32, Z + 24 * KB)
    PT = at("PT", [P, 2, 512], F32, Z + 32 * KB)
    ropeC = at("ropeC", [P, SEQ], F32, W)
    ropeS = at("ropeS", [P, SEQ], F32, W + 4 * KB)
    QD = at("QD", [P, 2, RH, P], F32, W + 8 * KB)
    DM = at("DM", [P, RH, P], F32, W + 14 * KB)
    qT = at("qT", [P, 2, SEQ], F32, W + 17 * KB)
    kT = at("kT", [P, SEQ], F32, W + 25 * KB)
    Ktok = at("Ktok", [P, 8, P], F32, W + 29 * KB)
    V = at("V", [P, 8, P], F32, W + 33 * KB)
    ST = at("ST", [P, 8, P], F32, W + 37 * KB)
    vT = at("vT", [P, SEQ], F32, W + 41 * KB)
    states = at("states", [P, 8, 2, P], F32, W + 45 * KB)
    rtmp = at("rtmp", [P, HALF], F32, Z + 36 * KB)
    dconst = at("dconst", [P, 6, P], F32, Z)
    dexp = at("dexp", [P, 2, P], F32, Z + 3 * KB)
    mvT = at("mvT", [P, 2, MEM], F32, W + 17 * KB)
    qbd = at("qbd", [P, 2, ROWS, 2, GW], F32, W)
    TB = at("TB", [P, 2, 15, GW], F32, W + 16 * KB)
    nmask = at("nmask", [P, 2, GW], F32, W + 24 * KB)
    vTn = at("vTn", [P, SEQ], F32, W + 25 * KB)
    Ve = at("Ve", [P, 8, P], F32, W + 29 * KB)
    Vo = at("Vo", [P, 7, P], F32, W + 33 * KB)

    with ExitStack() as ctx:
        PS = ctx.enter_context(nc.psum_tensor("PS", [P, 8, 512], F32))

        def sem(name):
            return ctx.enter_context(nc.semaphore(name))

        w_in = [sem(f"w_in{r}") for r in range(RING)]
        w_hi, w_lo, w_used = sem("w_hi"), sem("w_lo"), sem("w_used")
        c_ld = sem("c_ld")
        c_ids = sem("c_ids")
        x_ld = [sem(f"x_ld{i}") for i in range(10)]
        h_ld = [sem(f"h_ld{i}") for i in range(TT)]
        h_st = [sem(f"h_st{i}") for i in range(TT)]
        g_ld, pre_sq, pre_rs, xs = sem("g_ld"), sem("pre_sq"), sem("pre_rs"), sem("xs")
        t_done, t_low, a_hi, a_lo = sem("t_done"), sem("t_low"), sem("a_hi"), sem("a_lo")
        y_done, y_cp, y_sq, post_rs, h_new = sem("y_done"), sem("y_cp"), sem("y_sq"), sem("post_rs"), sem("h_new")
        g_act, hid_t, hid_rdy = sem("g_act"), sem("hid_t"), sem("hid_rdy")
        ev_act, ev_dve = sem("ev_act"), sem("ev_dve")
        oc_st = [sem(f"oc_st{i}") for i in range(2)]
        cat_ld = [sem(f"cat_ld{k}") for k in range(KD)]
        cat_hi, cat_lo = sem("cat_hi"), sem("cat_lo")
        dec_e, dec_rdy, mh_rdy, zer = sem("dec_e"), sem("dec_rdy"), sem("mh_rdy"), sem("zer")
        mvt, memv_rdy, mkv_st, mkv_ld = sem("mvt"), sem("memv_rdy"), sem("mkv_st"), sem("mkv_ld")
        ktr, vtr, st_mm, kv_mm, out_mm, y_tr = (sem(n) for n in ("ktr", "vtr", "st_mm", "kv_mm", "out_mm", "y_tr"))
        ktok_rdy, vfb_rdy, v_rdy, st_rdy, scan_rdy, qfb_rdy = (
            sem(n) for n in ("ktok_rdy", "vfb_rdy", "v_rdy", "st_rdy", "scan_rdy", "qfb_rdy"))
        var_rdy, grs_rdy, yn_rdy, aff, oc_rdy = (sem(n) for n in ("var_rdy", "grs_rdy", "yn_rdy", "aff", "oc_rdy"))
        s_mm, s_add, s_exp, s_nrm, s_tr, pt_ev, pv, o_ev = (
            sem(n) for n in ("s_mm", "s_add", "s_exp", "s_nrm", "s_tr", "pt_ev", "pv", "o_ev"))
        vn_tr, vn_a, vn_d = sem("vn_tr"), sem("vn_a"), sem("vn_d")
        rpb_st, tb_ld, tb_m, tb_rdy, nmask_ld, qz = (
            sem("rpb_st"), [sem("tb_ld0"), sem("tb_ld1")], sem("tb_m"), sem("tb_rdy"), sem("nmask_ld"), sem("qz"))
        d_own, p_own, a_own = sem("d_own"), sem("p_own"), sem("a_own")

        EV = {}
        counts = {"a": 0, "d": 0}

        def taken_by(n, who):
            counts[who] += 1
            EV[n] = (ev_act if who == "a" else ev_dve, counts[who])

        for n in range(4):
            taken_by(n, "ddaa"[n])
        for n in range(2):
            taken_by(U_RET + n, "a")
        for n in range(4 * RH):
            taken_by(U_RETH + n, "ddaa"[n % 4])
        for n in range(2):
            taken_by(U_NA + n, "a")
        for n in range(3 * HP):
            taken_by(U_NAH + n, "ada"[n % 3])

        def tiles_before(t):
            return 0 if t == 0 else 2 + 4 * (t - 1)

        N_TURNS = [2, 4, 4, KD, KD, KD, 4, KD, KD]

        def turned(t):
            return sum(N_TURNS[:t + 1])

        def set_of(s, th):
            return 2 * s + 1 + th

        def y_tiles(s, th):
            return Yb if s in (0, 2) and th == 0 else Y

        def set_tiles(t):
            return Hb if t == 0 else Yb if t in (1, 3, 7) else Y

        def pre_tile(xi):
            return Hb[:, xi, :] if xi < 2 else Yb[:, xi - 2, :] if xi < 6 else Y[:, xi - 6, :]

        GAIN = [4, 0, 0, 1, 1, 2, 2, 3, 3]
        U_FF = [U_FF0, U_FF1]
        U_OUT = [U_OUT0, U_OUT1]
        U_IN = [U_RET, U_NA]
        N_IN = [4 * RH + 2, 3 * HP + 2]
        R_ROW = 32
        R_END = [16, R_ROW + HP * ROWS]
        RUN_A0 = (0, 8, 0, 0)
        RUN_B0 = (8, 8, 1, 7)
        RUN_A1 = (16, 16, 0, 8)

        def o_count(r):
            return r if r <= R_ROW else R_ROW + (r - R_ROW) // 4

        DIRECT = (6, 7, 15)

        def stored(c):
            return 16 * len([b for b in range(c % 2, c + 1, 2) if b not in DIRECT])

        def banks(r):
            return (r % 2, 2, 3) if RUN_B0[0] <= r < R_END[0] else (4 + r % 2, 6, 7)

        def key_row(r):
            return min(max(r - WR // 2, 0), ROWS - WR)

        PIECES = 3 * KD

        def pieces_at(t, total=PIECES, steps=ROWS):
            return range(total * t // steps, total * (t + 1) // steps) if t < steps else range(0)

        def units_done(t, total, steps):
            return [u for u in range(total // KD) if KD * u + KD - 1 in pieces_at(t, total, steps)]

        def steps(run):
            return run[1] + 3
        LAST = ROWS + 4

        block = ctx.enter_context(nc.Block())

        @block.sync
        def _(sp):
            issued = [0]

            def load_units(upto):
                for n in range(issued[0], min(upto, U_END)):
                    if n >= RING:
                        sp.wait_ge(w_lo, n - RING + 1)
                    sp.dma_start(stage[:, n % RING, :], wpack[ROW[n], :, :]).then_inc(w_in[n % RING], 16)
                issued[0] = max(issued[0], min(upto, U_END))

            def load_pre(xi):
                src = mem[xi * P:(xi + 1) * P, :] if xi < 2 else x[(xi - 2) * P:(xi - 1) * P, :]
                sp.dma_start(pre_tile(xi), src).then_inc(x_ld[xi], 16)

            def load_h(e):
                s, t = e // 8, e % 8
                if e >= TT:
                    sp.wait_ge(h_st[e % TT], 16 * (e // TT))
                if e >= TT and e - TT < 24:
                    sp.wait_ge(xs, 10 + e - TT + 1)
                src = x if s == 0 else h_dram
                sp.dma_start(Hb[:, e % TT, :], src[t * P:(t + 1) * P, :]).then_inc(h_ld[e % TT], 16)

            def store_h(e):
                t = e % 8
                sp.wait_ge(h_new, e + 1)
                dst = h_dram if e < 24 else out
                sp.dma_start(dst[t * P:(t + 1) * P, :], Hb[:, e % TT, :]).then_inc(h_st[e % TT], 16)

            def load_gain(s):
                if s:
                    sp.wait_ge(h_new, 8 * s)
                sp.dma_start(gB[:, :], gain_rows[s:s + 1, :].partition_broadcast(P)).then_inc(g_ld, 16)

            def post(s, th):
                for i in range(TT):
                    store_h(8 * s + 4 * th + i)
                if (s, th) != (1, 1):
                    for i in range(TT):
                        if 8 * s + 4 * th + i + TT < N_E:
                            load_h(8 * s + 4 * th + i + TT)
                    if th and s < 3:
                        load_gain(s + 1)

            def before_out(l):
                sp.wait_ge(oc_rdy, 8 * l + 8)
                for i in range(TT):
                    load_h(16 * l + i)
                load_gain(2 * l)

            def store_cat(c):
                sp.wait_ge(oc_rdy, c + 1)
                sp.dma_start(cat_dram[c // 8, c % 8, :, :], OC[:, c % 2, :]).then_inc(oc_st[c % 2], 16)

            def cat_back(l, tiles):
                sp.wait_ge(w_used, U_IN[l] + N_IN[l])
                for k in tiles:
                    sp.wait_ge(oc_st[k % 2], stored(8 * l + k))
                    sp.dma_start(catf[:, k, :], cat_dram[l, k, :, :]).then_inc(cat_ld[k], 16)

            def ffn(l):
                for th in range(2):
                    n0 = U_FF[l] + 3 * KH * th
                    for j in range(3):
                        load_units(n0 + 2 * j + 7)
                    with sp.Fori(0, 6) as i:
                        for c in range(6):
                            m = n0 + 6 + c + 5
                            sp.wait_ge(w_lo, i * 6 + (m - RING + 1))
                            sp.dma_start(stage[:, m % RING, :], wpack[bass.ds(i * 6 + (ROW[n0] + m - n0), 1), :, :]
                                         .rearrange("a p c -> p (a c)")).then_inc(w_in[m % RING], 16)
                    issued[0] += 36
                    load_units(n0 + 3 * KH + 5)
                    post(1 + 2 * l, th)

            load_pre(0)
            load_pre(1)
            sp.dma_start(ident[:, :], ident_c).then_inc(c_ids, 16)
            sp.dma_start(gT[:, :, :], gains).then_inc(c_ids, 16)
            load_pre(2)
            load_pre(3)
            load_units(1)
            load_pre(4)
            load_pre(5)
            load_units(2)
            for xi in range(6, 10):
                load_pre(xi)
            load_units(5)
            sp.dma_start(colc[:, :], decay_consts[:, 6 * P:6 * P + 8]).then_inc(c_ld, 16)
            sp.dma_start(lgb[:, :], decay.partition_broadcast(P)).then_inc(c_ld, 16)
            sp.dma_start(gnT[:, :, :], gn).then_inc(c_ld, 16)
            sp.dma_start(ropeC[:, :], ropes[0, :, :]).then_inc(c_ld, 16)
            sp.dma_start(ropeS[:, :], ropes[1, :, :]).then_inc(c_ld, 16)
            sp.dma_start(rpb_dram[RPB_PAD:RPB_PAD + rpb_n], rpb).then_inc(rpb_st, 16)
            sp.wait_ge(zer, 2)
            for first in (0, RPB_PAD + rpb_n):
                sp.dma_start(bass.AP(rpb_dram, first, [[8, 8], [1, 8]]),
                             kprod[0:8, :, :].rearrange("p a c -> p (a c)")[:, 0:8]).then_inc(rpb_st, 16)
            load_units(U_RET + 5)
            sp.wait_ge(memv_rdy, 1)
            sp.wait_ge(ev_dve, 2)
            sp.dma_start(memkv_dram[:, 0:1024], bdK[:, :, :].rearrange("p a c -> p (a c)")).then_inc(mkv_st, 16)
            sp.dma_start(memkv_dram[:, 1024:1536], memV[:, :, :].rearrange("p a c -> p (a c)")).then_inc(mkv_st, 16)
            sp.wait_ge(t_done, turned(2))
            sp.dma_start(dconst[:, :, :], decay_consts[:, 0:6 * P].rearrange("p (a c) -> p a c", a=6)).then_inc(c_ld, 16)
            load_units(U_RETH + 4 + 5)
            store_cat(0)
            for h in range(1, RH):
                load_units(U_RETH + 4 * h + 4 + 5)
                store_cat(h)
            load_units(U_OUT0 + 5)
            cat_back(0, range(RH))
            before_out(0)
            for th in range(2):
                load_units(U_OUT0 + KD * (th + 1) + 5)
                post(0, th)
            ffn(0)

            def load_bias(hp):
                if hp >= 2:
                    sp.wait_ge(s_add, R_ROW + ROWS * (hp - 1))
                for g in range(2):
                    first = RPB_PAD + (2 * hp + g) * 465 + WC - 1 - (GW - 1)
                    src = bass.AP(rpb_dram, first, [[1, GW], [31, 15], [1, GW]])
                    sp.dma_start(TB[GW * g:GW * g + GW, hp % 2, :, :], src).then_inc(tb_ld[hp % 2], 16)

            sp.wait_ge(w_used, U_NA)
            sp.wait_ge(mkv_st, 32)
            sp.wait_ge(pre_sq, 26)
            sp.dma_start(bdK[:, :, :].rearrange("p a c -> p (a c)"), memkv_dram[:, 0:1024]).then_inc(mkv_ld, 16)
            sp.dma_start(memV[:, :, :].rearrange("p a c -> p (a c)"), memkv_dram[:, 1024:1536]).then_inc(mkv_ld, 16)
            sp.dma_start(nmask[:, :, :], na_masks).then_inc(nmask_ld, 16)
            sp.wait_ge(rpb_st, 48)
            load_bias(0)
            load_bias(1)
            load_units(U_NAH + 3 + 5)
            store_cat(8)
            store_cat(9)
            for hp in range(1, HP):
                load_units(U_NAH + 3 * hp + 3 + 5)
                store_cat(9 + hp)
                if hp + 1 < HP:
                    load_bias(hp + 1)
            load_units(U_OUT1 + 5)
            cat_back(1, range(KD - 1))
            before_out(1)
            for th in range(2):
                load_units(U_OUT1 + KD * (th + 1) + 5)
                post(2, th)
            ffn(1)
            for i in range(TT):
                sp.wait_ge(h_st[i], 16 * (N_E // TT))

        @block.gpsimd
        def _(pool):
            done = [0]
            own = [0]

            def link(ins):
                own[0] += 1
                ins.then_inc(p_own, 1)
                pool.wait_ge(p_own, own[0])

            def split_lo(n, slot, need):
                pool.wait_ge(w_hi, need)
                pool.tensor_tensor(wlo[:, slot, :], stage[:, slot, :], whi[:, slot, :].bitcast(F32), ALU.subtract)\
                    .then_inc(w_lo, 1)

            def los(upto):
                for n in range(done[0], min(upto, U_END)):
                    split_lo(n, n % RING, n + 1)
                done[0] = max(done[0], min(upto, U_END))

            def inv_rms(col, ready, need, signal):
                pool.wait_ge(ready, need)
                link(pool.tensor_scalar(msq[:, col:col + 1], sumsq[:, col:col + 1], 1.0 / D, 1e-6, ALU.mult, ALU.add))
                pool.tensor_tensor(rstd[:, col:col + 1], msq[:, col:col + 1], minus_half[:, 0:1], ALU.pow)\
                    .then_inc(signal, 1)

            def pre(xi):
                inv_rms(xi, pre_sq, xi + 1, pre_rs)

            def post(s, th, upto=None):
                for i in range(TT):
                    e = 8 * s + 4 * th + i
                    inv_rms(N_T + e, y_sq, e + 1, post_rs)
                for i in range(TT):
                    if upto is not None and i % 2 == 0:
                        los(upto - 1 + i // 2)
                    if s < 3:
                        pre(10 + 8 * s + 4 * th + i)

            def ffn(l):
                for th in range(2):
                    n0 = U_FF[l] + 3 * KH * th
                    for j in range(3):
                        los(n0 + 2 * j + 4)
                    with pool.Fori(0, 6) as i:
                        for c in range(6):
                            m = n0 + 6 + c + 2
                            split_lo(m, m % RING, i * 6 + (m + 1))
                    done[0] += 36
                    los(n0 + 3 * KH + 2)
                    post(1 + 2 * l, th, n0 + 3 * KH + 5 if th == 0 else None)

            pool.memset(minus_half[:, :], -0.5).then_inc(mh_rdy, 1)
            pool.wait_ge(mh_rdy, 1)
            pre(0)
            pre(1)
            pool.memset(bdK[:, :, :], 0.0).then_inc(zer, 1)
            pool.memset(kprod[:, :, :], 0.0).then_inc(zer, 1)
            pool.wait_ge(zer, 2)
            pre(2)
            pre(3)
            los(1)
            pre(4)
            pre(5)
            los(3)
            for xi in range(6, 10):
                pre(xi)
                if xi < 8:
                    los(xi - 2)
            los(U_RETH + 2)

            for h in range(RH + 1):
                n = U_RETH + 4 * h
                los(min(n + 3, U_OUT0 + 2))
                if h:
                    los(min(n + 5, U_OUT0 + 2))
                    pool.wait_ge(var_rdy, h)
                    link(pool.tensor_scalar(gvar[:, :], mv[:, :, 1], 1.0, 1e-5, ALU.mult, ALU.add))
                    pool.tensor_tensor(grstd[:, :], gvar[:, :], minus_half[:, :], ALU.pow).then_inc(grs_rdy, 1)
                if h < RH:
                    los(n + 6)
            los(U_OUT0 + 2)
            for th in range(2):
                los(U_OUT0 + KD * (th + 1) + 2)
                post(0, th, U_OUT0 + KD * (th + 1) + 5)
            ffn(0)
            pool.wait_ge(w_used, U_NA)
            pool.wait_ge(pre_rs, 26)
            pool.wait_ge(w_lo, done[0])
            for g in range(2):
                for b in range(2):
                    pool.memset(qbd[GW * b:GW * b + GW, g, :, 1 - b, :], 0.0).then_inc(qz, 1)
                    pool.wait_ge(qz, 2 * g + b + 1)

            def mask_bias(hp):
                pool.wait_ge(tb_ld[hp % 2], 32 * (hp // 2 + 1))
                t = TB[:, hp % 2, :, :]
                link(pool.tensor_tensor(t, t, nmask[:, 0:1, :].to_broadcast([P, 15, GW]), ALU.mult))
                pool.tensor_tensor(t, t, nmask[:, 1:2, :].to_broadcast([P, 15, GW]), ALU.add).then_inc(tb_rdy, 1)

            pool.wait_ge(nmask_ld, 16)
            mask_bias(0)
            los(U_NAH + 2)
            for hp in range(HP):
                los(min(U_NAH + 3 * hp + 5, U_OUT1 + 2))
                if hp + 1 < HP:
                    mask_bias(hp + 1)
            los(U_OUT1 + 2)
            for th in range(2):
                los(U_OUT1 + KD * (th + 1) + 2)
                post(2, th, U_OUT1 + KD * (th + 1) + 5)
            ffn(1)

        @block.scalar
        def _(act):
            done = [0]

            def split_hi(slot, come, used):
                act.wait_ge(w_in[slot], come)
                if used is not None:
                    act.wait_ge(w_used, used)
                act.activation(whi[:, slot, :], stage[:, slot, :], ACT.Copy).then_inc(w_hi, 1)

            def his(upto):
                for n in range(done[0], min(upto, U_END)):
                    split_hi(n % RING, 16 * (n // RING + 1), n - RING + 1 if n >= RING else None)
                done[0] = max(done[0], min(upto, U_END))

            squares = []

            def square(src, col, ready, need, signal):
                act.wait_ge(ready, need)
                n = len(squares)
                if n >= 2:
                    act.wait_ge(*squares[n - 2])
                squares.append((signal, 1 + sum(s is signal for s, _ in squares)))
                act.activation(junk[n % 2][:, :], src, ACT.Square, accum_out=sumsq[:, col:col + 1]).then_inc(signal, 1)

            def pre_x(xi):
                square(pre_tile(xi), xi, x_ld[xi], 16, pre_sq)

            def turn(t):
                width = MEM if t == 0 else HALF
                th = 1 if t in (2, 6) else 0
                if N_TURNS[t] < KD and t not in (2, 6):
                    act.wait_ge(t_done, turned(t))
                if t == 0:
                    act.wait_ge(c_ids, 32)
                for k in range(KD):
                    if t in (2, 6) and k == 0:
                        act.wait_ge(t_low, t // 4 + 1)
                    if t in (2, 6) and k == 4:
                        act.wait_ge(t_done, turned(t))
                    if N_TURNS[t] == KD:
                        act.wait_ge(t_done, turned(t - 1) + k + 1)
                    bank = 4 + k % 4 if t in (2, 6) else k
                    act.activation(aT[:, th, 0, k, 0:width], PS[:, bank, 0:width], ACT.Copy,
                                   scale=gT[:, GAIN[t], k:k + 1]).then_inc(a_hi, 1)

            def post_in(s, th):
                for i in range(TT):
                    e = 8 * s + 4 * th + i
                    square(PS[:, 2 * i:2 * i + 2, :].rearrange("p a c -> p (a c)"), N_T + e, y_done, e + 1, y_sq)

            def post_out(s, th, upto=None, first=None):
                for i in range(TT):
                    if i == 0 and first is not None:
                        first()
                    elif i == 0 and upto is not None:
                        his(upto - 1)
                    if i == 2 and upto is not None:
                        his(upto)
                    if s < 3:
                        e = 8 * s + 4 * th + i
                        square(Hb[:, i, :], 10 + e, h_new, e + 1, pre_sq)

            def silu_gate(slot, need, free):
                act.wait_ge(w_used, need)
                if free is not None:
                    act.wait_ge(hid_t, free)
                act.activation(sg[:, slot, :], PS[:, 2 * slot, :], ACT.Silu).then_inc(g_act, 1)

            def ffn_tile(l, th, j):
                n = U_FF[l] + 3 * KH * th + 2 * j
                g = (2 * l + th) * KH + j
                his(n + 3)
                silu_gate(j % 3, n + 1, g - 2 if g >= 3 else None)
                his(n + 4)

            def post_then_ffn(s, l, th):
                post_out(s, 1 - th, U_FF[l] + 3 * KH * th + 5, lambda: ffn_tile(l, th, 0))

            def ffn(l):
                for th in range(2):
                    n0 = U_FF[l] + 3 * KH * th
                    g0 = (2 * l + th) * KH
                    for j in range(1, 3):
                        ffn_tile(l, th, j)
                    with act.Fori(0, 6) as i:
                        for c in range(3):
                            m = n0 + 2 * (3 + c)
                            for part in range(2):
                                u = m + 2 + part
                                split_hi(u % RING, i * 32 + 16 * (u // RING + 1), i * 6 + (u - RING + 1))
                                if part == 0:
                                    silu_gate(c, i * 6 + (m + 1), i * 3 + (g0 + 3 + c - 2))
                    done[0] += 36
                    ffn_tile(l, th, KH - 1)
                    if th == 0 or l == 0:
                        turn(4 * l + 4 + th)
                    his(n0 + 3 * KH + 2)
                    post_in(1 + 2 * l, th)
                    if th == 0:
                        post_then_ffn(1 + 2 * l, l, 1)
                    else:
                        post_out(1 + 2 * l, th)

            def probs(r, is_mem):
                act.wait_ge(s_add, r + 1)
                if is_mem:
                    if r >= 3:
                        act.wait_ge(s_tr, r - 2)
                    bank = banks(r)[0]
                    for g in range(2):
                        ins = act.activation(SB[:, r % 3, MEM * g:MEM * g + MEM], PS[:, bank, MEM * g:MEM * g + MEM],
                                             ACT.Exp, bias=negmax[:, r % 4, g:g + 1], scale=0.125,
                                             accum_out=rowsum[:, r % 4, g:g + 1])
                    ins.then_inc(s_exp, 1)
                else:
                    act.activation(SB[:, r % 3, :], SB[:, r % 3, :], ACT.Exp, bias=negmax[:, r % 4, 0:1], scale=-1.0,
                                   accum_out=rowsum[:, r % 4, 0:1]).then_inc(s_exp, 1)

            def take_pt(r):
                act.wait_ge(s_tr, r + 1)
                if r >= 2:
                    act.wait_ge(pv, r - 1)
                act.activation(PT[:, r % 2, :], PS[:, banks(r)[1], :], ACT.Copy).then_inc(pt_ev, 1)

            def take(n, dst, func=ACT.Copy):
                act.wait_ge(w_used, n + 1)
                for th in range(2):
                    ins = act.activation(dst[:, HALF * th:HALF * th + HALF], PS[:, 2 * (n % 2) + th, :], func)
                ins.then_inc(ev_act, 1)

            def mem_step(run, t):
                r0, tiles = run[:2]
                if t < tiles:
                    probs(r0 + t, True)
                if 0 <= t - 2 < tiles:
                    take_pt(r0 + t - 2)

            def cat_split(l):
                for th in range(2):
                    for k in range(KD):
                        if 8 * l + k in DIRECT:
                            act.wait_ge(oc_rdy, 8 * l + k + 1)
                        else:
                            act.wait_ge(cat_ld[k], 16 if k == 6 else 16 * (l + 1))
                        act.activation(catT[:, th, 0, k, :], catf[:, k, HALF * th:HALF * th + HALF], ACT.Copy)\
                           .then_inc(cat_hi, 1)

            for xi in range(4):
                pre_x(xi)
            his(1)
            pre_x(4)
            pre_x(5)
            turn(0)
            his(3)
            for xi in range(6, 10):
                pre_x(xi)
                if xi == 8:
                    act.wait_ge(w_used, 3)
                    act.activation(mvT[:, 0, :], PS[:, 0, 0:MEM], ACT.Copy).then_inc(ev_act, 1)
                    act.wait_ge(w_used, 4)
                    act.activation(mvT[:, 1, :], PS[:, 2, 0:MEM], ACT.Copy).then_inc(ev_act, 1)
                elif xi < 8:
                    his(xi - 2)
            turn(1)
            his(U_RET + 2)
            turn(2)
            his(U_RET + 3)
            take(U_RET, MQ[:, 0, :])
            his(U_RET + 4)
            take(U_RET + 1, MQ[:, 1, :])

            def decays(t):
                if t == 2:
                    act.wait_ge(c_ld, 96)
                    act.activation(lgb[:, :], lgb[:, :], ACT.Exp).then_inc(dec_e, 1)
                if t == 3:
                    act.wait_ge(dec_rdy, 1)
                    act.activation(kdec[:, :, :], kprod[:, :, :], ACT.Exp)
                    act.activation(cdec[:, :, :], lg[:, :, :], ACT.Exp, scale=float(P)).then_inc(dec_e, 1)
                    for d in range(2):
                        for h in range(RH):
                            ins = act.activation(QD[:, d, h, :], dconst[:, 4 + d, :], ACT.Exp, scale=lg[:, d, h:h + 1])
                    ins.then_inc(dec_e, 1)
                if 4 <= t < 4 + RH:
                    h = t - 4
                    if h:
                        act.wait_ge(dec_rdy, 1 + h)
                    for d in range(2):
                        ins = act.activation(dexp[:, d, :], dconst[:, d, :], ACT.Exp, scale=lg[:, d, h:h + 1])
                    ins.then_inc(dec_e, 1)

            def take_value_gate(h, i):
                n = U_RETH + 4 * h + i
                his(n + 3)
                if i == 2:
                    take(n, vT[:, :])
                if i == 3:
                    c = 1 + h
                    if c >= 2:
                        act.wait_ge(oc_st[c % 2], stored(c - 2))
                    take(n, OC[:, c % 2, :], ACT.Silu)

            for t in range(steps(RUN_A0)):
                mem_step(RUN_A0, t)
                decays(t)
                for u in units_done(t, 4 * KD, steps(RUN_A0)):
                    take_value_gate(0, u)
            for h in range(1, RH + 1):
                n = U_RETH + 4 * h
                g = h - 1
                if h < RH:
                    his(n + 3)
                act.wait_ge(ktr, h)
                for b in range(2):
                    ins = act.activation(Ktok[:, 4 * b:4 * b + 4, :].rearrange("p a c -> p (a c)"), PS[:, 4 + b, :], ACT.Copy)
                ins.then_inc(ktok_rdy, 1)
                act.wait_ge(vtr, h)
                if h == 1:
                    act.wait_ge(dec_rdy, 2 + RH)
                for b in range(2):
                    for d in range(2):
                        ins = act.activation(vfb[:, 4 * b:4 * b + 4, d, :],
                                             PS[:, 6 + b, :].rearrange("p (a c) -> p a c", a=4), ACT.Copy,
                                             scale=kdec[:, d, g:g + 1])
                ins.then_inc(vfb_rdy, 1)
                if h < RH:
                    his(n + 4)
                    take_value_gate(h, 2)
                    take_value_gate(h, 3)
                else:
                    for t in range(9):
                        mem_step(RUN_B0, t)
                act.wait_ge(y_tr, h)
                for b in range(2):
                    ins = act.activation(PS[:, 4 + b, :], PS[:, 4 + b, :], ACT.Identity,
                                         scale=gnT[:, 0, g:g + 1], bias=gnT[:, 1, g:g + 1])
                ins.then_inc(aff, 1)
            for t in range(9, steps(RUN_B0)):
                mem_step(RUN_B0, t)
            his(U_OUT0 + 2)
            cat_split(0)
            his(U_OUT0 + KD + 2)
            post_in(0, 0)
            post_out(0, 0, U_OUT0 + KD + 5)
            his(U_OUT0 + 2 * KD + 2)
            post_in(0, 1)
            turn(3)
            post_then_ffn(0, 0, 0)
            ffn(0)
            turn(6)
            for i in range(TT):
                act.wait_ge(h_st[i], 64)
            act.wait_ge(h_new, 16)
            his(U_NA + 3)
            take(U_NA, MQ[:, 0, :])
            his(U_NA + 4)
            take(U_NA + 1, MQ[:, 1, :])

            def take_q(n, dst):
                act.wait_ge(w_used, n + 1)
                for th in range(2):
                    for b in range(2):
                        ins = act.activation(
                            dst[GW * b:GW * b + GW, 8 * th:8 * th + 8, b, ::-1],
                            PS[GW * b:GW * b + GW, 2 * (n % 2) + th, :].rearrange("p (a c) -> p a c", a=8),
                            ACT.Copy, scale=0.125)
                ins.then_inc(ev_act, 1)

            def take_query_value(hp, i):
                n = U_NAH + 3 * hp + i
                his(n + 3)
                if i == 0:
                    take_q(n, qbd[:, hp % 2, :, :, :])
                if i == 2:
                    take(n, vTn[:, :])

            act.wait_ge(qz, 4)
            for t in range(steps(RUN_A1)):
                mem_step(RUN_A1, t)
                for u in units_done(t, PIECES, steps(RUN_A1)):
                    take_query_value(0, u)
            for hp in range(1, HP + 1):
                act.wait_ge(vn_tr, 2 * hp - 1)
                for b in range(2):
                    ins = act.activation(Ve[:, 4 * b:4 * b + 4, :].rearrange("p a c -> p (a c)"), PS[:, 4 + b, :], ACT.Copy)
                ins.then_inc(vn_a, 1)
                r0 = R_ROW + ROWS * (hp - 1)
                for t in range(LAST):
                    if t < ROWS:
                        probs(r0 + t, False)
                    if 0 <= t - 2 < ROWS:
                        take_pt(r0 + t - 2)
                    if hp < HP:
                        for u in units_done(t, PIECES, ROWS):
                            take_query_value(hp, u)
            his(U_OUT1 + 2)
            cat_split(1)
            his(U_OUT1 + KD + 2)
            post_in(2, 0)
            post_out(2, 0, U_OUT1 + KD + 5)
            his(U_OUT1 + 2 * KD + 2)
            post_in(2, 1)
            turn(7)
            post_then_ffn(2, 1, 0)
            ffn(1)

        @block.vector
        def _(dve):
            own = [0]
            place = [None]

            def link(ins):
                own[0] += 1
                ins.then_inc(d_own, 1)
                dve.wait_ge(d_own, own[0])

            def pre(xi, src, dst):
                dve.wait_ge(pre_rs, xi + 1)
                dve.tensor_scalar(dst, src, rstd[:, xi:xi + 1], None, ALU.mult).then_inc(xs, 1)

            def turn(t):
                width = MEM if t == 0 else HALF
                th = 1 if t in (2, 6) else 0
                for k in range(KD):
                    bank = 4 + k % 4 if t in (2, 6) else k
                    dve.wait_ge(a_hi, 8 * t + k + 1)
                    dve.scalar_tensor_tensor(out=aT[:, th, 1, k, 0:width], in0=PS[:, bank, 0:width],
                                             scalar=gT[:, GAIN[t], k:k + 1],
                                             in1=aT[:, th, 0, k, 0:width].bitcast(F32),
                                             op0=ALU.mult, op1=ALU.subtract).then_inc(a_lo, 1)

            def post_in(s, th):
                Yt = y_tiles(s, th)
                dve.wait_ge(g_ld, 16 * (s + 1))
                if Yt is Y:
                    dve.wait_ge(t_done, turned({(0, 1): 2, (1, 0): 4, (1, 1): 5, (2, 1): 6, (3, 0): 8, (3, 1): 8}[s, th]))
                for i in range(TT):
                    e = 8 * s + 4 * th + i
                    dve.wait_ge(post_rs, e + 1)
                    dve.scalar_tensor_tensor(out=Yt[:, i, :], in0=PS[:, 2 * i:2 * i + 2, :].rearrange("p a c -> p (a c)"),
                                             scalar=rstd[:, N_T + e:N_T + e + 1], in1=gB[:, :],
                                             op0=ALU.mult, op1=ALU.mult).then_inc(y_cp, 1)

            def post_out(s, th):
                Yt = y_tiles(s, th)
                for i in range(TT):
                    e = 8 * s + 4 * th + i
                    dve.wait_ge(y_cp, e + 1)
                    dve.wait_ge(h_ld[i], 16 * (e // TT + 1))
                    dve.tensor_tensor(Hb[:, i, :], Hb[:, i, :], Yt[:, i, :], ALU.add).then_inc(h_new, 1)
                    if s < 3 and i:
                        pre(10 + e - 1, Hb[:, i - 1, :], Yt[:, i - 1, :])
                if s < 3:
                    pre(10 + e, Hb[:, TT - 1, :], Yt[:, TT - 1, :])

            def hidden(slot, up_need, gate_need, last):
                dve.wait_ge(g_act, gate_need)
                if last is not None:
                    dve.wait_ge(hid_rdy, last)
                dve.wait_ge(w_used, up_need)
                ins = dve.tensor_tensor(hidf[:, :], sg[:, slot, :], PS[:, 2 * slot + 1, :], ALU.mult)
                ins.then_inc(hid_t, 1)

            def hidden_split(dst_hi, dst_lo, need):
                dve.wait_ge(hid_t, need)
                link(dve.tensor_copy(dst_hi, hidf[:, :]))
                dve.tensor_tensor(dst_lo, hidf[:, :], dst_hi.bitcast(F32), ALU.subtract).then_inc(hid_rdy, 1)

            def ffn(l):
                for th in range(2):
                    n0 = U_FF[l] + 3 * KH * th
                    g0 = (2 * l + th) * KH

                    def tile(j):
                        hi, lo = hid[:, 0, j, :], hid[:, 1, j, :]
                        hidden(j % 3, n0 + 2 * j + 2, g0 + j + 1, g0 + j if g0 + j else None)
                        hidden_split(hi, lo, g0 + j + 1)

                    for j in range(3):
                        tile(j)
                    with dve.Fori(0, 6) as i:
                        for c in range(3):
                            j = 3 + c
                            hi = hid[:, 0, bass.ds(i * 3 + j, 1), :].rearrange("p a c -> p (a c)")
                            lo = hid[:, 1, bass.ds(i * 3 + j, 1), :].rearrange("p a c -> p (a c)")
                            hidden(c, i * 6 + (n0 + 2 * j + 2), i * 3 + (g0 + j + 1), i * 3 + (g0 + j))
                            dve.wait_ge(hid_t, i * 3 + (g0 + j + 1))
                            dve.tensor_copy(hi, hidf[:, :]).then_inc(d_own, 1)
                            dve.wait_ge(d_own, i * 3 + (own[0] + c + 1))
                            dve.tensor_tensor(lo, hidf[:, :], hi.bitcast(F32), ALU.subtract).then_inc(hid_rdy, 1)
                    own[0] += 18
                    tile(KH - 1)
                    if th == 0 or l == 0:
                        turn(4 * l + 4 + th)
                    post_in(1 + 2 * l, th)
                    post_out(1 + 2 * l, th)

            def peak(r, is_mem, row=0, hp=0):
                dve.wait_ge(s_mm, r + 1)
                if r >= 4:
                    dve.wait_ge(s_exp, r - 3)
                bank = banks(r)[0]
                if is_mem:
                    link(dve.tensor_reduce(maxraw[:, r % 4, :], PS[:, bank, :].rearrange("p (g c) -> p g c", g=2),
                                           AX.X, ALU.max))
                    dve.tensor_scalar(negmax[:, r % 4, :], maxraw[:, r % 4, :], -0.125, None, ALU.mult).then_inc(s_add, 1)
                else:
                    if row == 0:
                        dve.wait_ge(tb_rdy, hp + 1)
                    if r >= 3:
                        dve.wait_ge(s_tr, r - 2)
                    dr = key_row(row) - row + WR - 1
                    bias = TB[:, hp % 2, dr:dr + WR, :].rearrange("p a c -> p (a c)")
                    dve.tensor_tensor_reduce(SB[:, r % 3, :], PS[:, bank, :], bias, -1.0, 3.0e38,
                                             ALU.add, ALU.min, negmax[:, r % 4, 0:1]).then_inc(s_add, 1)

            def normalise(r, is_mem):
                dve.wait_ge(s_exp, r + 1)
                n = 2 if is_mem else 1
                link(dve.reciprocal(rowinv[:, r % 4, 0:n], rowsum[:, r % 4, 0:n]))
                w = 512 // n
                for g in range(n):
                    part = SB[:, r % 3, w * g:w * g + w]
                    ins = dve.tensor_scalar(part, part, rowinv[:, r % 4, g:g + 1], None, ALU.mult)
                ins.then_inc(s_nrm, 1)

            def output_place(c):
                if c in DIRECT:
                    dve.wait_ge(w_used, U_OUT[c // 8])
                    return catf[:, c % 8, :]
                if c >= 2:
                    dve.wait_ge(oc_st[c % 2], stored(c - 2))
                return OC[:, c % 2, :]

            def mem_step(run, t):
                r0, tiles, _, c0 = run
                q = t - 4
                if 0 <= q < tiles:
                    r, i = r0 + q, q % 8
                    if i == 0:
                        place[0] = output_place(c0 + q // 8)
                    dve.wait_ge(pv, r + 1)
                    for g in range(2):
                        ins = dve.tensor_copy(place[0][64 * g:64 * g + 64, i * P:(i + 1) * P],
                                              PS[64 * g:64 * g + 64, banks(r)[2], P * g:P * g + P])
                    ins.then_inc(o_ev, 1)
                    if i == 7:
                        dve.wait_ge(o_ev, o_count(r + 1))
                        dve.engine_nop().then_inc(oc_rdy, 1)
                if t < tiles:
                    peak(r0 + t, True)
                if 0 <= t - 1 < tiles:
                    normalise(r0 + t - 1, True)

            def cat_split(l):
                for th in range(2):
                    for k in range(KD):
                        dve.wait_ge(cat_hi, 16 * l + 8 * th + k + 1)
                        dve.tensor_tensor(catT[:, th, 1, k, :], catf[:, k, HALF * th:HALF * th + HALF],
                                          catT[:, th, 0, k, :].bitcast(F32), ALU.subtract).then_inc(cat_lo, 1)

            def rotate(n, dst):
                dve.wait_ge(w_used, n + 1)
                for th in range(2):
                    cols = slice(HALF * th, HALF * th + HALF)
                    src = PS[:, 2 * (n % 2) + th, :]
                    dve.tensor_tensor(dst[:, cols], src, ropeC[:, cols], ALU.mult)
                    dve.tensor_tensor(rtmp[0:64, :], src[64:128, :], ropeS[64:128, cols], ALU.mult)
                    link(dve.tensor_tensor(rtmp[64:128, :], src[0:64, :], ropeS[0:64, cols], ALU.mult))
                    ins = dve.tensor_tensor(dst[:, cols], dst[:, cols], rtmp[:, :], ALU.add)
                    if th == 0:
                        link(ins)
                ins.then_inc(ev_dve, 1)
                dve.wait_ge(*EV[n])

            for xi in range(4):
                pre(xi, pre_tile(xi), pre_tile(xi))
            turn(0)
            pre(4, pre_tile(4), pre_tile(4))
            pre(5, pre_tile(5), pre_tile(5))
            dve.wait_ge(zer, 1)
            for n in range(2):
                dve.wait_ge(w_used, n + 1)
                for g in range(2):
                    ins = dve.tensor_copy(bdK[64 * g:64 * g + 64, n, MEM * g:MEM * g + MEM],
                                          PS[64 * g:64 * g + 64, 2 * n, 0:MEM])
                ins.then_inc(ev_dve, 1)
            for xi in range(6, 10):
                pre(xi, pre_tile(xi), pre_tile(xi))
            dve.wait_ge(mvt, 1)
            dve.tensor_copy(memV[:, :, :].rearrange("p k (h f) -> p h k f", h=2),
                            PS[:, 4, :].rearrange("p (h k f) -> p h k f", h=2, k=2)).then_inc(memv_rdy, 1)
            turn(1)
            turn(2)

            def decays(t):
                if t == 2:
                    dve.wait_ge(dec_e, 1)
                    link(dve.tensor_scalar(lg[:, :, :].rearrange("p a c -> p (a c)"), lgb[:, :], -1.0, None, ALU.mult))
                    dve.wait_ge(zer, 2)
                    dve.wait_ge(rpb_st, 48)
                    for d in range(2):
                        ins = dve.tensor_scalar(kprod[:, d, :], lg[:, d, :], colc[:, d:d + 1], None, ALU.mult)
                    ins.then_inc(dec_rdy, 1)
                if t == 3:
                    dve.wait_ge(dec_e, 2)
                    link(dve.tensor_scalar(kdec[:, :, :], kdec[:, :, :], float(P) ** -0.5, None, ALU.mult))
                if 4 <= t < 4 + RH:
                    h = t - 4
                    dve.wait_ge(dec_e, 4 + h)
                    dve.tensor_tensor(dexp[:, 0, :], dexp[:, 0, :], dconst[:, 2, :], ALU.mult)
                    link(dve.tensor_tensor(dexp[:, 1, :], dexp[:, 1, :], dconst[:, 3, :], ALU.mult))
                    dve.tensor_tensor(DM[:, h, :], dexp[:, 0, :], dexp[:, 1, :], ALU.add).then_inc(dec_rdy, 1)
                if t == 4 + RH:
                    dve.wait_ge(dec_rdy, 1 + RH)
                    dve.memset(states[:, 0, 0, :], 0.0)
                    dve.memset(states[:, 7, 1, :], 0.0).then_inc(dec_rdy, 1)
                    dve.wait_ge(dec_rdy, 2 + RH)

            def values(h):
                dve.wait_ge(vfb_rdy, h)
                for b in range(2):
                    ins = dve.tensor_copy(V[:, 4 * b:4 * b + 4, :].rearrange("p a c -> p (a c)"), PS[:, 6 + b, :])
                ins.then_inc(v_rdy, 1)
                dve.wait_ge(st_mm, h)
                for b in range(2):
                    ins = dve.tensor_tensor(ST[:, 4 * b:4 * b + 4, :], PS[:, 4 + b, :].rearrange("p (a c) -> p a c", a=4),
                                            DM[:, h - 1:h, :].to_broadcast([P, 4, P]), ALU.mult)
                ins.then_inc(st_rdy, 1)

            def scan(h):
                g = h - 1
                dve.wait_ge(kv_mm, h)

                def kv(c, d):
                    bank = (6, 7, 4, 5)[c // 2]
                    return PS[:, bank, 256 * (c % 2) + P * d:256 * (c % 2) + P * d + P]

                for c in range(7):
                    dve.scalar_tensor_tensor(out=states[:, c + 1, 0, :], in0=states[:, c, 0, :],
                                             scalar=cdec[:, 0, g:g + 1], in1=kv(c, 0), op0=ALU.mult, op1=ALU.add)
                    b = 7 - c
                    ins = dve.scalar_tensor_tensor(out=states[:, b - 1, 1, :], in0=states[:, b, 1, :],
                                                   scalar=cdec[:, 1, g:g + 1], in1=kv(b, 1),
                                                   op0=ALU.mult, op1=ALU.add)
                    if c < 6:
                        link(ins)
                ins.then_inc(scan_rdy, 1)
                for d in range(2):
                    ins = dve.tensor_tensor(qfb[:, d, :].rearrange("p (a c) -> p a c", a=8),
                                            qT[:, g % 2, :].rearrange("p (a c) -> p a c", a=8),
                                            QD[:, d, g:g + 1, :].to_broadcast([P, 8, P]), ALU.mult)
                ins.then_inc(qfb_rdy, 1)

            def group_norm(h):
                dve.wait_ge(out_mm, h)
                for c in range(8):
                    ins = dve.bn_stats(stats[:, c, :], PS[:, 6 + c // 4, (c % 4) * P:(c % 4 + 1) * P])
                link(ins)
                for c in range(8):
                    ins = dve.bn_aggr(mv[:, c, :], stats[:, c, :])
                ins.then_inc(var_rdy, 1)
                dve.wait_ge(grs_rdy, h)
                for c in range(8):
                    ins = dve.tensor_scalar(ST[:, c, :], PS[:, 6 + c // 4, (c % 4) * P:(c % 4 + 1) * P],
                                            mv[:, c, 0:1], grstd[:, c:c + 1], ALU.subtract, ALU.mult)
                ins.then_inc(yn_rdy, 1)

            def gated(h):
                g = h - 1
                dve.wait_ge(aff, h)
                dve.wait_ge(ev_act, EV[U_RETH + 4 * g + 3][1])
                dst = output_place(h) if h in DIRECT else OC[:, h % 2, :]
                for b in range(2):
                    cols = slice(HALF * b, HALF * b + HALF)
                    ins = dve.tensor_tensor(dst[:, cols], OC[:, h % 2, cols], PS[:, 4 + b, :], ALU.mult)
                ins.then_inc(oc_rdy, 1)

            for t in range(steps(RUN_A0) + 1):
                mem_step(RUN_A0, t)
                decays(t)
                for u in units_done(t, 4 * KD, steps(RUN_A0)):
                    if u < 2:
                        rotate(U_RETH + u, (qT[:, 0, :], kT[:, :])[u])
            for h in range(1, RH + 1):
                n = U_RETH + 4 * h
                if h < RH:
                    rotate(n, qT[:, h % 2, :])
                    values(h)
                    rotate(n + 1, kT[:, :])
                    scan(h)
                    group_norm(h)
                    gated(h)
                    continue
                values(h)
                for t in range(3):
                    mem_step(RUN_B0, t)
                scan(h)
                for t in range(3, 6):
                    mem_step(RUN_B0, t)
                group_norm(h)
                for t in range(6, 9):
                    mem_step(RUN_B0, t)
                gated(h)
                for t in range(9, steps(RUN_B0) + 1):
                    mem_step(RUN_B0, t)
            cat_split(0)
            post_in(0, 0)
            post_out(0, 0)
            post_in(0, 1)
            turn(3)
            post_out(0, 1)
            ffn(0)
            turn(6)
            for i in range(TT):
                dve.wait_ge(h_st[i], 64)

            def take_k(n):
                dve.wait_ge(w_used, n + 1)
                for th in range(2):
                    ins = dve.tensor_copy(kTn[:, ((n - U_NAH) // 3) % 2, HALF * th:HALF * th + HALF],
                                          PS[:, 2 * (n % 2) + th, :])
                ins.then_inc(ev_dve, 1)

            for t in range(steps(RUN_A1) + 1):
                mem_step(RUN_A1, t)
                for u in units_done(t, PIECES, steps(RUN_A1)):
                    if u == 1:
                        take_k(U_NAH + 1)
            for hp in range(1, HP + 1):
                dve.wait_ge(vn_tr, 2 * hp)
                dve.tensor_copy(Vo[:, 0:4, :].rearrange("p a c -> p (a c)"), PS[:, 6, :])
                dve.tensor_copy(Vo[:, 4:7, :].rearrange("p a c -> p (a c)"), PS[:, 7, 0:3 * P]).then_inc(vn_d, 1)
                g = hp - 1
                r0 = R_ROW + ROWS * g
                for t in range(LAST):
                    q = t - 4
                    if 0 <= q < ROWS and q % 4 == 3:
                        if q == 3:
                            place[0] = output_place(9 + hp)
                        dve.wait_ge(pv, r0 + q + 1)
                        for b in range(2):
                            ins = dve.tensor_copy(
                                place[0][64 * b:64 * b + 64, (q - 3) * GW:(q + 1) * GW].rearrange("p (a c) -> p a c", a=4),
                                PS[64 * b:64 * b + 64, 7, :].rearrange("p (a b c) -> p a b c", a=4, b=2)[:, :, b, ::-1])
                        ins.then_inc(o_ev, 1)
                        if q == ROWS - 1:
                            dve.wait_ge(o_ev, o_count(r0 + ROWS))
                            dve.engine_nop().then_inc(oc_rdy, 1)
                    if t < ROWS:
                        peak(r0 + t, False, t, g)
                    if 0 <= t - 1 < ROWS:
                        normalise(r0 + t - 1, False)
                    if hp < HP and 1 in units_done(t, PIECES, ROWS):
                        take_k(U_NAH + 3 * hp + 1)
            cat_split(1)
            post_in(2, 0)
            post_out(2, 0)
            post_in(2, 1)
            turn(7)
            post_out(2, 1)
            ffn(1)

        @block.tensor
        def _(pe):
            def three(dst, stat, mov, start, stop):
                pe.matmul(dst, stat[0], mov[0], start=start, stop=False)
                pe.matmul(dst, stat[0], mov[1], start=False, stop=False)
                return pe.matmul(dst, stat[1], mov[0], start=False, stop=stop)

            def wtile(n, k):
                c = slice(k * P, (k + 1) * P)
                return whi[:, n % RING, c], wlo[:, n % RING, c]

            def turn(t, free):
                if N_TURNS[t] == 4:
                    for s, v in free:
                        pe.wait_ge(s, v)
                if t:
                    pe.wait_ge(a_hi, 8 * t)
                    pe.wait_ge(a_lo, 8 * t)
                Yt = set_tiles(t)
                if N_TURNS[t] == KD:
                    pe.wait_ge(xs, tiles_before(t + 1))
                    for k in range(KD):
                        for s, v in free(k):
                            pe.wait_ge(s, v)
                        for i in range(TT):
                            ins = pe.transpose(PS[:, k, i * P:(i + 1) * P], Yt[:, i, k * P:(k + 1) * P], ident[:, :])
                        ins.then_inc(t_done, 1)
                    return
                for i in range(tiles_before(t + 1) - tiles_before(t)):
                    pe.wait_ge(xs, tiles_before(t) + i + 1)
                    for k in range(KD):
                        ins = pe.transpose(PS[:, k, i * P:(i + 1) * P], Yt[:, i, k * P:(k + 1) * P], ident[:, :])
                    ins.then_inc(t_done, 1)

            def turn_late(t):
                if t == 6:
                    pe.wait_ge(y_cp, 16)
                    pe.wait_ge(y_sq, 16)
                for part in range(2):
                    if part:
                        pe.wait_ge(a_lo, 8 * t + 4)
                    for i in range(TT):
                        if not part:
                            pe.wait_ge(xs, tiles_before(t) + i + 1)
                        for k in range(4):
                            f = (4 * part + k) * P
                            ins = pe.transpose(PS[:, 4 + k, i * P:(i + 1) * P], Y[:, i, f:f + P], ident[:, :])
                        if part:
                            ins.then_inc(t_done, 1)
                    if not part:
                        ins.then_inc(t_low, 1)

            def project(n, k, halves=(0, 1), sets=None):
                if k == 0 and 0 in halves:
                    pe.wait_ge(w_lo, n + 1)
                    if n - 2 in EV:
                        pe.wait_ge(*EV[n - 2])
                if sets is not None:
                    pe.wait_ge(a_lo, 8 * sets + max(k + 1, 2))
                for th in halves:
                    ins = three(PS[:, 2 * (n % 2) + th, :], wtile(n, k), (aT[:, th, 0, k, :], aT[:, th, 1, k, :]),
                                k == 0, k == KD - 1)
                if k == KD - 1 and 1 in halves:
                    ins.then_inc(w_used, 1)

            def first_two(n, t):
                if t == 6:
                    pe.wait_ge(y_cp, 14)
                    pe.wait_ge(y_sq, 14)
                for u in range(2):
                    for k in range(KD):
                        project(n + u, k, (0,), t - 1 if u == 0 else None)
                turn_late(t)
                for u in range(2):
                    for k in range(KD):
                        project(n + u, k, (1,), t if u == 0 else None)

            def gate_up(n, bank, need_w, last_set=None):
                pe.wait_ge(w_lo, need_w)
                for k in range(KD):
                    if last_set is not None:
                        pe.wait_ge(a_lo, 8 * last_set + max(k + 1, 2))
                    ins = three(PS[:, bank, :], wtile(n, k), (aT[:, 0, 0, k, :], aT[:, 0, 1, k, :]), k == 0, k == KD - 1)
                ins.then_inc(w_used, 1)

            def contract(n0, kn, source, ready, free):
                for k in range(kn):
                    n = n0 + k
                    pe.wait_ge(w_lo, n + 1)
                    pe.wait_ge(*ready(k))
                    for i in range(TT):
                        if k == 0:
                            for s, v in free(i):
                                pe.wait_ge(s, v)
                        c = slice(i * P, (i + 1) * P)
                        for fh in range(2):
                            f = slice(512 * fh, 512 * fh + 512)
                            ins = three(PS[:, 2 * i + fh, :], (source[:, 0, k, c], source[:, 1, k, c]),
                                        (whi[:, n % RING, f], wlo[:, n % RING, f]), k == 0, k == kn - 1)
                        if k == kn - 1:
                            ins.then_inc(y_done, 1)
                    if k < kn - 1:
                        ins.then_inc(w_used, 1)
                pe.wait_ge(y_done, Y_DONE[0] + TT)
                pe.sem_inc(w_used, 1)
                Y_DONE[0] += TT

            Y_DONE = [0]

            def ffn(l):
                for th in range(2):
                    n0 = U_FF[l] + 3 * KH * th
                    g0 = (2 * l + th) * KH
                    s = 1 + 2 * l
                    t = 4 * l + 3 + th

                    def tile(j):
                        n = n0 + 2 * j
                        if j >= 3:
                            pe.wait_ge(hid_t, g0 + j - 2)
                        elif th:
                            pe.wait_ge(y_cp, 8 * s + j + 1)
                            pe.wait_ge(y_sq, 8 * s + j + 1)
                        gate_up(n, 2 * (j % 3), n + 1, t if j == 0 else None)
                        gate_up(n + 1, 2 * (j % 3) + 1, n + 2)

                    for j in range(3):
                        tile(j)
                    with pe.Fori(0, 6) as i:
                        for c in range(3):
                            j = 3 + c
                            n = n0 + 2 * j
                            pe.wait_ge(hid_t, i * 3 + (g0 + j - 2))
                            gate_up(n, 2 * c, i * 6 + (n + 1))
                            gate_up(n + 1, 2 * c + 1, i * 6 + (n + 2))
                    tile(KH - 1)
                    if th == 0 or l == 0:
                        turn(t + 1, lambda k: [(hid_t, g0 + (KH, KH - 2, KH - 1)[k // 2])] if k < 6 else
                             [(y_cp, 8 * s + TT), (y_sq, 8 * s + TT)] if th else [])

                    def free(i):
                        if th == 0 or l == 0:
                            return [(a_lo, 8 * (t + 1) + 2 * i + 2)]
                        return [(hid_t, g0 + KH), (y_cp, 8 * s + TT), (y_sq, 8 * s + TT)]

                    contract(n0 + 2 * KH, KH, hid, lambda k: (hid_rdy, g0 + k + 1), free)

            def out_project(l):
                for th in range(2):
                    e0 = 16 * l + 4 * th

                    def free(i):
                        if th:
                            return [(y_cp, e0 - TT + i + 1), (y_sq, e0 - TT + i + 1)]
                        return [(oc_rdy, 8 * l + 8), (pt_ev, R_END[l]), (s_exp, R_END[l])]

                    contract(U_OUT[l] + KD * th, KD, catT[:, th, :, :, :],
                             lambda k: (cat_lo, 16 * l + 8 * th + k + 1), free)

            def scores(r, stat, mov):
                if r >= 2:
                    pe.wait_ge(s_add, r - 1)
                    pe.wait_ge(s_exp, r - 1)
                pe.matmul(PS[:, banks(r)[0], :], stat, mov, start=True, stop=True).then_inc(s_mm, 1)

            def turn_probs(r):
                pe.wait_ge(s_nrm, r + 1)
                if r:
                    pe.wait_ge(pt_ev, r)
                for c in range(4):
                    ins = pe.transpose(PS[:, banks(r)[1], c * P:(c + 1) * P], SB[:, r % 3, c * P:(c + 1) * P], ident[:, :])
                ins.then_inc(s_tr, 1)

            def mem_step(run, t, fill=()):
                r0, tiles, hp0 = run[:3]
                fill = list(fill)
                if t < tiles:
                    hp, i = hp0 + t // 8, t % 8
                    scores(r0 + t, MQ[:, hp, i * P:(i + 1) * P], bdK[:, hp, :])
                for n, k in fill[:2]:
                    project(n, k)
                if 0 <= t - 2 < tiles:
                    turn_probs(r0 + t - 2)
                for n, k in fill[2:]:
                    project(n, k)
                if 0 <= t - 3 < tiles:
                    r = r0 + t - 3
                    hp = hp0 + (t - 3) // 8
                    pe.wait_ge(pt_ev, r + 1)
                    if r:
                        pe.wait_ge(o_ev, o_count(r))
                    for kc in range(2):
                        ins = pe.matmul(
                            PS[:, banks(r)[2], 0:256].rearrange("p (g c) -> p g c", g=2),
                            memV[:, kc, P * hp:P * hp + P],
                            PT[:, r % 2, :].rearrange("p (g k c) -> p g k c", g=2, k=2)[:, :, kc, :],
                            start=(kc == 0), stop=(kc == 1))
                    ins.then_inc(pv, 1)

            pe.wait_ge(c_ids, 32)
            turn(0, [])
            for n in range(4):
                pe.wait_ge(w_lo, n + 1)
                if n >= 2:
                    pe.wait_ge(*EV[n - 2])
                for k in range(KD):
                    if n == 0:
                        pe.wait_ge(a_lo, 8)
                    ins = three(PS[:, 2 * (n % 2), 0:MEM], wtile(n, k), (aT[:, 0, 0, k, 0:MEM], aT[:, 0, 1, k, 0:MEM]),
                                k == 0, k == KD - 1)
                ins.then_inc(w_used, 1)
            pe.wait_ge(*EV[3])
            for hp in range(2):
                for kc in range(2):
                    c = (2 * hp + kc) * P
                    ins = pe.transpose(PS[:, 4, c:c + P], mvT[:, hp, kc * P:(kc + 1) * P], ident[:, :])
            ins.then_inc(mvt, 1)
            turn(1, [EV[1], (memv_rdy, 1)])
            first_two(U_RET, 2)
            pe.wait_ge(*EV[U_RET + 1])
            pe.wait_ge(a_lo, 24)
            for t in range(steps(RUN_A0)):
                mem_step(RUN_A0, t, [(U_RETH + p // KD, p % KD) for p in pieces_at(t, 4 * KD, steps(RUN_A0))])

            def unit(n):
                for k in range(KD):
                    project(n, k)

            def chunk_scores(h):
                n = U_RETH + 4 * h
                pe.wait_ge(*EV[n - 3])
                if h >= 2:
                    pe.wait_ge(oc_rdy, h)
                else:
                    pe.wait_ge(s_exp, 8)
                    pe.wait_ge(pt_ev, 8)
                    pe.wait_ge(o_ev, 8)
                for c in range(8):
                    ins = pe.transpose(PS[:, 4 + c // 4, (c % 4) * P:(c % 4 + 1) * P], kT[:, c * P:(c + 1) * P], ident[:, :])
                ins.then_inc(ktr, 1)
                pe.wait_ge(*EV[n - 2])
                if h >= 2:
                    pe.wait_ge(yn_rdy, h - 1)
                for c in range(8):
                    ins = pe.transpose(PS[:, 6 + c // 4, (c % 4) * P:(c % 4 + 1) * P], vT[:, c * P:(c + 1) * P], ident[:, :])
                ins.then_inc(vtr, 1)
                pe.wait_ge(ktok_rdy, h)
                for c in range(8):
                    cc = slice(c * P, (c + 1) * P)
                    ins = pe.matmul(PS[:, 4 + c // 4, (c % 4) * P:(c % 4 + 1) * P], kT[:, cc], qT[:, (h - 1) % 2, cc],
                                    start=True, stop=True)
                ins.then_inc(st_mm, 1)

            def chunk_states(h):
                pe.wait_ge(vfb_rdy, h)
                pe.wait_ge(v_rdy, h)
                for c in range(8):
                    if c == 4:
                        pe.wait_ge(st_rdy, h)
                    bank = (6, 7, 4, 5)[c // 2]
                    ins = pe.matmul(PS[:, bank, 256 * (c % 2):256 * (c % 2) + 256], Ktok[:, c, :],
                                    vfb[:, c, :, :].rearrange("p a c -> p (a c)"), start=True, stop=True)
                ins.then_inc(kv_mm, 1)

            def chunk_outputs(h):
                pe.wait_ge(scan_rdy, h)
                pe.wait_ge(qfb_rdy, h)
                for c in range(8):
                    dst = PS[:, 6 + c // 4, (c % 4) * P:(c % 4 + 1) * P]
                    cc = slice(c * P, (c + 1) * P)
                    pe.matmul(dst, ST[:, c, :], V[:, c, :], start=True, stop=False)
                    pe.matmul(dst, qfb[:, 0, cc], states[:, c, 0, :], start=False, stop=False)
                    ins = pe.matmul(dst, qfb[:, 1, cc], states[:, c, 1, :], start=False, stop=True)
                ins.then_inc(out_mm, 1)

            def turn_outputs(h):
                pe.wait_ge(yn_rdy, h)
                for c in range(8):
                    ins = pe.transpose(PS[:, 4 + c // 4, (c % 4) * P:(c % 4 + 1) * P], ST[:, c, :], ident[:, :])
                ins.then_inc(y_tr, 1)

            for h in range(1, RH):
                n = U_RETH + 4 * h
                unit(n)
                chunk_scores(h)
                unit(n + 1)
                chunk_states(h)
                unit(n + 2)
                chunk_outputs(h)
                unit(n + 3)
                turn_outputs(h)
            chunk_scores(RH)
            for u in range(1, 4):
                pe.wait_ge(*EV[U_OUT0 - u])
            for t in range(3):
                mem_step(RUN_B0, t)
            chunk_states(RH)
            for t in range(3, 6):
                mem_step(RUN_B0, t)
            chunk_outputs(RH)
            for t in range(6, 9):
                mem_step(RUN_B0, t)
            turn_outputs(RH)
            for t in range(9, steps(RUN_B0)):
                mem_step(RUN_B0, t)
            out_project(0)
            turn(3, lambda k: [(y_cp, 5 + k // 2), (y_sq, 5 + k // 2)])
            ffn(0)
            first_two(U_NA, 6)
            pe.wait_ge(*EV[U_NA + 1])
            pe.wait_ge(a_lo, 56)
            pe.wait_ge(mkv_ld, 32)
            for t in range(steps(RUN_A1)):
                mem_step(RUN_A1, t, [(U_NAH + p // KD, p % KD) for p in pieces_at(t, PIECES, steps(RUN_A1))])
            for hp in range(1, HP + 1):
                n = U_NAH + 3 * hp
                g = hp - 1
                r0 = R_ROW + ROWS * g
                pe.wait_ge(*EV[n - 1])
                pe.wait_ge(s_exp, r0)
                pe.wait_ge(s_add, r0)
                for m in range(8):
                    ins = pe.transpose(PS[:, 4 + m // 4, (m % 4) * P:(m % 4 + 1) * P], vTn[:, m * P:(m + 1) * P], ident[:, :])
                ins.then_inc(vn_tr, 1)
                pe.wait_ge(pt_ev, r0)
                pe.wait_ge(o_ev, o_count(r0))
                for m in range(7):
                    ins = pe.transpose(PS[:, 6 + m // 4, (m % 4) * P:(m % 4 + 1) * P], vTn[:, m * P + GW:(m + 1) * P + GW], ident[:, :])
                ins.then_inc(vn_tr, 1)
                pe.wait_ge(vn_a, hp)
                pe.wait_ge(*EV[n - 3])
                pe.wait_ge(*EV[n - 2])
                for t in range(LAST):
                    if t < ROWS:
                        kr = key_row(t)
                        scores(r0 + t, qbd[:, g % 2, t, :, :].rearrange("p a c -> p (a c)"),
                               kTn[:, g % 2, kr * GW:kr * GW + 512])
                    for piece in pieces_at(t):
                        if hp < HP:
                            project(n + piece // KD, piece % KD)
                    if 0 <= t - 2 < ROWS:
                        if t == 2:
                            pe.wait_ge(vn_d, hp)
                        turn_probs(r0 + t - 2)
                    q = t - 3
                    if 0 <= q < ROWS:
                        r = r0 + q
                        pe.wait_ge(pt_ev, r + 1)
                        if q % 4 == 0:
                            pe.wait_ge(o_ev, o_count(r))
                        kr = key_row(q)
                        for c in range(4):
                            vt = Vo[:, (kr - 1) // 2 + c, :] if kr % 2 else Ve[:, kr // 2 + c, :]
                            ins = pe.matmul(PS[:, 7, (q % 4) * P:(q % 4 + 1) * P], vt, PT[:, r % 2, c * P:(c + 1) * P],
                                            start=(c == 0), stop=(c == 3))
                        ins.then_inc(pv, 1)
            out_project(1)
            turn(7, lambda k: [(y_cp, 21 + k // 2), (y_sq, 21 + k // 2)])
            ffn(1)


def constants():
    half = P // 2
    inv = (np.float32(10000.0) ** (-np.arange(half, dtype=np.float32) / np.float32(half))).astype(np.float32)
    ang = (np.arange(SEQ, dtype=np.float32)[None, :] * inv[:, None]).astype(np.float32)
    c, s = np.cos(ang), np.sin(ang)
    ropes = np.stack([np.concatenate([c, c]), np.concatenate([s, -s])]).astype(np.float32)
    i = np.arange(P, dtype=np.float32)
    rel = i[None, :] - i[:, None]
    scale = np.float32(float(P) ** -0.5)
    rows = [np.maximum(rel, 0), np.maximum(-rel, 0), (rel >= 0) * scale, (rel <= 0) * scale,
            np.broadcast_to(i[None, :] + 1, (P, P)), np.broadcast_to(P - i[None, :], (P, P)),
            np.stack([P - 1 - i, i] + [0 * i] * 6, axis=1)]
    decay_consts = np.concatenate(rows, axis=1).astype(np.float32)
    q = np.arange(GW)[::-1, None]
    k = np.arange(GW)[None, :]
    start = np.clip(q - WC // 2, 0, GW - WC)
    inside = (k >= start) & (k < start + WC)
    m = np.stack([inside.astype(np.float32), np.where(inside, 0, -1e30).astype(np.float32)], axis=1)
    return ropes, decay_consts, np.concatenate([m, m]), np.eye(P, dtype=np.float32)


def kernel(x, mem, norm_g, mem_norm_g, mem_w_kv, ret_w_in, ret_w_out, ret_gn_g, ret_gn_b, ret_decay,
           na_w_in, na_w_out, na_rpb, ffn_w_in, ffn_w_out):
    import concourse.bacc as bacc
    from concourse.bass_utils import run_bass_kernel_spmd

    a = {k: np.asarray(v) for k, v in locals().items() if k not in ("bacc", "run_bass_kernel_spmd")}

    def tiles(w, *groups):
        g = len(groups)
        w = w.reshape((KD, P) + groups + (P,))
        return w.transpose(tuple(range(2 + g - 1, 1, -1)) + (1, 0, 2 + g)).reshape(-1, P, UW)

    def rows(w, order):
        return w.reshape(KD, P, D)[order]

    tok = RH * P
    ret, na = a["ret_w_in"][0], a["na_w_in"][0]
    wpack = np.concatenate([
        tiles(a["mem_w_kv"], 4),
        tiles(ret[:, 4 * tok:], 2), tiles(ret[:, :4 * tok], 4, RH), rows(a["ret_w_out"][0], [6, 0, 1, 2, 3, 4, 5, 7]),
        tiles(a["ffn_w_in"][0], 2, KH), a["ffn_w_out"][0].reshape(KH, P, D),
        tiles(na[:, 3 * tok:], 2), tiles(na[:, :3 * tok], 3, HP), rows(a["na_w_out"][0], [6, 7, 0, 1, 2, 3, 4, 5]),
        tiles(a["ffn_w_in"][1], 2, KH), a["ffn_w_out"][1].reshape(KH, P, D)])
    g = a["norm_g"]
    pre = np.stack([g[0, 0], g[0, 2], g[1, 0], g[1, 2], a["mem_norm_g"]])
    ropes, decay_consts, na_masks, ident = constants()
    arrays = {
        "wpack": wpack, "x": a["x"][0], "mem": a["mem"][0],
        "gains": pre.reshape(5, KD, P).transpose(2, 0, 1),
        "gain_rows": np.stack([g[0, 1], g[0, 3], g[1, 1], g[1, 3]]),
        "gn": np.stack([a["ret_gn_g"][0], a["ret_gn_b"][0]]).reshape(2, RH, P).transpose(2, 0, 1),
        "decay": a["ret_decay"].reshape(1, 2 * RH), "rpb": a["na_rpb"].reshape(-1),
        "ropes": ropes, "decay_consts": decay_consts, "na_masks": na_masks, "ident_c": ident}
    nc = bacc.Bacc("TRN2", target_bir_lowering=False, num_devices=1)
    arrays = {f"in_{k}": np.ascontiguousarray(v) for k, v in arrays.items()}
    args = [nc.dram_tensor(k, v.shape, mybir.dt.from_np(v.dtype), kind="ExternalInput").ap() for k, v in arrays.items()]
    out = nc.dram_tensor("out_h", (SEQ, D), mybir.dt.float32, kind="ExternalOutput").ap()
    trunk_program(nc, *args, out)
    r = run_bass_kernel_spmd(nc, [arrays], core_ids=[0])
    return r.results[0]["out_h"].reshape(1, SEQ, D)
```

```python
import numpy as np
from contextlib import ExitStack
import concourse.bass as bass
from concourse import mybir

P = 128
D = 1024
KD = D // P
SEQ = 1024
HALF = SEQ // 2
TT = HALF // P
MEM = 256
RH = 6
HP = 6
ROWS, GW = 16, 64
WR, WC = 8, 16
HID = 2816
KH = HID // P
RING = 3
UW = 1024
QC, KC, KR = 32, 40, 9
OFFS = 2 * WR - 2
BIASW = KC + 8
V_ROWS = (0, 3, 6, 2, 5, 8, 4, 7, 10, 9, 12, 11, 14)
RPB_PAD = 64

U_MEM = 0
U_RET = U_MEM + 4
U_RETH = U_RET + 2
U_OUT0 = U_RETH + 4 * RH
U_FF0 = U_OUT0 + 2 * KD
U_NA = U_FF0 + 2 * (3 * KH)
U_NAH = U_NA + 2
U_OUT1 = U_NAH + 3 * HP
U_FF1 = U_OUT1 + 2 * KD
U_END = U_FF1 + 2 * (3 * KH)
N_T = 34
N_E = 32


def unit_rows():
    rows, at = [], 0
    for count, times, phase in ((4, 1, "mem"), (4 * RH + 2, 1, "ret"), (KD, 2, "out"), (3 * KH, 2, "ffn"),
                                (3 * HP + 2, 1, "na"), (KD, 2, "out"), (3 * KH, 2, "ffn")):
        for _ in range(times):
            rows += list(range(at, at + count))
        at += count
    return rows


def trunk_program(nc, wpack, x, mem, gains, gain_rows, gn, decay, rpb, ropes, decay_consts, na_masks, ident_c, out):
    F32, F32R, BF16 = mybir.dt.float32, mybir.dt.float32r, mybir.dt.bfloat16
    ACT = mybir.ActivationFunctionType
    ALU = mybir.AluOpType
    AX = mybir.AxisListType
    ROW = unit_rows()
    assert len(ROW) == U_END

    h_dram = nc.dram_tensor("h_scratch", [SEQ, D], F32).ap()
    cat_dram = nc.dram_tensor("cat_scratch", [2, KD, P, SEQ], F32).ap()
    memkv_dram = nc.dram_tensor("memkv_scratch", [P, 1536], F32).ap()
    rpb_n = 12 * 15 * 31
    rpb_dram = nc.dram_tensor("rpb_scratch", [RPB_PAD + rpb_n + RPB_PAD], F32)

    KB = 1024
    base = (nc.sbuf_base + 31) // 32 * 32

    def at(name, shape, dt, off):
        return nc.alloc_sbuf_tensor_at(name, shape, dt, offset=base + off)

    stage = at("stage", [P, RING, UW], F32, 0)
    whi = at("whi", [P, RING, UW], F32R, 12 * KB)
    wlo = at("wlo", [P, RING, UW], F32R, 24 * KB)
    SM = 36 * KB
    ident = at("ident", [P, P], F32, SM)
    sumsq = at("sumsq", [P, 72], F32, SM + 512)
    msq = at("msq", [P, 72], F32, SM + 800)
    rstd = at("rstd", [P, 72], F32, SM + 1088)
    gT = at("gT", [P, 5, KD], F32, SM + 1376)
    gnT = at("gnT", [P, 2, RH], F32, SM + 1536)
    lgb = at("lgb", [P, 12], F32, SM + 1600)
    lg = at("lg", [P, 2, RH], F32, SM + 1664)
    kdec = at("kdec", [P, 2, RH], F32, SM + 1728)
    cdec = at("cdec", [P, 2, RH], F32, SM + 1792)
    negmax = at("negmax", [P, 4, 2], F32, SM + 1920)
    rowsum = at("rowsum", [P, 4, 2], F32, SM + 1952)
    rowinv = at("rowinv", [P, 4, 2], F32, SM + 1984)
    stats = at("stats", [P, 8, 6], F32, SM + 2048)
    mv = at("mv", [P, 8, 2], F32, SM + 2240)
    gvar = at("gvar", [P, 8], F32, SM + 2304)
    grstd = at("grstd", [P, 8], F32, SM + 2336)
    minus_half = at("minus_half", [P, 8], F32, SM + 2368)
    maxraw = at("maxraw", [P, 4, 2], F32, SM + 2400)
    colc = at("colc", [P, 8], F32, SM + 2528)
    kprod = at("kprod", [P, 2, RH], F32, SM + 2432)
    Z = SM + 3 * KB
    Y = at("Y", [P, TT, D], F32, Z)
    vfb = at("vfb", [P, 8, 2, P], F32, Z)
    qfb = at("qfb", [P, 2, SEQ], F32, Z)
    kTn = at("kTn", [P, 2, SEQ], F32, Z)
    OC = at("OC", [P, 2, SEQ], F32, Z + 8 * KB)
    Hb = at("Hb", [P, TT, D], F32, Z + 16 * KB)
    gB = at("gB", [P, D], F32, Z + 32 * KB)
    junk = [at("junk0", [P, D], BF16, Z + 36 * KB), at("junk1", [P, D], BF16, Z + 166 * KB)]
    X = Z + 38 * KB
    aT = at("aT", [P, 2, 2, KD, HALF], F32R, X)
    catf = at("catf", [P, KD, SEQ], F32, X)
    catT = at("catT", [P, 2, 2, KD, HALF], F32R, X + 32 * KB)
    hid = at("hid", [P, 2, KH, HALF], F32R, X + 32 * KB)
    sg = at("sg", [P, RING, HALF], F32, X + 120 * KB)
    hidf = at("hidf", [P, HALF], F32, X + 126 * KB)
    Yb = at("Yb", [P, TT, D], F32, X + 96 * KB)
    W = X + 64 * KB
    W += 6 * KB
    bdK = at("bdK", [P, 2, 2 * MEM], F32, W + 53 * KB)
    memV = at("memV", [P, 2, 2 * P], F32, W + 57 * KB)
    MQ = at("MQ", [P, 2, SEQ], F32, Z + 16 * KB)
    SB = at("SB", [P, 3, 512], F32, Z + 24 * KB)
    PT = at("PT", [P, 2, 512], F32, Z + 32 * KB)
    ropeC = at("ropeC", [P, SEQ], F32, W)
    ropeS = at("ropeS", [P, SEQ], F32, W + 4 * KB)
    QD = at("QD", [P, 2, RH, P], F32, W + 8 * KB)
    DM = at("DM", [P, RH, P], F32, W + 14 * KB)
    qT = at("qT", [P, 2, SEQ], F32, W + 17 * KB)
    kT = at("kT", [P, SEQ], F32, W + 25 * KB)
    Ktok = at("Ktok", [P, 8, P], F32, W + 29 * KB)
    V = at("V", [P, 8, P], F32, W + 33 * KB)
    ST = at("ST", [P, 8, P], F32, W + 37 * KB)
    vT = at("vT", [P, SEQ], F32, W + 41 * KB)
    states = at("states", [P, 8, 2, P], F32, W + 45 * KB)
    rtmp = at("rtmp", [P, HALF], F32, Z + 36 * KB)
    dconst = at("dconst", [P, 6, P], F32, Z)
    dexp = at("dexp", [P, 2, P], F32, Z + 3 * KB)
    mvT = at("mvT", [P, 2, MEM], F32, W + 17 * KB)
    qbd = at("qbd", [P, 2, ROWS, 2, 2 * QC], F32, W)
    TB = at("TB", [P, 2, 2, OFFS, KC], F32, W + 16 * KB)
    nmask = at("nmask", [P, 2 * 2 * KC + KR], F32, W + 25 * KB)
    vTn = at("vTn", [P, 2, ROWS * KC], F32, W + 25 * KB + 768)
    TI = at("TI", [P, 2, 2, KR, KC], F32, W + 30 * KB + 768)
    Vc = at("Vc", [P, 2 * len(V_ROWS), P], F32, W + 36 * KB + 512)
    TR = at("TR", [P, OFFS, BIASW], F32, W + 49 * KB + 512)

    with ExitStack() as ctx:
        PS = ctx.enter_context(nc.psum_tensor("PS", [P, 8, 512], F32))

        def sem(name):
            return ctx.enter_context(nc.semaphore(name))

        w_in = [sem(f"w_in{r}") for r in range(RING)]
        w_hi, w_lo, w_used = sem("w_hi"), sem("w_lo"), sem("w_used")
        c_ld = sem("c_ld")
        c_ids = sem("c_ids")
        x_ld = [sem(f"x_ld{i}") for i in range(10)]
        h_ld = [sem(f"h_ld{i}") for i in range(TT)]
        h_st = [sem(f"h_st{i}") for i in range(TT)]
        g_ld, pre_sq, pre_rs, xs = sem("g_ld"), sem("pre_sq"), sem("pre_rs"), sem("xs")
        t_done, t_low, a_hi, a_lo = sem("t_done"), sem("t_low"), sem("a_hi"), sem("a_lo")
        y_done, y_cp, y_sq, post_rs, h_new = sem("y_done"), sem("y_cp"), sem("y_sq"), sem("post_rs"), sem("h_new")
        g_act, hid_t, hid_rdy = sem("g_act"), sem("hid_t"), sem("hid_rdy")
        ev_act, ev_dve = sem("ev_act"), sem("ev_dve")
        oc_st = [sem(f"oc_st{i}") for i in range(2)]
        cat_ld = [sem(f"cat_ld{k}") for k in range(KD)]
        cat_hi, cat_lo = sem("cat_hi"), sem("cat_lo")
        dec_e, dec_rdy, mh_rdy, zer = sem("dec_e"), sem("dec_rdy"), sem("mh_rdy"), sem("zer")
        mvt, memv_rdy, mkv_st, mkv_ld = sem("mvt"), sem("memv_rdy"), sem("mkv_st"), sem("mkv_ld")
        ktr, vtr, st_mm, kv_mm, out_mm, y_tr = (sem(n) for n in ("ktr", "vtr", "st_mm", "kv_mm", "out_mm", "y_tr"))
        ktok_rdy, vfb_rdy, v_rdy, st_rdy, scan_rdy, qfb_rdy = (
            sem(n) for n in ("ktok_rdy", "vfb_rdy", "v_rdy", "st_rdy", "scan_rdy", "qfb_rdy"))
        var_rdy, grs_rdy, yn_rdy, aff, oc_rdy = (sem(n) for n in ("var_rdy", "grs_rdy", "yn_rdy", "aff", "oc_rdy"))
        s_mm, s_add, s_exp, s_nrm, s_tr, pt_ev, pv, o_ev = (
            sem(n) for n in ("s_mm", "s_add", "s_exp", "s_nrm", "s_tr", "pt_ev", "pv", "o_ev"))
        vn_tr, vn_a, vn_d = sem("vn_tr"), sem("vn_a"), sem("vn_d")
        rpb_st, tb_ld, tb_rdy, nmask_ld, qz = (
            sem("rpb_st"), sem("tb_ld"), sem("tb_rdy"), sem("nmask_ld"), sem("qz"))
        d_own, p_own = sem("d_own"), sem("p_own")

        EV = {}
        counts = {"a": 0, "d": 0}

        def taken_by(n, who):
            counts[who] += 1
            EV[n] = (ev_act if who == "a" else ev_dve, counts[who])

        for n in range(4):
            taken_by(n, "ddaa"[n])
        for n in range(2):
            taken_by(U_RET + n, "a")
        for n in range(4 * RH):
            taken_by(U_RETH + n, "ddaa"[n % 4])
        for n in range(2):
            taken_by(U_NA + n, "a")
        for n in range(3 * HP):
            taken_by(U_NAH + n, "ada"[n % 3])

        def tiles_before(t):
            return 0 if t == 0 else 2 + 4 * (t - 1)

        N_TURNS = [2, KD, 4, KD, KD, KD, 4, KD, KD]

        def turned(t):
            return sum(N_TURNS[:t + 1])

        def set_of(s, th):
            return 2 * s + 1 + th

        def y_tiles(s, th):
            return Yb if s in (0, 2) and th == 0 else Y

        def set_tiles(t):
            return Hb if t == 0 else Yb if t in (1, 3, 7) else Y

        def pre_tile(xi):
            return Hb[:, xi, :] if xi < 2 else Yb[:, xi - 2, :] if xi < 6 else Y[:, xi - 6, :]

        GAIN = [4, 0, 0, 1, 1, 2, 2, 3, 3]
        U_FF = [U_FF0, U_FF1]
        U_OUT = [U_OUT0, U_OUT1]
        U_IN = [U_RET, U_NA]
        N_IN = [4 * RH + 2, 3 * HP + 2]
        R_ROW = 32
        R_END = [16, R_ROW + HP * ROWS]
        RUN_A0 = (0, 8, 0, 0)
        RUN_B0 = (8, 8, 1, 7)
        RUN_A1 = (16, 16, 0, 8)

        def o_count(r):
            return r if r <= R_ROW else R_ROW + (r - R_ROW) // 4

        DIRECT = (6, 7, 15)

        def stored(c):
            return 16 * len([b for b in range(c % 2, c + 1, 2) if b not in DIRECT])

        def banks(r):
            return (r % 2, 2, 3) if RUN_B0[0] <= r < R_END[0] else (4 + r % 2, 6, 7)

        def window(t):
            j = t // 2
            edge = j < WR // 4 or j >= (ROWS - WR // 2) // 2
            first = min(max(2 * j - WR // 2, 0), ROWS - WR)
            return first, WR if edge else KR, 2 * j, t % 2

        def chunks(t):
            first, n, _, w = window(t)
            return [(2 * V_ROWS.index(first + r) + w, KC * min(3, n - r)) for r in range(0, n, 3)]

        PIECES = 3 * KD
        AHEAD, EARLY = 3, 5

        def pieces_at(t, total, steps, early=0):
            left = total - early
            return range(early + left * t // steps, early + left * (t + 1) // steps) if t < steps else range(0)

        def units_done(t, total, steps, early=0):
            return [u for u in range(total // KD) if KD * u + KD - 1 in pieces_at(t, total, steps, early)]

        def steps(run):
            return run[1] + 3
        LAST = ROWS + 4

        block = ctx.enter_context(nc.Block())

        @block.sync
        def _(sp):
            issued = [0]

            def load_units(upto):
                for n in range(issued[0], min(upto, U_END)):
                    if n >= RING:
                        sp.wait_ge(w_lo, n - RING + 1)
                    sp.dma_start(stage[:, n % RING, :], wpack[ROW[n], :, :]).then_inc(w_in[n % RING], 16)
                issued[0] = max(issued[0], min(upto, U_END))

            def load_pre(xi):
                src = mem[xi * P:(xi + 1) * P, :] if xi < 2 else x[(xi - 2) * P:(xi - 1) * P, :]
                sp.dma_start(pre_tile(xi), src).then_inc(x_ld[xi], 16)

            def load_h(e):
                s, t = e // 8, e % 8
                if e >= TT:
                    sp.wait_ge(h_st[e % TT], 16 * (e // TT))
                if e >= TT and e - TT < 24:
                    sp.wait_ge(xs, 10 + e - TT + 1)
                src = x if s == 0 else h_dram
                sp.dma_start(Hb[:, e % TT, :], src[t * P:(t + 1) * P, :]).then_inc(h_ld[e % TT], 16)

            def store_h(e):
                t = e % 8
                sp.wait_ge(h_new, e + 1)
                dst = h_dram if e < 24 else out
                sp.dma_start(dst[t * P:(t + 1) * P, :], Hb[:, e % TT, :]).then_inc(h_st[e % TT], 16)

            def load_gain(s):
                if s:
                    sp.wait_ge(h_new, 8 * s)
                sp.dma_start(gB[:, :], gain_rows[s:s + 1, :].partition_broadcast(P)).then_inc(g_ld, 16)

            def post(s, th, nxt=None):
                for i in range(TT):
                    if nxt is not None and i == 2:
                        load_units(nxt + 6)
                    store_h(8 * s + 4 * th + i)
                if nxt is not None:
                    load_units(nxt + 7)
                if (s, th) != (1, 1):
                    for i in range(TT):
                        if nxt is not None and i == 2:
                            load_units(nxt + 8)
                        if 8 * s + 4 * th + i + TT < N_E:
                            load_h(8 * s + 4 * th + i + TT)
                    if th and s < 3:
                        load_gain(s + 1)

            def before_out(l):
                sp.wait_ge(oc_rdy, 8 * l + 8)
                for i in range(TT):
                    load_h(16 * l + i)
                load_gain(2 * l)

            def store_cat(c):
                sp.wait_ge(oc_rdy, c + 1)
                sp.dma_start(cat_dram[c // 8, c % 8, :, :], OC[:, c % 2, :]).then_inc(oc_st[c % 2], 16)

            def cat_back(l, tiles):
                sp.wait_ge(w_used, U_IN[l] + N_IN[l])
                for k in tiles:
                    sp.wait_ge(oc_st[k % 2], stored(8 * l + k))
                    sp.dma_start(catf[:, k, :], cat_dram[l, k, :, :]).then_inc(cat_ld[k], 16)

            def ffn(l):
                for th in range(2):
                    n0 = U_FF[l] + 3 * KH * th
                    for j in range(3):
                        load_units(n0 + 2 * j + 7)
                    with sp.Fori(0, 6) as i:
                        for c in range(6):
                            m = n0 + 6 + c + 5
                            sp.wait_ge(w_lo, i * 6 + (m - RING + 1))
                            sp.dma_start(stage[:, m % RING, :], wpack[bass.ds(i * 6 + (ROW[n0] + m - n0), 1), :, :]
                                         .rearrange("a p c -> p (a c)")).then_inc(w_in[m % RING], 16)
                    issued[0] += 36
                    load_units(n0 + 3 * KH + 5)
                    post(1 + 2 * l, th, n0 + 3 * KH if th == 0 else None)

            load_pre(0)
            load_pre(1)
            sp.dma_start(ident[:, :], ident_c).then_inc(c_ids, 16)
            sp.dma_start(gT[:, :, :], gains).then_inc(c_ids, 16)
            load_pre(2)
            load_pre(3)
            load_units(1)
            load_pre(4)
            load_pre(5)
            load_units(2)
            for xi in range(6, 10):
                load_pre(xi)
            load_units(5)
            sp.dma_start(colc[:, :], decay_consts[:, 6 * P:6 * P + 8]).then_inc(c_ld, 16)
            sp.dma_start(lgb[:, :], decay.partition_broadcast(P)).then_inc(c_ld, 16)
            sp.dma_start(gnT[:, :, :], gn).then_inc(c_ld, 16)
            sp.dma_start(ropeC[:, :], ropes[0, :, :]).then_inc(c_ld, 16)
            sp.dma_start(ropeS[:, :], ropes[1, :, :]).then_inc(c_ld, 16)
            sp.dma_start(rpb_dram[RPB_PAD:RPB_PAD + rpb_n], rpb).then_inc(rpb_st, 16)
            sp.wait_ge(zer, 2)
            for first in (0, RPB_PAD + rpb_n):
                sp.dma_start(bass.AP(rpb_dram, first, [[8, 8], [1, 8]]),
                             kprod[0:8, :, :].rearrange("p a c -> p (a c)")[:, 0:8]).then_inc(rpb_st, 16)
            load_units(U_RET + 5)
            sp.wait_ge(memv_rdy, 1)
            sp.wait_ge(ev_dve, 2)
            sp.dma_start(memkv_dram[:, 0:1024], bdK[:, :, :].rearrange("p a c -> p (a c)")).then_inc(mkv_st, 16)
            sp.dma_start(memkv_dram[:, 1024:1536], memV[:, :, :].rearrange("p a c -> p (a c)")).then_inc(mkv_st, 16)
            sp.wait_ge(t_done, turned(2))
            sp.dma_start(dconst[:, :, :], decay_consts[:, 0:6 * P].rearrange("p (a c) -> p a c", a=6)).then_inc(c_ld, 16)
            load_units(U_RETH + 4 + 5)
            store_cat(0)
            for h in range(1, RH):
                load_units(U_RETH + 4 * h + 4 + 5)
                store_cat(h)
            load_units(U_OUT0 + 5)
            cat_back(0, range(RH))
            before_out(0)
            for th in range(2):
                load_units(U_OUT0 + KD * (th + 1) + 5)
                post(0, th, U_OUT0 + KD * (th + 1))
            ffn(0)

            def load_bias(hp):
                if hp:
                    sp.wait_ge(tb_rdy, hp)
                for g in range(2):
                    for p in range(2):
                        first = RPB_PAD + (2 * hp + g) * 465 + 31 * (1 - p) - 24
                        src = bass.AP(rpb_dram, first, [[1, QC], [31, OFFS], [1, BIASW]])
                        at_p = 2 * QC * g + QC * p
                        sp.dma_start(TR[at_p:at_p + QC, :, :], src).then_inc(tb_ld, 16)

            sp.wait_ge(w_used, U_NA)
            sp.wait_ge(mkv_st, 32)
            sp.wait_ge(pre_sq, 26)
            sp.dma_start(bdK[:, :, :].rearrange("p a c -> p (a c)"), memkv_dram[:, 0:1024]).then_inc(mkv_ld, 16)
            sp.dma_start(memV[:, :, :].rearrange("p a c -> p (a c)"), memkv_dram[:, 1024:1536]).then_inc(mkv_ld, 16)
            sp.dma_start(nmask[:, :], na_masks).then_inc(nmask_ld, 16)
            sp.wait_ge(rpb_st, 48)
            load_bias(0)
            load_bias(1)
            load_units(U_NAH + 3 + 5)
            store_cat(8)
            store_cat(9)
            for hp in range(1, HP):
                load_units(U_NAH + 3 * hp + 3 + 5)
                if hp + 1 < HP:
                    load_bias(hp + 1)
                store_cat(9 + hp)
            load_units(U_OUT1 + 5)
            cat_back(1, range(KD - 1))
            before_out(1)
            for th in range(2):
                load_units(U_OUT1 + KD * (th + 1) + 5)
                post(2, th, U_OUT1 + KD * (th + 1))
            ffn(1)
            for i in range(TT):
                sp.wait_ge(h_st[i], 16 * (N_E // TT))

        @block.gpsimd
        def _(pool):
            done = [0]
            own = [0]

            def link(ins):
                own[0] += 1
                ins.then_inc(p_own, 1)
                pool.wait_ge(p_own, own[0])

            def split_lo(n, slot, need):
                pool.wait_ge(w_hi, need)
                pool.tensor_tensor(wlo[:, slot, :], stage[:, slot, :], whi[:, slot, :].bitcast(F32), ALU.subtract)\
                    .then_inc(w_lo, 1)

            def los(upto):
                for n in range(done[0], min(upto, U_END)):
                    split_lo(n, n % RING, n + 1)
                done[0] = max(done[0], min(upto, U_END))

            def inv_rms(col, ready, need, signal):
                pool.wait_ge(ready, need)
                link(pool.tensor_scalar(msq[:, col:col + 1], sumsq[:, col:col + 1], 1.0 / D, 1e-6, ALU.mult, ALU.add))
                pool.tensor_tensor(rstd[:, col:col + 1], msq[:, col:col + 1], minus_half[:, 0:1], ALU.pow)\
                    .then_inc(signal, 1)

            def pre(xi):
                inv_rms(xi, pre_sq, xi + 1, pre_rs)

            def post(s, th, upto=None):
                for i in range(TT):
                    e = 8 * s + 4 * th + i
                    inv_rms(N_T + e, y_sq, e + 1, post_rs)
                for i in range(TT):
                    if upto is not None and i % 2 == 0:
                        los(upto - 1 + i // 2)
                    if s < 3:
                        pre(10 + 8 * s + 4 * th + i)

            def ffn(l):
                for th in range(2):
                    n0 = U_FF[l] + 3 * KH * th
                    for j in range(3):
                        los(n0 + 2 * j + 4)
                    with pool.Fori(0, 6) as i:
                        for c in range(6):
                            m = n0 + 6 + c + 2
                            split_lo(m, m % RING, i * 6 + (m + 1))
                    done[0] += 36
                    los(n0 + 3 * KH + 2)
                    post(1 + 2 * l, th, n0 + 3 * KH + 5 if th == 0 else None)

            pool.memset(minus_half[:, :], -0.5).then_inc(mh_rdy, 1)
            pool.wait_ge(mh_rdy, 1)
            pre(0)
            pre(1)
            pool.memset(bdK[:, :, :], 0.0).then_inc(zer, 1)
            pool.memset(kprod[:, :, :], 0.0).then_inc(zer, 1)
            pool.wait_ge(zer, 2)
            pre(2)
            pre(3)
            los(1)
            pre(4)
            pre(5)
            los(3)
            for xi in range(6, 10):
                pre(xi)
                if xi < 8:
                    los(xi - 2)
            los(U_RETH + 2)

            for h in range(RH + 1):
                n = U_RETH + 4 * h
                los(min(n + 3, U_OUT0 + 2))
                if h:
                    pool.wait_ge(kv_mm, h)
                    pool.wait_ge(*EV[n - 4])
                    pool.wait_ge(dec_e, 3)
                    for d in range(2):
                        ins = pool.tensor_tensor(qfb[:, d, :].rearrange("p (a c) -> p a c", a=8),
                                                 qT[:, (h - 1) % 2, :].rearrange("p (a c) -> p a c", a=8),
                                                 QD[:, d, h - 1:h, :].to_broadcast([P, 8, P]), ALU.mult)
                    ins.then_inc(qfb_rdy, 1)
                    los(min(n + 5, U_OUT0 + 2))
                    pool.wait_ge(var_rdy, h)
                    link(pool.tensor_scalar(gvar[:, :], mv[:, :, 1], 1.0, 1e-5, ALU.mult, ALU.add))
                    pool.tensor_tensor(grstd[:, :], gvar[:, :], minus_half[:, :], ALU.pow).then_inc(grs_rdy, 1)
                if h < RH:
                    los(n + 6)
            los(U_OUT0 + 2)
            for th in range(2):
                los(U_OUT0 + KD * (th + 1) + 2)
                post(0, th, U_OUT0 + KD * (th + 1) + 5)
            ffn(0)
            pool.wait_ge(w_used, U_NA)
            pool.wait_ge(pre_rs, 26)
            pool.wait_ge(w_lo, done[0])
            for g in range(2):
                for b in range(2):
                    pool.memset(qbd[GW * b:GW * b + GW, g, :, 1 - b, :], 0.0).then_inc(qz, 1)
                    pool.wait_ge(qz, 2 * g + b + 1)

            def mask_bias(hp):
                pool.wait_ge(tb_ld, 64 * (hp + 1))
                if hp >= 2:
                    pool.wait_ge(s_add, R_ROW + ROWS * (hp - 1))
                for w in range(2):
                    t = TB[:, hp % 2, w, :, :]
                    mul, add = (nmask[:, (2 * w + i) * KC:(2 * w + i + 1) * KC].rearrange("p (a c) -> p a c", a=1)
                                .to_broadcast([P, OFFS, KC]) for i in range(2))
                    link(pool.tensor_tensor(t, TR[:, :, 8 - 8 * w:8 - 8 * w + KC], mul, ALU.mult))
                    link(pool.tensor_tensor(t, t, add, ALU.add))
                    rows = nmask[:, 4 * KC:4 * KC + KR].rearrange("p (a c) -> p a c", c=1).to_broadcast([P, KR, KC])
                    ins = pool.tensor_tensor(TI[:, hp % 2, w, :, :], t[:, 2:2 + KR, :], rows, ALU.add)
                    if w == 0:
                        link(ins)
                ins.then_inc(tb_rdy, 1)

            pool.wait_ge(nmask_ld, 16)
            mask_bias(0)
            los(U_NAH + 2)
            for hp in range(HP):
                los(min(U_NAH + 3 * hp + 5, U_OUT1 + 2))
                if hp + 1 < HP:
                    mask_bias(hp + 1)
            los(U_OUT1 + 2)
            for th in range(2):
                los(U_OUT1 + KD * (th + 1) + 2)
                post(2, th, U_OUT1 + KD * (th + 1) + 5)
            ffn(1)

        @block.scalar
        def _(act):
            done = [0]

            def split_hi(slot, come, used):
                act.wait_ge(w_in[slot], come)
                if used is not None:
                    act.wait_ge(w_used, used)
                act.activation(whi[:, slot, :], stage[:, slot, :], ACT.Copy).then_inc(w_hi, 1)

            def his(upto):
                for n in range(done[0], min(upto, U_END)):
                    split_hi(n % RING, 16 * (n // RING + 1), n - RING + 1 if n >= RING else None)
                done[0] = max(done[0], min(upto, U_END))

            squares = []

            def square(src, col, ready, need, signal):
                act.wait_ge(ready, need)
                n = len(squares)
                if n >= 2:
                    act.wait_ge(*squares[n - 2])
                squares.append((signal, 1 + sum(s is signal for s, _ in squares)))
                act.activation(junk[n % 2][:, :], src, ACT.Square, accum_out=sumsq[:, col:col + 1]).then_inc(signal, 1)

            def pre_x(xi):
                square(pre_tile(xi), xi, x_ld[xi], 16, pre_sq)

            def turn(t):
                width = MEM if t == 0 else HALF
                th = 1 if t in (2, 6) else 0
                if N_TURNS[t] < KD and t not in (2, 6):
                    act.wait_ge(t_done, turned(t))
                if t == 0:
                    act.wait_ge(c_ids, 32)
                for k in range(KD):
                    if t in (2, 6) and k == 0:
                        act.wait_ge(t_low, t // 4 + 1)
                    if t in (2, 6) and k == 4:
                        act.wait_ge(t_done, turned(t))
                    if N_TURNS[t] == KD:
                        act.wait_ge(t_done, turned(t - 1) + k + 1)
                    bank = 4 + k % 4 if t in (2, 6) else k
                    act.activation(aT[:, th, 0, k, 0:width], PS[:, bank, 0:width], ACT.Copy,
                                   scale=gT[:, GAIN[t], k:k + 1]).then_inc(a_hi, 1)

            def post_in(s, th):
                for i in range(TT):
                    e = 8 * s + 4 * th + i
                    square(PS[:, 2 * i:2 * i + 2, :].rearrange("p a c -> p (a c)"), N_T + e, y_done, e + 1, y_sq)

            def post_out(s, th, upto=None, first=None):
                for i in range(TT):
                    if i == 0 and first is not None:
                        first()
                    elif i == 0 and upto is not None:
                        his(upto - 1)
                    if i == 2 and upto is not None:
                        his(upto)
                    if s < 3:
                        e = 8 * s + 4 * th + i
                        square(Hb[:, i, :], 10 + e, h_new, e + 1, pre_sq)

            def silu_gate(slot, need, free):
                act.wait_ge(w_used, need)
                if free is not None:
                    act.wait_ge(hid_t, free)
                act.activation(sg[:, slot, :], PS[:, 2 * slot, :], ACT.Silu).then_inc(g_act, 1)

            def ffn_tile(l, th, j):
                n = U_FF[l] + 3 * KH * th + 2 * j
                g = (2 * l + th) * KH + j
                his(n + 3)
                silu_gate(j % 3, n + 1, g - 2 if g >= 3 else None)
                his(n + 4)

            def post_then_ffn(s, l, th):
                post_out(s, 1 - th, U_FF[l] + 3 * KH * th + 5, lambda: ffn_tile(l, th, 0))

            def ffn(l):
                for th in range(2):
                    n0 = U_FF[l] + 3 * KH * th
                    g0 = (2 * l + th) * KH
                    for j in range(1, 3):
                        ffn_tile(l, th, j)
                    with act.Fori(0, 6) as i:
                        for c in range(3):
                            m = n0 + 2 * (3 + c)
                            for part in range(2):
                                u = m + 2 + part
                                split_hi(u % RING, i * 32 + 16 * (u // RING + 1), i * 6 + (u - RING + 1))
                                if part == 0:
                                    silu_gate(c, i * 6 + (m + 1), i * 3 + (g0 + 3 + c - 2))
                    done[0] += 36
                    ffn_tile(l, th, KH - 1)
                    if th == 0 or l == 0:
                        turn(4 * l + 4 + th)
                    his(n0 + 3 * KH + 2)
                    post_in(1 + 2 * l, th)
                    if th == 0:
                        post_then_ffn(1 + 2 * l, l, 1)
                    else:
                        post_out(1 + 2 * l, th)

            def probs(r, is_mem):
                act.wait_ge(s_add, r + 1)
                if is_mem:
                    if r >= 3:
                        act.wait_ge(s_tr, r - 2)
                    bank = banks(r)[0]
                    for g in range(2):
                        ins = act.activation(SB[:, r % 3, MEM * g:MEM * g + MEM], PS[:, bank, MEM * g:MEM * g + MEM],
                                             ACT.Exp, bias=negmax[:, r % 4, g:g + 1], scale=0.125,
                                             accum_out=rowsum[:, r % 4, g:g + 1])
                    ins.then_inc(s_exp, 1)
                else:
                    keys = KC * window((r - R_ROW) % ROWS)[1]
                    act.activation(SB[:, r % 3, 0:keys], SB[:, r % 3, 0:keys], ACT.Exp, bias=negmax[:, r % 4, 0:1], scale=-1.0,
                                   accum_out=rowsum[:, r % 4, 0:1]).then_inc(s_exp, 1)

            def take_pt(r):
                act.wait_ge(s_tr, r + 1)
                if r >= 2:
                    act.wait_ge(pv, r - 1)
                if r < R_ROW:
                    parts = [(P, 0, 512)]
                elif window((r - R_ROW) % ROWS)[1] == KR:
                    parts = [(3 * KC, 0, 3 * P)]
                else:
                    parts = [(3 * KC, 0, 2 * P), (2 * KC, 2 * P, 3 * P)]
                for keys, c0, c1 in parts:
                    ins = act.activation(PT[0:keys, r % 2, c0:c1], PS[0:keys, banks(r)[1], c0:c1], ACT.Copy)
                ins.then_inc(pt_ev, 1)

            def take(n, dst, func=ACT.Copy):
                act.wait_ge(w_used, n + 1)
                for th in range(2):
                    ins = act.activation(dst[:, HALF * th:HALF * th + HALF], PS[:, 2 * (n % 2) + th, :], func)
                ins.then_inc(ev_act, 1)

            def mem_step(run, t):
                r0, tiles = run[:2]
                if t < tiles:
                    probs(r0 + t, True)
                if 0 <= t - 2 < tiles:
                    take_pt(r0 + t - 2)

            def cat_split(l, pieces):
                for piece in pieces:
                    th, k = piece // KD, piece % KD
                    if 8 * l + k in DIRECT:
                        act.wait_ge(oc_rdy, 8 * l + k + 1)
                    else:
                        act.wait_ge(cat_ld[k], 16 if k == 6 else 16 * (l + 1))
                    act.activation(catT[:, th, 0, k, :], catf[:, k, HALF * th:HALF * th + HALF], ACT.Copy)\
                       .then_inc(cat_hi, 1)

            for xi in range(4):
                pre_x(xi)
            his(1)
            pre_x(4)
            pre_x(5)
            turn(0)
            his(3)
            for xi in range(6, 10):
                pre_x(xi)
                if xi == 8:
                    act.wait_ge(w_used, 3)
                    act.activation(mvT[:, 0, :], PS[:, 0, 0:MEM], ACT.Copy).then_inc(ev_act, 1)
                    act.wait_ge(w_used, 4)
                    act.activation(mvT[:, 1, :], PS[:, 2, 0:MEM], ACT.Copy).then_inc(ev_act, 1)
                elif xi < 8:
                    his(xi - 2)
            turn(1)
            his(U_RET + 2)
            turn(2)
            his(U_RET + 3)
            take(U_RET, MQ[:, 0, :])
            his(U_RET + 4)
            take(U_RET + 1, MQ[:, 1, :])

            def decays(t):
                if t == 2:
                    act.wait_ge(c_ld, 96)
                    act.activation(lgb[:, :], lgb[:, :], ACT.Exp).then_inc(dec_e, 1)
                if t == 3:
                    act.wait_ge(dec_rdy, 1)
                    act.activation(kdec[:, :, :], kprod[:, :, :], ACT.Exp)
                    act.activation(cdec[:, :, :], lg[:, :, :], ACT.Exp, scale=float(P)).then_inc(dec_e, 1)
                    for d in range(2):
                        for h in range(RH):
                            ins = act.activation(QD[:, d, h, :], dconst[:, 4 + d, :], ACT.Exp, scale=lg[:, d, h:h + 1])
                    ins.then_inc(dec_e, 1)
                if 4 <= t < 4 + RH:
                    h = t - 4
                    if h:
                        act.wait_ge(dec_rdy, 1 + h)
                    for d in range(2):
                        ins = act.activation(dexp[:, d, :], dconst[:, d, :], ACT.Exp, scale=lg[:, d, h:h + 1])
                    ins.then_inc(dec_e, 1)

            def take_value_gate(h, i):
                n = U_RETH + 4 * h + i
                his(n + 3)
                if i == 2:
                    take(n, vT[:, :])
                if i == 3:
                    c = 1 + h
                    if c >= 2:
                        act.wait_ge(oc_st[c % 2], stored(c - 2))
                    take(n, OC[:, c % 2, :], ACT.Silu)

            for t in range(steps(RUN_A0)):
                mem_step(RUN_A0, t)
                decays(t)
                for u in units_done(t, 4 * KD, steps(RUN_A0)):
                    take_value_gate(0, u)
            for h in range(1, RH + 1):
                n = U_RETH + 4 * h
                g = h - 1
                if h < RH:
                    his(n + 3)
                act.wait_ge(ktr, h)
                for b in range(2):
                    ins = act.activation(Ktok[:, 4 * b:4 * b + 4, :].rearrange("p a c -> p (a c)"), PS[:, 4 + b, :], ACT.Copy)
                ins.then_inc(ktok_rdy, 1)
                act.wait_ge(vtr, h)
                if h == 1:
                    act.wait_ge(dec_rdy, 2 + RH)
                for b in range(2):
                    for d in range(2):
                        ins = act.activation(vfb[:, 4 * b:4 * b + 4, d, :],
                                             PS[:, 6 + b, :].rearrange("p (a c) -> p a c", a=4), ACT.Copy,
                                             scale=kdec[:, d, g:g + 1])
                ins.then_inc(vfb_rdy, 1)
                if h < RH:
                    his(n + 4)
                    take_value_gate(h, 2)
                    take_value_gate(h, 3)
                else:
                    for t in range(9):
                        mem_step(RUN_B0, t)
                    cat_split(0, range(2))
                act.wait_ge(y_tr, h)
                for b in range(2):
                    ins = act.activation(PS[:, 4 + b, :], PS[:, 4 + b, :], ACT.Identity,
                                         scale=gnT[:, 0, g:g + 1], bias=gnT[:, 1, g:g + 1])
                ins.then_inc(aff, 1)
            for t in range(9, steps(RUN_B0)):
                mem_step(RUN_B0, t)
            his(U_OUT0 + 2)
            cat_split(0, range(2, 2 * KD))
            his(U_OUT0 + KD + 2)
            post_in(0, 0)
            post_out(0, 0, U_OUT0 + KD + 5)
            his(U_OUT0 + 2 * KD + 2)
            post_in(0, 1)
            turn(3)
            post_then_ffn(0, 0, 0)
            ffn(0)
            turn(6)
            for i in range(TT):
                act.wait_ge(h_st[i], 64)
            act.wait_ge(h_new, 16)
            his(U_NA + 3)
            take(U_NA, MQ[:, 0, :])
            his(U_NA + 4)
            take(U_NA + 1, MQ[:, 1, :])

            def take_q(n, dst):
                act.wait_ge(w_used, n + 1)
                for th in range(2):
                    for b in range(2):
                        for w in range(2):
                            ins = act.activation(
                                dst[GW * b:GW * b + GW, 8 * th:8 * th + 8, b, :]
                                .rearrange("q (j w) (p c) -> q w j p c", w=2, p=2)[:, w, :, :, ::-1],
                                PS[GW * b:GW * b + GW, 2 * (n % 2) + th, :]
                                .rearrange("q (j p w c) -> q w j p c", p=2, w=2, c=QC)[:, w, :, :, :],
                                ACT.Copy, scale=0.125)
                ins.then_inc(ev_act, 1)

            def take_query_value(hp, i):
                n = U_NAH + 3 * hp + i
                his(n + 3)
                if i == 0:
                    take_q(n, qbd[:, hp % 2, :, :, :])
                if i == 2:
                    act.wait_ge(w_used, n + 1)
                    for th in range(2):
                        for w in range(2):
                            first = (GW - KC) * w
                            ins = act.activation(
                                vTn[:, w, th * ROWS // 2 * KC:(th + 1) * ROWS // 2 * KC].rearrange("p (a c) -> p a c", c=KC),
                                PS[:, 2 * (n % 2) + th, :].rearrange("p (a c) -> p a c", c=GW)[:, :, first:first + KC],
                                ACT.Copy)
                    ins.then_inc(ev_act, 1)

            act.wait_ge(qz, 4)
            for t in range(steps(RUN_A1)):
                mem_step(RUN_A1, t)
                for u in units_done(t, PIECES, steps(RUN_A1)):
                    take_query_value(0, u)
            for hp in range(1, HP + 1):
                for i, c in enumerate((0, 16)):
                    act.wait_ge(vn_tr, 4 * hp - 3 + 2 * i)
                    for b in range(2):
                        ins = act.activation(Vc[0:3 * KC, c + 4 * b:c + 4 * b + 4, :].rearrange("p a c -> p (a c)"),
                                             PS[0:3 * KC, 4 + b, :], ACT.Copy)
                    ins.then_inc(vn_a, 1)
                r0 = R_ROW + ROWS * (hp - 1)
                for t in range(LAST):
                    if t < ROWS:
                        probs(r0 + t, False)
                    if 0 <= t - 2 < ROWS:
                        take_pt(r0 + t - 2)
                    if hp < HP:
                        for u in units_done(t, PIECES, ROWS, EARLY):
                            take_query_value(hp, u)
                    elif t in (10, 12):
                        cat_split(1, [(t - 10) // 2])
            his(U_OUT1 + 2)
            cat_split(1, range(2, 2 * KD))
            his(U_OUT1 + KD + 2)
            post_in(2, 0)
            post_out(2, 0, U_OUT1 + KD + 5)
            his(U_OUT1 + 2 * KD + 2)
            post_in(2, 1)
            turn(7)
            post_then_ffn(2, 1, 0)
            ffn(1)

        @block.vector
        def _(dve):
            own = [0]
            place = [None]

            def link(ins):
                own[0] += 1
                ins.then_inc(d_own, 1)
                dve.wait_ge(d_own, own[0])

            def pre(xi, src, dst):
                dve.wait_ge(pre_rs, xi + 1)
                dve.tensor_scalar(dst, src, rstd[:, xi:xi + 1], None, ALU.mult).then_inc(xs, 1)

            def turn(t):
                width = MEM if t == 0 else HALF
                th = 1 if t in (2, 6) else 0
                for k in range(KD):
                    bank = 4 + k % 4 if t in (2, 6) else k
                    dve.wait_ge(a_hi, 8 * t + k + 1)
                    dve.scalar_tensor_tensor(out=aT[:, th, 1, k, 0:width], in0=PS[:, bank, 0:width],
                                             scalar=gT[:, GAIN[t], k:k + 1],
                                             in1=aT[:, th, 0, k, 0:width].bitcast(F32),
                                             op0=ALU.mult, op1=ALU.subtract).then_inc(a_lo, 1)

            def post_in(s, th):
                Yt = y_tiles(s, th)
                dve.wait_ge(g_ld, 16 * (s + 1))
                if Yt is Y:
                    dve.wait_ge(t_done, turned({(0, 1): 2, (1, 0): 4, (1, 1): 5, (2, 1): 6, (3, 0): 8, (3, 1): 8}[s, th]))
                for i in range(TT):
                    e = 8 * s + 4 * th + i
                    dve.wait_ge(post_rs, e + 1)
                    dve.scalar_tensor_tensor(out=Yt[:, i, :], in0=PS[:, 2 * i:2 * i + 2, :].rearrange("p a c -> p (a c)"),
                                             scalar=rstd[:, N_T + e:N_T + e + 1], in1=gB[:, :],
                                             op0=ALU.mult, op1=ALU.mult).then_inc(y_cp, 1)

            def post_out(s, th):
                Yt = y_tiles(s, th)
                for i in range(TT):
                    e = 8 * s + 4 * th + i
                    dve.wait_ge(y_cp, e + 1)
                    dve.wait_ge(h_ld[i], 16 * (e // TT + 1))
                    dve.tensor_tensor(Hb[:, i, :], Hb[:, i, :], Yt[:, i, :], ALU.add).then_inc(h_new, 1)
                    if s < 3 and i:
                        pre(10 + e - 1, Hb[:, i - 1, :], Yt[:, i - 1, :])
                if s < 3:
                    pre(10 + e, Hb[:, TT - 1, :], Yt[:, TT - 1, :])

            def hidden(slot, up_need, gate_need, last):
                dve.wait_ge(g_act, gate_need)
                if last is not None:
                    dve.wait_ge(hid_rdy, last)
                dve.wait_ge(w_used, up_need)
                ins = dve.tensor_tensor(hidf[:, :], sg[:, slot, :], PS[:, 2 * slot + 1, :], ALU.mult)
                ins.then_inc(hid_t, 1)

            def hidden_split(dst_hi, dst_lo, need):
                dve.wait_ge(hid_t, need)
                link(dve.tensor_copy(dst_hi, hidf[:, :]))
                dve.tensor_tensor(dst_lo, hidf[:, :], dst_hi.bitcast(F32), ALU.subtract).then_inc(hid_rdy, 1)

            def ffn(l):
                for th in range(2):
                    n0 = U_FF[l] + 3 * KH * th
                    g0 = (2 * l + th) * KH

                    def tile(j):
                        hi, lo = hid[:, 0, j, :], hid[:, 1, j, :]
                        hidden(j % 3, n0 + 2 * j + 2, g0 + j + 1, g0 + j if g0 + j else None)
                        hidden_split(hi, lo, g0 + j + 1)

                    for j in range(3):
                        tile(j)
                    with dve.Fori(0, 6) as i:
                        for c in range(3):
                            j = 3 + c
                            hi = hid[:, 0, bass.ds(i * 3 + j, 1), :].rearrange("p a c -> p (a c)")
                            lo = hid[:, 1, bass.ds(i * 3 + j, 1), :].rearrange("p a c -> p (a c)")
                            hidden(c, i * 6 + (n0 + 2 * j + 2), i * 3 + (g0 + j + 1), i * 3 + (g0 + j))
                            dve.wait_ge(hid_t, i * 3 + (g0 + j + 1))
                            dve.tensor_copy(hi, hidf[:, :]).then_inc(d_own, 1)
                            dve.wait_ge(d_own, i * 3 + (own[0] + c + 1))
                            dve.tensor_tensor(lo, hidf[:, :], hi.bitcast(F32), ALU.subtract).then_inc(hid_rdy, 1)
                    own[0] += 18
                    tile(KH - 1)
                    if th == 0 or l == 0:
                        turn(4 * l + 4 + th)
                    post_in(1 + 2 * l, th)
                    post_out(1 + 2 * l, th)

            def peak(r, is_mem, t=0, hp=0):
                dve.wait_ge(s_mm, r + 1)
                if r >= 4:
                    dve.wait_ge(s_exp, r - 3)
                bank = banks(r)[0]
                if is_mem:
                    link(dve.tensor_reduce(maxraw[:, r % 4, :], PS[:, bank, :].rearrange("p (g c) -> p g c", g=2),
                                           AX.X, ALU.max))
                    dve.tensor_scalar(negmax[:, r % 4, :], maxraw[:, r % 4, :], -0.125, None, ALU.mult).then_inc(s_add, 1)
                else:
                    if t == 0:
                        dve.wait_ge(tb_rdy, hp + 1)
                    if r >= 3:
                        dve.wait_ge(s_tr, r - 2)
                    first, n, row, w = window(t)
                    dr = first - row + WR - 2
                    bias = (TI[:, hp % 2, w, :, :] if n == KR else TB[:, hp % 2, w, dr:dr + WR, :]).rearrange("p a c -> p (a c)")
                    dve.tensor_tensor_reduce(SB[:, r % 3, 0:n * KC], PS[:, bank, 0:n * KC], bias, -1.0, 3.0e38,
                                             ALU.add, ALU.min, negmax[:, r % 4, 0:1]).then_inc(s_add, 1)

            def normalise(r, is_mem):
                dve.wait_ge(s_exp, r + 1)
                n = 2 if is_mem else 1
                link(dve.reciprocal(rowinv[:, r % 4, 0:n], rowsum[:, r % 4, 0:n]))
                w = MEM if is_mem else KC * window((r - R_ROW) % ROWS)[1]
                for g in range(n):
                    part = SB[:, r % 3, w * g:w * g + w]
                    ins = dve.tensor_scalar(part, part, rowinv[:, r % 4, g:g + 1], None, ALU.mult)
                ins.then_inc(s_nrm, 1)

            def output_place(c):
                if c in DIRECT:
                    dve.wait_ge(w_used, U_OUT[c // 8])
                    return catf[:, c % 8, :]
                if c >= 2:
                    dve.wait_ge(oc_st[c % 2], stored(c - 2))
                return OC[:, c % 2, :]

            def mem_step(run, t):
                r0, tiles, _, c0 = run
                q = t - 4
                if 0 <= q < tiles:
                    r, i = r0 + q, q % 8
                    if i == 0:
                        place[0] = output_place(c0 + q // 8)
                    dve.wait_ge(pv, r + 1)
                    for g in range(2):
                        ins = dve.tensor_copy(place[0][64 * g:64 * g + 64, i * P:(i + 1) * P],
                                              PS[64 * g:64 * g + 64, banks(r)[2], P * g:P * g + P])
                    ins.then_inc(o_ev, 1)
                    if i == 7:
                        dve.wait_ge(o_ev, o_count(r + 1))
                        dve.engine_nop().then_inc(oc_rdy, 1)
                if t < tiles:
                    peak(r0 + t, True)
                if 0 <= t - 1 < tiles:
                    normalise(r0 + t - 1, True)

            def cat_split(l, pieces):
                for piece in pieces:
                    th, k = piece // KD, piece % KD
                    dve.wait_ge(cat_hi, 16 * l + piece + 1)
                    dve.tensor_tensor(catT[:, th, 1, k, :], catf[:, k, HALF * th:HALF * th + HALF],
                                      catT[:, th, 0, k, :].bitcast(F32), ALU.subtract).then_inc(cat_lo, 1)

            def rotate(n, dst):
                dve.wait_ge(w_used, n + 1)
                for th in range(2):
                    cols = slice(HALF * th, HALF * th + HALF)
                    src = PS[:, 2 * (n % 2) + th, :]
                    dve.tensor_tensor(dst[:, cols], src, ropeC[:, cols], ALU.mult)
                    dve.tensor_tensor(rtmp[0:64, :], src[64:128, :], ropeS[64:128, cols], ALU.mult)
                    link(dve.tensor_tensor(rtmp[64:128, :], src[0:64, :], ropeS[0:64, cols], ALU.mult))
                    ins = dve.tensor_tensor(dst[:, cols], dst[:, cols], rtmp[:, :], ALU.add)
                    if th == 0:
                        link(ins)
                ins.then_inc(ev_dve, 1)
                dve.wait_ge(*EV[n])

            for xi in range(4):
                pre(xi, pre_tile(xi), pre_tile(xi))
            turn(0)
            pre(4, pre_tile(4), pre_tile(4))
            pre(5, pre_tile(5), pre_tile(5))
            dve.wait_ge(zer, 1)
            for n in range(2):
                dve.wait_ge(w_used, n + 1)
                for g in range(2):
                    ins = dve.tensor_copy(bdK[64 * g:64 * g + 64, n, MEM * g:MEM * g + MEM],
                                          PS[64 * g:64 * g + 64, 2 * n, 0:MEM])
                ins.then_inc(ev_dve, 1)
            for xi in range(6, 9):
                pre(xi, pre_tile(xi), pre_tile(xi))
            dve.wait_ge(pre_sq, 10)
            dve.wait_ge(mvt, 1)
            dve.tensor_copy(memV[:, :, :].rearrange("p k (h f) -> p h k f", h=2),
                            PS[:, 4, :].rearrange("p (h k f) -> p h k f", h=2, k=2)).then_inc(memv_rdy, 1)
            pre(9, pre_tile(9), pre_tile(9))
            turn(1)
            turn(2)

            def decays(t):
                if t == 2:
                    dve.wait_ge(dec_e, 1)
                    link(dve.tensor_scalar(lg[:, :, :].rearrange("p a c -> p (a c)"), lgb[:, :], -1.0, None, ALU.mult))
                    dve.wait_ge(zer, 2)
                    dve.wait_ge(rpb_st, 48)
                    for d in range(2):
                        ins = dve.tensor_scalar(kprod[:, d, :], lg[:, d, :], colc[:, d:d + 1], None, ALU.mult)
                    ins.then_inc(dec_rdy, 1)
                if t == 3:
                    dve.wait_ge(dec_e, 2)
                    link(dve.tensor_scalar(kdec[:, :, :], kdec[:, :, :], float(P) ** -0.5, None, ALU.mult))
                if 4 <= t < 4 + RH:
                    h = t - 4
                    dve.wait_ge(dec_e, 4 + h)
                    dve.tensor_tensor(dexp[:, 0, :], dexp[:, 0, :], dconst[:, 2, :], ALU.mult)
                    link(dve.tensor_tensor(dexp[:, 1, :], dexp[:, 1, :], dconst[:, 3, :], ALU.mult))
                    dve.tensor_tensor(DM[:, h, :], dexp[:, 0, :], dexp[:, 1, :], ALU.add).then_inc(dec_rdy, 1)
                if t == 4 + RH:
                    dve.wait_ge(dec_rdy, 1 + RH)
                    dve.memset(states[:, 0, 0, :], 0.0)
                    dve.memset(states[:, 7, 1, :], 0.0).then_inc(dec_rdy, 1)
                    dve.wait_ge(dec_rdy, 2 + RH)

            def values(h):
                dve.wait_ge(vfb_rdy, h)
                for b in range(2):
                    ins = dve.tensor_copy(V[:, 4 * b:4 * b + 4, :].rearrange("p a c -> p (a c)"), PS[:, 6 + b, :])
                ins.then_inc(v_rdy, 1)
                dve.wait_ge(st_mm, h)
                for b in range(2):
                    ins = dve.tensor_tensor(ST[:, 4 * b:4 * b + 4, :], PS[:, 4 + b, :].rearrange("p (a c) -> p a c", a=4),
                                            DM[:, h - 1:h, :].to_broadcast([P, 4, P]), ALU.mult)
                ins.then_inc(st_rdy, 1)

            def scan(h, beside=None):
                g = h - 1
                dve.wait_ge(kv_mm, h)

                def kv(c, d):
                    bank = (6, 7, 4, 5)[c // 2]
                    return PS[:, bank, 256 * (c % 2) + P * d:256 * (c % 2) + P * d + P]

                for c in range(7):
                    dve.scalar_tensor_tensor(out=states[:, c + 1, 0, :], in0=states[:, c, 0, :],
                                             scalar=cdec[:, 0, g:g + 1], in1=kv(c, 0), op0=ALU.mult, op1=ALU.add)
                    b = 7 - c
                    ins = dve.scalar_tensor_tensor(out=states[:, b - 1, 1, :], in0=states[:, b, 1, :],
                                                   scalar=cdec[:, 1, g:g + 1], in1=kv(b, 1),
                                                   op0=ALU.mult, op1=ALU.add)
                    if c < 6:
                        link(ins)
                        if beside is not None:
                            beside(c)
                ins.then_inc(scan_rdy, 1)

            def group_norm(h, beside=None):
                dve.wait_ge(out_mm, h)
                for c in range(8):
                    ins = dve.bn_stats(stats[:, c, :], PS[:, 6 + c // 4, (c % 4) * P:(c % 4 + 1) * P])
                link(ins)
                for c in range(8):
                    ins = dve.bn_aggr(mv[:, c, :], stats[:, c, :])
                ins.then_inc(var_rdy, 1)
                if beside is not None:
                    beside()
                dve.wait_ge(grs_rdy, h)
                for c in range(8):
                    ins = dve.tensor_scalar(ST[:, c, :], PS[:, 6 + c // 4, (c % 4) * P:(c % 4 + 1) * P],
                                            mv[:, c, 0:1], grstd[:, c:c + 1], ALU.subtract, ALU.mult)
                ins.then_inc(yn_rdy, 1)

            def gated(h):
                g = h - 1
                dve.wait_ge(aff, h)
                dve.wait_ge(ev_act, EV[U_RETH + 4 * g + 3][1])
                dst = output_place(h) if h in DIRECT else OC[:, h % 2, :]
                for b in range(2):
                    cols = slice(HALF * b, HALF * b + HALF)
                    ins = dve.tensor_tensor(dst[:, cols], OC[:, h % 2, cols], PS[:, 4 + b, :], ALU.mult)
                ins.then_inc(oc_rdy, 1)

            for t in range(steps(RUN_A0) + 1):
                mem_step(RUN_A0, t)
                decays(t)
                for u in units_done(t, 4 * KD, steps(RUN_A0)):
                    if u < 2:
                        rotate(U_RETH + u, (qT[:, 0, :], kT[:, :])[u])
            for h in range(1, RH + 1):
                n = U_RETH + 4 * h
                if h < RH:
                    if h >= 2:
                        dve.wait_ge(qfb_rdy, h - 1)
                    rotate(n, qT[:, h % 2, :])
                    values(h)
                    rotate(n + 1, kT[:, :])
                    scan(h)
                    group_norm(h)
                    gated(h)
                    continue
                values(h)
                for t in range(3):
                    mem_step(RUN_B0, t)
                scan(h, lambda c: mem_step(RUN_B0, 3 + c // 2) if c in (1, 3, 5) else None)
                mem_step(RUN_B0, 6)
                group_norm(h, lambda: mem_step(RUN_B0, 7))
                mem_step(RUN_B0, 8)
                cat_split(0, range(2))
                gated(h)
                for t in range(9, steps(RUN_B0) + 1):
                    mem_step(RUN_B0, t)
            cat_split(0, range(2, 2 * KD))
            post_in(0, 0)
            post_out(0, 0)
            post_in(0, 1)
            turn(3)
            post_out(0, 1)
            ffn(0)
            turn(6)
            for i in range(TT):
                dve.wait_ge(h_st[i], 64)

            def take_k(n):
                dve.wait_ge(w_used, n + 1)
                for th in range(2):
                    ins = dve.tensor_copy(kTn[:, ((n - U_NAH) // 3) % 2, HALF * th:HALF * th + HALF],
                                          PS[:, 2 * (n % 2) + th, :])
                ins.then_inc(ev_dve, 1)

            for t in range(steps(RUN_A1) + 1):
                mem_step(RUN_A1, t)
                for u in units_done(t, PIECES, steps(RUN_A1)):
                    if u == 1:
                        take_k(U_NAH + 1)
            for hp in range(1, HP + 1):
                dve.wait_ge(vn_tr, 4 * hp - 2)
                for b in range(2):
                    ins = dve.tensor_copy(Vc[0:3 * KC, 8 + 4 * b:8 + 4 * b + 4, :].rearrange("p a c -> p (a c)"),
                                          PS[0:3 * KC, 6 + b, :])
                ins.then_inc(vn_d, 1)
                dve.wait_ge(vn_tr, 4 * hp)
                dve.tensor_copy(Vc[0:2 * KC, 24:26, :].rearrange("p a c -> p (a c)"), PS[0:2 * KC, 6, 0:2 * P]).then_inc(vn_d, 1)
                g = hp - 1
                r0 = R_ROW + ROWS * g
                for t in range(LAST):
                    q = t - 4
                    if 0 <= q < ROWS and q % 4 == 3:
                        if q == 3:
                            place[0] = output_place(9 + hp)
                        dve.wait_ge(pv, r0 + q + 1)
                        for b in range(2):
                            for w in range(2):
                                ins = dve.tensor_copy(
                                    place[0][64 * b:64 * b + 64, (q - 3) * GW:(q + 1) * GW]
                                    .rearrange("q (j p w c) -> q w j p c", p=2, w=2, c=QC)[:, w, :, :, :],
                                    PS[64 * b:64 * b + 64, 7, :]
                                    .rearrange("q (j w b p c) -> q w b j p c", w=2, b=2, p=2, c=QC)[:, w, b, :, :, ::-1])
                        ins.then_inc(o_ev, 1)
                        if q == ROWS - 1:
                            dve.wait_ge(o_ev, o_count(r0 + ROWS))
                            dve.engine_nop().then_inc(oc_rdy, 1)
                    if t < ROWS:
                        peak(r0 + t, False, t, g)
                    if 0 <= t - 1 < ROWS:
                        normalise(r0 + t - 1, False)
                    if hp < HP and 1 in units_done(t, PIECES, ROWS, EARLY):
                        take_k(U_NAH + 3 * hp + 1)
                    if hp == HP and t in (10, 12):
                        cat_split(1, [(t - 10) // 2])
            cat_split(1, range(2, 2 * KD))
            post_in(2, 0)
            post_out(2, 0)
            post_in(2, 1)
            turn(7)
            post_out(2, 1)
            ffn(1)

        @block.tensor
        def _(pe):
            def three(dst, stat, mov, start, stop):
                pe.matmul(dst, stat[0], mov[0], start=start, stop=False)
                pe.matmul(dst, stat[0], mov[1], start=False, stop=False)
                return pe.matmul(dst, stat[1], mov[0], start=False, stop=stop)

            def wtile(n, k):
                c = slice(k * P, (k + 1) * P)
                return whi[:, n % RING, c], wlo[:, n % RING, c]

            def turn(t, free):
                if N_TURNS[t] == 4:
                    for s, v in free:
                        pe.wait_ge(s, v)
                if t:
                    pe.wait_ge(a_hi, 8 * t)
                    pe.wait_ge(a_lo, 8 * t)
                Yt = set_tiles(t)
                if N_TURNS[t] == KD:
                    pe.wait_ge(xs, tiles_before(t + 1))
                    for k in range(KD):
                        for s, v in free(k):
                            pe.wait_ge(s, v)
                        for i in range(TT):
                            ins = pe.transpose(PS[:, k, i * P:(i + 1) * P], Yt[:, i, k * P:(k + 1) * P], ident[:, :])
                        ins.then_inc(t_done, 1)
                    return
                for i in range(tiles_before(t + 1) - tiles_before(t)):
                    pe.wait_ge(xs, tiles_before(t) + i + 1)
                    for k in range(KD):
                        ins = pe.transpose(PS[:, k, i * P:(i + 1) * P], Yt[:, i, k * P:(k + 1) * P], ident[:, :])
                    ins.then_inc(t_done, 1)

            def turn_late(t, part):
                if part:
                    pe.wait_ge(a_lo, 8 * t + 4)
                elif t == 6:
                    pe.wait_ge(y_cp, 16)
                    pe.wait_ge(y_sq, 16)
                for i in range(TT):
                    if not part:
                        pe.wait_ge(xs, tiles_before(t) + i + 1)
                    for k in range(4):
                        f = (4 * part + k) * P
                        ins = pe.transpose(PS[:, 4 + k, i * P:(i + 1) * P], Y[:, i, f:f + P], ident[:, :])
                    if part:
                        ins.then_inc(t_done, 1)
                if not part:
                    ins.then_inc(t_low, 1)

            def project(n, k, halves=(0, 1), sets=None):
                if k == 0 and 0 in halves:
                    pe.wait_ge(w_lo, n + 1)
                    if n - 2 in EV:
                        pe.wait_ge(*EV[n - 2])
                if sets is not None:
                    pe.wait_ge(a_lo, 8 * sets + max(k + 1, 2))
                for th in halves:
                    ins = three(PS[:, 2 * (n % 2) + th, :], wtile(n, k), (aT[:, th, 0, k, :], aT[:, th, 1, k, :]),
                                k == 0, k == KD - 1)
                if k == KD - 1 and 1 in halves:
                    ins.then_inc(w_used, 1)

            def first_two(n, t):
                if t == 6:
                    pe.wait_ge(y_cp, 14)
                    pe.wait_ge(y_sq, 14)
                for k in range(KD):
                    project(n, k, (0,), t - 1)
                for k in range(KD // 2):
                    project(n + 1, k, (0,))
                turn_late(t, 0)
                for k in range(KD // 2, KD):
                    project(n + 1, k, (0,))
                turn_late(t, 1)
                for k in range(KD):
                    project(n, k, (1,), t)
                for k in range(KD):
                    project(n + 1, k, (1,))

            def gate_up(n, bank, need_w, last_set=None):
                pe.wait_ge(w_lo, need_w)
                for k in range(KD):
                    if last_set is not None:
                        pe.wait_ge(a_lo, 8 * last_set + max(k + 1, 2))
                    ins = three(PS[:, bank, :], wtile(n, k), (aT[:, 0, 0, k, :], aT[:, 0, 1, k, :]), k == 0, k == KD - 1)
                ins.then_inc(w_used, 1)

            def contract(n0, kn, source, ready, free, order=range(TT)):
                for k in range(kn):
                    n = n0 + k
                    pe.wait_ge(w_lo, n + 1)
                    pe.wait_ge(*ready(k))
                    for i in order if k == 0 else range(TT):
                        if k == 0:
                            for s, v in free(i):
                                pe.wait_ge(s, v)
                        c = slice(i * P, (i + 1) * P)
                        for fh in range(2):
                            f = slice(512 * fh, 512 * fh + 512)
                            ins = three(PS[:, 2 * i + fh, :], (source[:, 0, k, c], source[:, 1, k, c]),
                                        (whi[:, n % RING, f], wlo[:, n % RING, f]), k == 0, k == kn - 1)
                        if k == kn - 1:
                            ins.then_inc(y_done, 1)
                    if k < kn - 1:
                        ins.then_inc(w_used, 1)
                pe.wait_ge(y_done, Y_DONE[0] + TT)
                pe.sem_inc(w_used, 1)
                Y_DONE[0] += TT

            Y_DONE = [0]

            def ffn(l):
                for th in range(2):
                    n0 = U_FF[l] + 3 * KH * th
                    g0 = (2 * l + th) * KH
                    s = 1 + 2 * l
                    t = 4 * l + 3 + th

                    def tile(j):
                        n = n0 + 2 * j
                        if j >= 3:
                            pe.wait_ge(hid_t, g0 + j - 2)
                        elif th:
                            pe.wait_ge(y_cp, 8 * s + j + 1)
                            pe.wait_ge(y_sq, 8 * s + j + 1)
                        gate_up(n, 2 * (j % 3), n + 1, t if j == 0 else None)
                        gate_up(n + 1, 2 * (j % 3) + 1, n + 2)

                    for j in range(3):
                        tile(j)
                    with pe.Fori(0, 6) as i:
                        for c in range(3):
                            j = 3 + c
                            n = n0 + 2 * j
                            pe.wait_ge(hid_t, i * 3 + (g0 + j - 2))
                            gate_up(n, 2 * c, i * 6 + (n + 1))
                            gate_up(n + 1, 2 * c + 1, i * 6 + (n + 2))
                    tile(KH - 1)
                    if th == 0 or l == 0:
                        turn(t + 1, lambda k: [(hid_t, g0 + (KH, KH - 2, KH - 1)[k // 2])] if k < 6 else
                             [(y_cp, 8 * s + TT), (y_sq, 8 * s + TT)] if th else [])

                    def free(i):
                        if th == 0 or l == 0:
                            return [(a_lo, 8 * (t + 1) + 2 * i + 2)]
                        return [(hid_t, g0 + KH), (y_cp, 8 * s + TT), (y_sq, 8 * s + TT)]

                    contract(n0 + 2 * KH, KH, hid, lambda k: (hid_rdy, g0 + k + 1), free)

            def out_project(l):
                for th in range(2):
                    e0 = 16 * l + 4 * th

                    def free(i):
                        if th:
                            return [(y_cp, e0 - TT + i + 1), (y_sq, e0 - TT + i + 1)]
                        if l == 0:
                            return [[(s_exp, 16)], [(oc_rdy, 8), (pt_ev, 16)], [(oc_rdy, 7)], [(yn_rdy, RH)]][i]
                        return [[EV[U_OUT1 - 1], EV[U_OUT1 - 2]], [EV[U_OUT1 - 1], EV[U_OUT1 - 2]],
                                [(s_exp, R_END[1])], [(pt_ev, R_END[1]), (oc_rdy, 16)]][i]

                    contract(U_OUT[l] + KD * th, KD, catT[:, th, :, :, :],
                             lambda k: (cat_lo, 16 * l + 8 * th + k + 1), free,
                             (3, 2, 0, 1) if l == 0 and th == 0 else range(TT))

            def scores(r, stat, mov):
                if r >= 2:
                    pe.wait_ge(s_add, r - 1)
                    pe.wait_ge(s_exp, r - 1)
                dst = PS[:, banks(r)[0], :]
                if len(mov.shape) == 3:
                    rows, cols = mov.shape[1:]
                    dst = PS[:, banks(r)[0], 0:rows * cols].rearrange("p (a c) -> p a c", a=rows)
                pe.matmul(dst, stat, mov, start=True, stop=True).then_inc(s_mm, 1)

            def turn_probs(r):
                pe.wait_ge(s_nrm, r + 1)
                if r:
                    pe.wait_ge(pt_ev, r)
                width, sizes = P, [P] * 4
                if r >= R_ROW:
                    width, sizes = 3 * KC, [keys for _, keys in chunks((r - R_ROW) % ROWS)]
                for c, keys in enumerate(sizes):
                    ins = pe.transpose(PS[0:keys, banks(r)[1], c * P:(c + 1) * P],
                                       SB[:, r % 3, c * width:c * width + keys], ident[:, :])
                ins.then_inc(s_tr, 1)

            def mem_step(run, t, fill=()):
                r0, tiles, hp0 = run[:3]
                fill = list(fill)
                if t < tiles:
                    hp, i = hp0 + t // 8, t % 8
                    scores(r0 + t, MQ[:, hp, i * P:(i + 1) * P], bdK[:, hp, :])
                for n, k in fill[:2]:
                    project(n, k)
                if 0 <= t - 2 < tiles:
                    turn_probs(r0 + t - 2)
                for n, k in fill[2:]:
                    project(n, k)
                if 0 <= t - 3 < tiles:
                    r = r0 + t - 3
                    hp = hp0 + (t - 3) // 8
                    pe.wait_ge(pt_ev, r + 1)
                    if r:
                        pe.wait_ge(o_ev, o_count(r))
                    for kc in range(2):
                        ins = pe.matmul(
                            PS[:, banks(r)[2], 0:256].rearrange("p (g c) -> p g c", g=2),
                            memV[:, kc, P * hp:P * hp + P],
                            PT[:, r % 2, :].rearrange("p (g k c) -> p g k c", g=2, k=2)[:, :, kc, :],
                            start=(kc == 0), stop=(kc == 1))
                    ins.then_inc(pv, 1)

            pe.wait_ge(c_ids, 32)
            turn(0, [])
            for n in range(4):
                pe.wait_ge(w_lo, n + 1)
                if n >= 2:
                    pe.wait_ge(*EV[n - 2])
                for k in range(KD):
                    if n == 0:
                        pe.wait_ge(a_lo, k + 1)
                    ins = three(PS[:, 2 * (n % 2), 0:MEM], wtile(n, k), (aT[:, 0, 0, k, 0:MEM], aT[:, 0, 1, k, 0:MEM]),
                                k == 0, k == KD - 1)
                ins.then_inc(w_used, 1)
            pe.wait_ge(*EV[3])
            for hp in range(2):
                for kc in range(2):
                    c = (2 * hp + kc) * P
                    ins = pe.transpose(PS[:, 4, c:c + P], mvT[:, hp, kc * P:(kc + 1) * P], ident[:, :])
            ins.then_inc(mvt, 1)
            turn(1, lambda k: [(memv_rdy, 1)] if k == 4 else [EV[1]])
            first_two(U_RET, 2)
            pe.wait_ge(*EV[U_RET])
            pe.wait_ge(a_lo, 24)
            for t in range(steps(RUN_A0)):
                mem_step(RUN_A0, t, [(U_RETH + p // KD, p % KD) for p in pieces_at(t, 4 * KD, steps(RUN_A0))])

            def unit(n):
                for k in range(KD):
                    project(n, k)

            def chunk_scores(h):
                n = U_RETH + 4 * h
                pe.wait_ge(*EV[n - 3])
                if h >= 2:
                    pe.wait_ge(oc_rdy, h)
                else:
                    pe.wait_ge(s_exp, 8)
                    pe.wait_ge(pt_ev, 8)
                    pe.wait_ge(o_ev, 8)
                for c in range(8):
                    ins = pe.transpose(PS[:, 4 + c // 4, (c % 4) * P:(c % 4 + 1) * P], kT[:, c * P:(c + 1) * P], ident[:, :])
                ins.then_inc(ktr, 1)
                pe.wait_ge(*EV[n - 2])
                if h >= 2:
                    pe.wait_ge(yn_rdy, h - 1)
                for c in range(8):
                    ins = pe.transpose(PS[:, 6 + c // 4, (c % 4) * P:(c % 4 + 1) * P], vT[:, c * P:(c + 1) * P], ident[:, :])
                ins.then_inc(vtr, 1)
                pe.wait_ge(ktok_rdy, h)
                for c in range(8):
                    cc = slice(c * P, (c + 1) * P)
                    ins = pe.matmul(PS[:, 4 + c // 4, (c % 4) * P:(c % 4 + 1) * P], kT[:, cc], qT[:, (h - 1) % 2, cc],
                                    start=True, stop=True)
                ins.then_inc(st_mm, 1)

            def chunk_states(h):
                pe.wait_ge(vfb_rdy, h)
                pe.wait_ge(v_rdy, h)
                for c in range(8):
                    if c == 4:
                        pe.wait_ge(st_rdy, h)
                    bank = (6, 7, 4, 5)[c // 2]
                    ins = pe.matmul(PS[:, bank, 256 * (c % 2):256 * (c % 2) + 256], Ktok[:, c, :],
                                    vfb[:, c, :, :].rearrange("p a c -> p (a c)"), start=True, stop=True)
                ins.then_inc(kv_mm, 1)

            def chunk_outputs(h):
                pe.wait_ge(scan_rdy, h)
                pe.wait_ge(qfb_rdy, h)
                for c in range(8):
                    dst = PS[:, 6 + c // 4, (c % 4) * P:(c % 4 + 1) * P]
                    cc = slice(c * P, (c + 1) * P)
                    pe.matmul(dst, ST[:, c, :], V[:, c, :], start=True, stop=False)
                    pe.matmul(dst, qfb[:, 0, cc], states[:, c, 0, :], start=False, stop=False)
                    ins = pe.matmul(dst, qfb[:, 1, cc], states[:, c, 1, :], start=False, stop=True)
                ins.then_inc(out_mm, 1)

            def turn_outputs(h):
                pe.wait_ge(yn_rdy, h)
                for c in range(8):
                    ins = pe.transpose(PS[:, 4 + c // 4, (c % 4) * P:(c % 4 + 1) * P], ST[:, c, :], ident[:, :])
                ins.then_inc(y_tr, 1)

            for h in range(1, RH):
                n = U_RETH + 4 * h
                unit(n)
                chunk_scores(h)
                unit(n + 1)
                chunk_states(h)
                unit(n + 2)
                chunk_outputs(h)
                unit(n + 3)
                turn_outputs(h)
            chunk_scores(RH)
            for u in range(1, 4):
                pe.wait_ge(*EV[U_OUT0 - u])
            for t in range(3):
                mem_step(RUN_B0, t)
            chunk_states(RH)
            for t in range(3, 6):
                mem_step(RUN_B0, t)
            chunk_outputs(RH)
            for t in range(6, 9):
                mem_step(RUN_B0, t)
            turn_outputs(RH)
            for t in range(9, steps(RUN_B0)):
                mem_step(RUN_B0, t)
            out_project(0)
            turn(3, lambda k: [(y_cp, 5 + k // 2), (y_sq, 5 + k // 2)])
            ffn(0)
            first_two(U_NA, 6)
            pe.wait_ge(*EV[U_NA])
            pe.wait_ge(a_lo, 56)
            pe.wait_ge(mkv_ld, 32)
            for t in range(steps(RUN_A1)):
                if t == 8:
                    pe.wait_ge(*EV[U_NA + 1])
                mem_step(RUN_A1, t, [(U_NAH + p // KD, p % KD) for p in pieces_at(t, PIECES, steps(RUN_A1))])
            for hp in range(1, HP + 1):
                n = U_NAH + 3 * hp
                g = hp - 1
                r0 = R_ROW + ROWS * g

                def pieces(hp, which):
                    if hp < HP:
                        for piece in which:
                            project(U_NAH + 3 * hp + piece // KD, piece % KD)

                if hp == 1:
                    pieces(hp, range(AHEAD))
                pe.wait_ge(*EV[n - 1])
                pe.wait_ge(s_exp, r0)
                pe.wait_ge(s_add, r0)

                def turn_values(c, bank):
                    row, keys = V_ROWS[c // 2], KC * min(3, ROWS - V_ROWS[c // 2])
                    return pe.transpose(PS[0:keys, bank, (c % 4) * P:(c % 4 + 1) * P],
                                        vTn[:, c % 2, row * KC:row * KC + keys], ident[:, :])

                for c in range(8):
                    ins = turn_values(c, 4 + c // 4)
                ins.then_inc(vn_tr, 1)
                pe.wait_ge(pt_ev, r0)
                pe.wait_ge(o_ev, o_count(r0))
                for c in range(8, 16):
                    ins = turn_values(c, 4 + c // 4)
                ins.then_inc(vn_tr, 1)
                pieces(hp, range(AHEAD, EARLY))
                pe.wait_ge(vn_a, 2 * hp - 1)
                for c in range(16, 24):
                    ins = turn_values(c, c // 4)
                ins.then_inc(vn_tr, 1)
                pe.wait_ge(vn_d, 2 * hp - 1)
                for c in range(24, 26):
                    ins = turn_values(c, 6)
                ins.then_inc(vn_tr, 1)
                pe.wait_ge(vn_a, 2 * hp)
                pe.wait_ge(*EV[n - 3])
                pe.wait_ge(*EV[n - 2])
                for t in range(LAST):
                    if t < ROWS:
                        first, rows, _, w = window(t)
                        keys = kTn[:, g % 2, first * GW:(first + rows) * GW].rearrange("p (a c) -> p a c", c=GW)
                        scores(r0 + t, qbd[:, g % 2, t, :, :].rearrange("p a c -> p (a c)"),
                               keys[:, :, (GW - KC) * w:(GW - KC) * w + KC])
                    pieces(hp, pieces_at(t, PIECES, ROWS, EARLY))
                    if 0 <= t - ROWS < AHEAD:
                        pieces(hp + 1, [t - ROWS])
                    if 0 <= t - 2 < ROWS:
                        if t == 2:
                            pe.wait_ge(vn_d, 2 * hp)
                        turn_probs(r0 + t - 2)
                    q = t - 3
                    if 0 <= q < ROWS:
                        r = r0 + q
                        pe.wait_ge(pt_ev, r + 1)
                        if q % 4 == 0:
                            pe.wait_ge(o_ev, o_count(r))
                        parts = chunks(q)
                        for c, (place, keys) in enumerate(parts):
                            ins = pe.matmul(PS[:, 7, (q % 4) * P:(q % 4 + 1) * P], Vc[0:keys, place, :],
                                            PT[0:keys, r % 2, c * P:(c + 1) * P], start=(c == 0), stop=(c == len(parts) - 1))
                        ins.then_inc(pv, 1)
            out_project(1)
            turn(7, lambda k: [(y_cp, 21 + k // 2), (y_sq, 21 + k // 2)])
            ffn(1)


def constants():
    half = P // 2
    inv = (np.float32(10000.0) ** (-np.arange(half, dtype=np.float32) / np.float32(half))).astype(np.float32)
    ang = (np.arange(SEQ, dtype=np.float32)[None, :] * inv[:, None]).astype(np.float32)
    c, s = np.cos(ang), np.sin(ang)
    ropes = np.stack([np.concatenate([c, c]), np.concatenate([s, -s])]).astype(np.float32)
    i = np.arange(P, dtype=np.float32)
    rel = i[None, :] - i[:, None]
    scale = np.float32(float(P) ** -0.5)
    rows = [np.maximum(rel, 0), np.maximum(-rel, 0), (rel >= 0) * scale, (rel <= 0) * scale,
            np.broadcast_to(i[None, :] + 1, (P, P)), np.broadcast_to(P - i[None, :], (P, P)),
            np.stack([P - 1 - i, i] + [0 * i] * 6, axis=1)]
    decay_consts = np.concatenate(rows, axis=1).astype(np.float32)
    masks = np.zeros((2, 2, QC, 2 * 2 * KC + KR), dtype=np.float32)
    for w in range(2):
        q = QC * w + np.arange(QC)[::-1, None]
        k = (GW - KC) * w + np.arange(KC)[None, :]
        start = np.clip(q - WC // 2, 0, GW - WC)
        inside = (k >= start) & (k < start + WC)
        masks[:, :, :, 2 * w * KC:(2 * w + 1) * KC] = inside
        masks[:, :, :, (2 * w + 1) * KC:(2 * w + 2) * KC] = np.where(inside, 0, -1e30)
    masks[:, 0, :, 4 * KC + KR - 1] = -1e30
    masks[:, 1, :, 4 * KC] = -1e30
    return ropes, decay_consts, masks.reshape(P, -1), np.eye(P, dtype=np.float32)


def kernel(x, mem, norm_g, mem_norm_g, mem_w_kv, ret_w_in, ret_w_out, ret_gn_g, ret_gn_b, ret_decay,
           na_w_in, na_w_out, na_rpb, ffn_w_in, ffn_w_out):
    import concourse.bacc as bacc
    from concourse.bass_utils import run_bass_kernel_spmd

    a = {k: np.asarray(v) for k, v in locals().items() if k not in ("bacc", "run_bass_kernel_spmd")}

    def tiles(w, *groups):
        g = len(groups)
        w = w.reshape((KD, P) + groups + (P,))
        return w.transpose(tuple(range(2 + g - 1, 1, -1)) + (1, 0, 2 + g)).reshape(-1, P, UW)

    def rows(w, order):
        return w.reshape(KD, P, D)[order]

    tok = RH * P
    ret, na = a["ret_w_in"][0], a["na_w_in"][0]
    wpack = np.concatenate([
        tiles(a["mem_w_kv"], 4),
        tiles(ret[:, 4 * tok:], 2), tiles(ret[:, :4 * tok], 4, RH), rows(a["ret_w_out"][0], [6, 0, 1, 2, 3, 4, 5, 7]),
        tiles(a["ffn_w_in"][0], 2, KH), a["ffn_w_out"][0].reshape(KH, P, D),
        tiles(na[:, 3 * tok:], 2), tiles(na[:, :3 * tok], 3, HP), rows(a["na_w_out"][0], [6, 7, 0, 1, 2, 3, 4, 5]),
        tiles(a["ffn_w_in"][1], 2, KH), a["ffn_w_out"][1].reshape(KH, P, D)])
    g = a["norm_g"]
    pre = np.stack([g[0, 0], g[0, 2], g[1, 0], g[1, 2], a["mem_norm_g"]])
    ropes, decay_consts, na_masks, ident = constants()
    arrays = {
        "wpack": wpack, "x": a["x"][0], "mem": a["mem"][0],
        "gains": pre.reshape(5, KD, P).transpose(2, 0, 1),
        "gain_rows": np.stack([g[0, 1], g[0, 3], g[1, 1], g[1, 3]]),
        "gn": np.stack([a["ret_gn_g"][0], a["ret_gn_b"][0]]).reshape(2, RH, P).transpose(2, 0, 1),
        "decay": a["ret_decay"].reshape(1, 2 * RH), "rpb": a["na_rpb"].reshape(-1),
        "ropes": ropes, "decay_consts": decay_consts, "na_masks": na_masks, "ident_c": ident}
    nc = bacc.Bacc("TRN2", target_bir_lowering=False, num_devices=1)
    arrays = {f"in_{k}": np.ascontiguousarray(v) for k, v in arrays.items()}
    args = [nc.dram_tensor(k, v.shape, mybir.dt.from_np(v.dtype), kind="ExternalInput").ap() for k, v in arrays.items()]
    out = nc.dram_tensor("out_h", (SEQ, D), mybir.dt.float32, kind="ExternalOutput").ap()
    trunk_program(nc, *args, out)
    r = run_bass_kernel_spmd(nc, [arrays], core_ids=[0])
    return r.results[0]["out_h"].reshape(1, SEQ, D)
```
